# Optimizing a Trainium2 kernel written in Bass

```python
import math
import jax, jax.numpy as jnp
from jax import lax
import numpy as np

D_MODEL = 1024
BATCH = 1
SEQ = 1024
DEPTH = 4
DEC_BATCH = 8
DEC_SEQ = 1
PAST_LEN = 1024
PAGE_SIZE = 128

N_MIXERS = 3
N_RET = (DEPTH + 2) // 3
N_DIFF = (DEPTH + 1) // 3
N_LRU = DEPTH // 3

RET_HEADS = 4
RET_DK = 256
RET_DV = 512
RET_QK = RET_HEADS * RET_DK
RET_V = RET_HEADS * RET_DV
RET_CHUNK = 128

DIFF_HEADS = 8
DIFF_DK = 64
DIFF_DV = 2 * DIFF_DK
DIFF_QK = DIFF_HEADS * 2 * DIFF_DK
DIFF_V = DIFF_HEADS * DIFF_DV
Q_BLOCK = 128

LRU_WIDTH = 1536
LRU_BLOCKS = 12
LRU_BW = LRU_WIDTH // LRU_BLOCKS
CONV_W = 4
LRU_C = 8.0

NORM_EPS = 1e-6

kernel_name = 'hybrid_ret_diffattn_rglru_step'

def rms_norm(x, gain=None):
    xf = x.astype(jnp.float32)
    y = xf * lax.rsqrt(jnp.mean(xf * xf, axis=-1, keepdims=True) + NORM_EPS)
    if gain is not None:
        y = y * gain.astype(jnp.float32)
    return y.astype(x.dtype)

def ret_log_gamma():
    return jnp.log1p(-jnp.exp2(-5.0 - jnp.arange(RET_HEADS, dtype=jnp.float32)))

def alibi_slopes():
    return jnp.exp2(-8.0 * (jnp.arange(DIFF_HEADS, dtype=jnp.float32) + 1.0) / DIFF_HEADS)

def retention_chunk(S0, qkv, lg):
    q, k, v = qkv
    C = q.shape[1]
    idx = jnp.arange(C, dtype=jnp.float32)
    rel = idx[:, None] - idx[None, :]
    decay = jnp.where(rel >= 0, jnp.exp(jnp.maximum(rel, 0.0)[None] * lg[:, None, None]), 0.0)
    s = jnp.einsum('bihd,bjhd->bhij', q, k) * decay
    o = jnp.einsum('bhij,bjhv->bihv', s, v)
    q_dec = jnp.exp((idx + 1.0)[:, None] * lg[None, :])
    o = o + jnp.einsum('bihd,bhdv->bihv', q, S0) * q_dec[None, :, :, None]
    k_dec = jnp.exp((C - 1.0 - idx)[:, None] * lg[None, :])
    S = jnp.exp(C * lg)[None, :, None, None] * S0 + jnp.einsum('bjhd,bjhv->bhdv', k * k_dec[None, :, :, None], v)
    return S, o

def retention_branch(h, S0, w_in, w_out):
    B, T, _ = h.shape
    q, k, v, g = jnp.split(h @ w_in, [RET_QK, 2 * RET_QK, 2 * RET_QK + RET_V], axis=-1)
    q = q.reshape(B, T, RET_HEADS, RET_DK).astype(jnp.float32)
    k = k.reshape(B, T, RET_HEADS, RET_DK).astype(jnp.float32) * (RET_DK ** -0.5)
    v = v.reshape(B, T, RET_HEADS, RET_DV).astype(jnp.float32)
    C = min(RET_CHUNK, T)
    n = T // C
    to_chunks = lambda a: jnp.moveaxis(a.reshape(B, n, C, *a.shape[2:]), 1, 0)
    lg = ret_log_gamma()
    S, o = lax.scan(lambda S, c: retention_chunk(S, c, lg), S0.astype(jnp.float32),
                    (to_chunks(q), to_chunks(k), to_chunks(v)))
    o = jnp.moveaxis(o, 0, 1).reshape(B, T, RET_HEADS, RET_DV)
    o = rms_norm(o).reshape(B, T, RET_V).astype(h.dtype)
    return (o * jax.nn.silu(g)) @ w_out, S

def diff_project(h, w_in, q_gain, k_gain):
    B, T, _ = h.shape
    q, k, v, g = jnp.split(h @ w_in, [DIFF_QK, 2 * DIFF_QK, 2 * DIFF_QK + DIFF_V], axis=-1)
    q = rms_norm(q.reshape(B, T, DIFF_HEADS, 2, DIFF_DK), q_gain)
    k = rms_norm(k.reshape(B, T, DIFF_HEADS, 2, DIFF_DK), k_gain)
    v = v.reshape(B, T, DIFF_HEADS, DIFF_DV)
    return q, k, v, g

def diff_lambda(lq1, lk1, lq2, lk2, lam_init):
    f = lambda a: a.astype(jnp.float32)
    return jnp.exp(jnp.sum(f(lq1) * f(lk1))) - jnp.exp(jnp.sum(f(lq2) * f(lk2))) + lam_init

def diff_attend_prompt(q, k, v, lam):
    B, T = q.shape[:2]
    nb = T // Q_BLOCK
    scale = DIFF_DK ** -0.5
    slopes = alibi_slopes()
    pos_s = jnp.arange(T, dtype=jnp.float32)
    vf = v.astype(jnp.float32)
    q_blocks = jnp.moveaxis(q.reshape(B, nb, Q_BLOCK, DIFF_HEADS, 2, DIFF_DK), 1, 0)

    def block(args):
        qb, t0 = args
        pos_t = t0 + jnp.arange(Q_BLOCK, dtype=jnp.float32)
        dist = pos_t[:, None] - pos_s[None, :]
        s = jnp.einsum('bthmd,bshmd->bmhts', qb, k).astype(jnp.float32) * scale - slopes[:, None, None] * dist[None]
        s = jnp.where(dist >= 0, s, -jnp.inf)
        p = jax.nn.softmax(s, axis=-1)
        o = jnp.einsum('bmhts,bshv->bmhtv', p, vf)
        return jnp.moveaxis(o[:, 0] - lam * o[:, 1], 1, 2)

    o = lax.map(block, (q_blocks, jnp.arange(nb, dtype=jnp.float32) * Q_BLOCK))
    return jnp.moveaxis(o, 0, 1).reshape(B, T, DIFF_HEADS, DIFF_DV)

def diff_attend_sample(q, k, v, cache_k, cache_v, layer, page_table, lam):
    B, T = q.shape[:2]
    n_pages = page_table.shape[1]
    past = n_pages * PAGE_SIZE
    scale = DIFF_DK ** -0.5
    slopes = alibi_slopes()
    pos_t = past + jnp.arange(T, dtype=jnp.float32)
    dist = (jnp.arange(T)[:, None] - jnp.arange(T)[None, :]).astype(jnp.float32)
    s = jnp.einsum('bthmd,bshmd->bmhts', q, k).astype(jnp.float32) * scale - slopes[:, None, None] * dist[None]
    s = jnp.where(dist >= 0, s, -jnp.inf)
    m = jnp.max(s, axis=-1)
    p = jnp.exp(s - m[..., None])
    l = jnp.sum(p, axis=-1)
    acc = jnp.einsum('bmhts,bshv->bmhtv', p, v.astype(jnp.float32))

    def page_step(carry, xs):
        m, l, acc = carry
        pidx, pt = xs
        kp = cache_k[layer, pt].reshape(B, PAGE_SIZE, DIFF_HEADS, 2, DIFF_DK)
        vp = cache_v[layer, pt].astype(jnp.float32)
        pos_s = pidx.astype(jnp.float32) * PAGE_SIZE + jnp.arange(PAGE_SIZE, dtype=jnp.float32)
        d = pos_t[:, None] - pos_s[None, :]
        s = jnp.einsum('bthmd,bshmd->bmhts', q, kp).astype(jnp.float32) * scale - slopes[:, None, None] * d[None]
        m_new = jnp.maximum(m, jnp.max(s, axis=-1))
        corr = jnp.exp(m - m_new)
        p = jnp.exp(s - m_new[..., None])
        l = l * corr + jnp.sum(p, axis=-1)
        acc = acc * corr[..., None] + jnp.einsum('bmhts,bshv->bmhtv', p, vp)
        return (m_new, l, acc), None

    (m, l, acc), _ = lax.scan(page_step, (m, l, acc), (jnp.arange(n_pages), page_table.T))
    o = acc / l[..., None]
    return jnp.moveaxis(o[:, 0] - lam * o[:, 1], 1, 2)

def diff_output(o, g, sub_gain, lam_init, w_out):
    B, T = o.shape[:2]
    o = rms_norm(o, sub_gain) * (1.0 - lam_init)
    o = o.reshape(B, T, DIFF_V).astype(g.dtype)
    return (o * jax.nn.silu(g)) @ w_out

def rg_lru_branch(h, h0, conv0, w_in, conv_w, conv_b, wa, ba, wx, bx, lam_param, w_out):
    B, T, _ = h.shape
    xb, g = jnp.split(h @ w_in, 2, axis=-1)
    xc = jnp.concatenate([conv0.astype(xb.dtype), xb], axis=1)
    xconv = conv_b + sum(xc[:, kk:kk + T] * conv_w[kk] for kk in range(CONV_W))
    conv_new = xc[:, T:]
    xblk = xconv.reshape(B, T, LRU_BLOCKS, LRU_BW)
    r = jax.nn.sigmoid(jnp.einsum('btnc,ncd->btnd', xblk, wa).reshape(B, T, LRU_WIDTH) + ba)
    i = jax.nn.sigmoid(jnp.einsum('btnc,ncd->btnd', xblk, wx).reshape(B, T, LRU_WIDTH) + bx)
    log_a = -LRU_C * r.astype(jnp.float32) * jax.nn.softplus(-lam_param.astype(jnp.float32))
    a = jnp.exp(log_a)
    b = jnp.sqrt(-jnp.expm1(2.0 * log_a)) * (i * xconv).astype(jnp.float32)
    b = b.at[:, 0].add(a[:, 0] * h0.astype(jnp.float32))

    def combine(e1, e2):
        a1, b1 = e1
        a2, b2 = e2
        return a1 * a2, a2 * b1 + b2

    _, hs = lax.associative_scan(combine, (a, b), axis=1)
    out = (hs.astype(h.dtype) * jax.nn.silu(g)) @ w_out
    return out, hs[:, -1], conv_new

def setup_inputs(seed: int = 0) -> dict:
    key = jax.random.key(seed)
    ks = iter(jax.random.split(key, 48))
    nrm = lambda shape, scale: jax.random.normal(next(ks), shape, jnp.float32) * scale
    n_pages = PAST_LEN // PAGE_SIZE
    n_used = DEC_BATCH * n_pages
    n_phys = (5 * n_used + 3) // 4
    page_table = jax.random.permutation(next(ks), n_phys)[:n_used].reshape(DEC_BATCH, n_pages).astype(jnp.int32)
    u = jax.random.uniform(next(ks), (N_LRU, LRU_WIDTH), jnp.float32, minval=0.9, maxval=0.999)
    sig = u ** (1.0 / LRU_C)
    lru_lambda = jnp.log(sig) - jnp.log1p(-sig)
    return {
        'x_prompt': nrm((BATCH, SEQ, D_MODEL), 1.0),
        'x_sample': nrm((DEC_BATCH, DEC_SEQ, D_MODEL), 1.0),
        'state_ret': nrm((N_RET, DEC_BATCH, RET_HEADS, RET_DK, RET_DV), 0.5),
        'cache_k': nrm((N_DIFF, n_phys, PAGE_SIZE, DIFF_HEADS, 2 * DIFF_DK), 1.0),
        'cache_v': nrm((N_DIFF, n_phys, PAGE_SIZE, DIFF_HEADS, DIFF_DV), 1.0),
        'page_table': page_table,
        'state_lru_h': nrm((N_LRU, DEC_BATCH, LRU_WIDTH), 0.5),
        'state_lru_conv': nrm((N_LRU, DEC_BATCH, CONV_W - 1, LRU_WIDTH), 1.0),
        'norm_g': 1.0 + nrm((DEPTH, D_MODEL), 0.02),
        'ret_w_in': nrm((N_RET, D_MODEL, 2 * RET_QK + 2 * RET_V), D_MODEL ** -0.5),
        'ret_w_out': nrm((N_RET, RET_V, D_MODEL), RET_V ** -0.5),
        'diff_w_in': nrm((N_DIFF, D_MODEL, 2 * DIFF_QK + 2 * DIFF_V), D_MODEL ** -0.5),
        'diff_q_gain': 1.0 + nrm((N_DIFF, DIFF_DK), 0.02),
        'diff_k_gain': 1.0 + nrm((N_DIFF, DIFF_DK), 0.02),
        'diff_lam_q1': nrm((N_DIFF, DIFF_DK), 0.1),
        'diff_lam_k1': nrm((N_DIFF, DIFF_DK), 0.1),
        'diff_lam_q2': nrm((N_DIFF, DIFF_DK), 0.1),
        'diff_lam_k2': nrm((N_DIFF, DIFF_DK), 0.1),
        'diff_sub_gain': 1.0 + nrm((N_DIFF, DIFF_DV), 0.02),
        'diff_w_out': nrm((N_DIFF, DIFF_V, D_MODEL), DIFF_V ** -0.5),
        'lru_w_in': nrm((N_LRU, D_MODEL, 2 * LRU_WIDTH), D_MODEL ** -0.5),
        'lru_conv_w': nrm((N_LRU, CONV_W, LRU_WIDTH), CONV_W ** -0.5),
        'lru_conv_b': nrm((N_LRU, LRU_WIDTH), 0.02),
        'lru_wa': nrm((N_LRU, LRU_BLOCKS, LRU_BW, LRU_BW), LRU_BW ** -0.5),
        'lru_ba': nrm((N_LRU, LRU_WIDTH), 0.1),
        'lru_wx': nrm((N_LRU, LRU_BLOCKS, LRU_BW, LRU_BW), LRU_BW ** -0.5),
        'lru_bx': nrm((N_LRU, LRU_WIDTH), 0.1),
        'lru_lambda': lru_lambda,
        'lru_w_out': nrm((N_LRU, LRU_WIDTH, D_MODEL), LRU_WIDTH ** -0.5),
    }

def reference(x_prompt, x_sample, state_ret, cache_k, cache_v, page_table, state_lru_h, state_lru_conv,
              norm_g, ret_w_in, ret_w_out, diff_w_in, diff_q_gain, diff_k_gain,
              diff_lam_q1, diff_lam_k1, diff_lam_q2, diff_lam_k2, diff_sub_gain, diff_w_out,
              lru_w_in, lru_conv_w, lru_conv_b, lru_wa, lru_ba, lru_wx, lru_bx, lru_lambda, lru_w_out):
    xp, xs = x_prompt, x_sample
    Bp, Tp = xp.shape[:2]
    ret_p, ret_s, kp_l, vp_l, ks_l, vs_l, hp_l, cp_l, hs_l, cs_l = ([] for _ in range(10))
    for i in range(DEPTH):
        kind, j = i % N_MIXERS, i // N_MIXERS
        hp = rms_norm(xp, norm_g[i])
        hs = rms_norm(xs, norm_g[i])
        if kind == 0:
            S0 = jnp.zeros((Bp, RET_HEADS, RET_DK, RET_DV), jnp.float32)
            op, Sp = retention_branch(hp, S0, ret_w_in[j], ret_w_out[j])
            os_, Ss = retention_branch(hs, state_ret[j], ret_w_in[j], ret_w_out[j])
            ret_p.append(Sp.astype(state_ret.dtype))
            ret_s.append(Ss.astype(state_ret.dtype))
        elif kind == 1:
            lam_init = 0.8 - 0.6 * math.exp(-0.3 * i)
            lam = diff_lambda(diff_lam_q1[j], diff_lam_k1[j], diff_lam_q2[j], diff_lam_k2[j], lam_init)
            q, k, v, g = diff_project(hp, diff_w_in[j], diff_q_gain[j], diff_k_gain[j])
            op = diff_output(diff_attend_prompt(q, k, v, lam), g, diff_sub_gain[j], lam_init, diff_w_out[j])
            kp_l.append(k.reshape(Bp, Tp, DIFF_HEADS, 2 * DIFF_DK))
            vp_l.append(v)
            q, k, v, g = diff_project(hs, diff_w_in[j], diff_q_gain[j], diff_k_gain[j])
            o_s = diff_attend_sample(q, k, v, cache_k, cache_v, j, page_table, lam)
            os_ = diff_output(o_s, g, diff_sub_gain[j], lam_init, diff_w_out[j])
            ks_l.append(k.reshape(xs.shape[0], xs.shape[1], DIFF_HEADS, 2 * DIFF_DK))
            vs_l.append(v)
        else:
            lru_args = (lru_w_in[j], lru_conv_w[j], lru_conv_b[j], lru_wa[j], lru_ba[j],
                        lru_wx[j], lru_bx[j], lru_lambda[j], lru_w_out[j])
            h0 = jnp.zeros((Bp, LRU_WIDTH), jnp.float32)
            c0 = jnp.zeros((Bp, CONV_W - 1, LRU_WIDTH), hp.dtype)
            op, hpl, cpl = rg_lru_branch(hp, h0, c0, *lru_args)
            os_, hsl, csl = rg_lru_branch(hs, state_lru_h[j], state_lru_conv[j], *lru_args)
            hp_l.append(hpl.astype(state_lru_h.dtype))
            cp_l.append(cpl.astype(state_lru_conv.dtype))
            hs_l.append(hsl.astype(state_lru_h.dtype))
            cs_l.append(csl.astype(state_lru_conv.dtype))
        xp = xp + op.astype(xp.dtype)
        xs = xs + os_.astype(xs.dtype)
    return (xp, xs, jnp.stack(ret_p), jnp.stack(ret_s), jnp.stack(kp_l), jnp.stack(vp_l),
            jnp.stack(ks_l), jnp.stack(vs_l), jnp.stack(hp_l), jnp.stack(cp_l), jnp.stack(hs_l), jnp.stack(cs_l))


_drawn_inputs = setup_inputs


def setup_inputs(seed=0):
    import zlib

    import numpy as np

    out = dict(_drawn_inputs(seed))
    spreads = {}
    factors = {'diff_q_gain': 6.592,
     'diff_k_gain': 2.93,
     'diff_lam_k1': 2.999,
     'diff_lam_k2': 4.702,
     'diff_sub_gain': 5.101}
    for name, (base, spread) in spreads.items():
        noise = np.random.default_rng([zlib.crc32(name.encode()), seed]).standard_normal(out[name].shape)
        drawn = base * np.exp(spread * noise) if base else spread * noise
        out[name] = __import__('jax').numpy.asarray(drawn.astype(out[name].dtype))
    for name, factor in factors.items():
        out[name] = (out[name] * factor).astype(out[name].dtype)
    return out
```

```python
from contextlib import ExitStack
import math

import numpy as np
import concourse.bass as bass
from concourse import mybir

P = 128
D_MODEL = 1024
SEQ = 1024
NS = 8
T = SEQ + NS
KT = D_MODEL // P
CHUNKS = [(0, 384), (384, 384), (768, 264)]
NC_ = len(CHUNKS)
WMAX = 384
NBLK = SEQ // P
EPS = 1e-6
UNIT = KT * P

RH, RDK, RDV = 4, 256, 512
RQK, RV = RH * RDK, RH * RDV
RU_IN = 12
RU_OUT = 16
RET_UNITS = RH * RU_IN + RU_OUT

DH, DV = 8, 128
PAGES = 8
LAM_INIT = 0.8 - 0.6 * math.exp(-0.3 * 1)
DIFF_IN, DIFF_OUT = 32, 8
LRU_W, LRU_B = 1536, 12
LRU_IN, LRU_OUT = 24, 16

F32 = mybir.dt.float32
F32R = mybir.dt.float32r
I32 = mybir.dt.int32
ALU = mybir.AluOpType
ACT = mybir.ActivationFunctionType
AX = mybir.AxisListType

RHC = 128 + 128 + 3


def blocks_of(c):
    c0, w = CHUNKS[c]
    return [(b, min(P, c0 + w - b * P)) for b in range(c0 // P, (c0 + w + P - 1) // P)]


def constants():
    ident = np.eye(P, dtype=np.float32)
    lg = np.log1p(-np.exp2(-5.0 - np.arange(RH)))
    idx = np.arange(P, dtype=np.float64)
    rel = idx[None, :] - idx[:, None]
    ret = np.zeros((RH, P, RHC), np.float32)
    for h in range(RH):
        ret[h, :, 0:P] = np.where(rel >= 0, np.exp(np.maximum(rel, 0) * lg[h]), 0.0)
        ret[h, :, P:2 * P] = np.exp((idx + 1.0) * lg[h])[None, :]
        ret[h, :, 2 * P] = np.exp((P - 1.0 - idx) * lg[h])
        ret[h, :, 2 * P + 1] = np.exp(lg[h])
        ret[h, :, 2 * P + 2] = np.exp(P * lg[h])
    dist = np.arange(SEQ)[None, :] - (SEQ - P) - idx[:, None]
    dist = np.where(dist <= 0, dist, -1e32).astype(np.float32)
    sdist = np.tile((np.arange(SEQ) - SEQ).astype(np.float32), (NS, 1))
    return {"c_ident": ident, "c_ret": ret, "c_dist": dist, "c_sdist": sdist}


class Chain:

    def __init__(self, eng, sem):
        self.eng, self.sem, self.n, self.off = eng, sem, 0, 0

    def link(self, ins):
        self.n += 1
        ins.then_inc(self.sem, 1)
        self.eng.wait_ge(self.sem, self.n + self.off)

    def loop(self, i, start, per):
        self.at, self.per = self.n, per
        self.off = (i - start) * per

    def done(self, rounds):
        assert self.n - self.at == self.per, (self.n - self.at, self.per)
        self.n = self.at + self.per * rounds
        self.off = 0


class Pos:

    def __init__(self, base, i=0, per=0):
        self.base, self.i, self.per = base, i, per

    def at(self, k):
        return self.base + k if self.per == 0 else self.i * self.per + (self.base + k)

    def half(self, k):
        return (self.base + k) // 2 if self.per == 0 else self.i * (self.per // 2) + (self.base + k) // 2


class Arena:

    def __init__(self, ap, size):
        self.ap, self.size, self.at = ap, size, 0

    def take(self, *shape):
        n = int(np.prod(shape))
        assert self.at + n <= self.size, f"arena: {self.at + n} of {self.size}"
        v = self.ap[:, self.at:self.at + n]
        self.at += n
        names = "abcd"[:len(shape)]
        if len(shape) > 1:
            kw = {names[i]: shape[i] for i in range(1, len(shape))}
            v = v.rearrange(f"p ({' '.join(names)}) -> p {' '.join(names)}", **kw)
        return v



UNIT_AT = [0, RET_UNITS, RET_UNITS + DIFF_IN + DIFF_OUT, RET_UNITS + DIFF_IN + DIFF_OUT + LRU_IN + LRU_OUT]
RAW_AT = UNIT_AT
FILL_AT = [0, 3, 5, 8]
FILL_K = [8, 8, 8, 8, 8, 8, 8, 4, 8, 8, 8]


def fill_tiles(f, c):
    return sum(FILL_K[:f]) * NC_ + c * FILL_K[f]


def trunk(nc, A, LAYERS=4):
    ctx = ExitStack()
    with ctx:
        def sb(name, shape, dt=F32):
            return ctx.enter_context(nc.sbuf_tensor(name, shape, dt))

        def sem(name):
            return ctx.enter_context(nc.semaphore(name))

        def sems(name, n):
            return [sem(f"{name}{i}") for i in range(n)]

        xT = sb("xT", [P, KT, T])
        Hh, Hl = sb("Hh", [P, KT, T], F32R), sb("Hl", [P, KT, T], F32R)
        wraw = sb("wraw", [P, 2, UNIT])
        Wh, Wl = sb("Wh", [P, 2, UNIT], F32R), sb("Wl", [P, 2, UNIT], F32R)
        ident, ones = sb("ident", [P, P]), sb("ones", [P, P])
        ss = sb("ss", [P, T])
        rst = sb("rst", [P, WMAX])
        hraw = sb("hraw", [P, 2, WMAX])
        ng = sb("ng", [P, 4, KT])
        eps_t = sb("eps_t", [P, 1])
        ASZ = 19808
        arena_t = sb("arena", [P, ASZ])
        psum = ctx.enter_context(nc.psum_tensor("psum", [P, 8, 512], F32))
        bank = [psum[:, i, :] for i in range(8)]
        on_d = nc.dram_tensor("scratch_on", (2 * KT, P, T), F32, kind="Internal").ap()
        g_d = nc.dram_tensor("scratch_g", (2 * KT, P, T), F32, kind="Internal").ap()

        def arena():
            return Arena(arena_t[:, :], ASZ)

        w_loaded = sems("w_loaded", 2)
        raw_free = sem("raw_free")
        w_hi, w_lo = sem("w_hi"), sem("w_lo")
        unit_ps = sem("unit_ps")
        unit_ev = sem("unit_ev")
        h_raw, h_hi, h_lo = sem("h_raw"), sem("h_hi"), sem("h_lo")
        sq_done, ss_done = sem("sq_done"), sem("ss_done")
        nrm_ps, nrm_sq = sem("nrm_ps"), sem("nrm_sq")
        const_ld, const_ms, const_tr, const_ev = sem("const_ld"), sem("const_ms"), sem("const_tr"), sem("const_ev")
        dve_own = sem("dve_own")
        stage_ld = sems("stage_ld", 2)
        final_st = sem("final_st")
        stores = {"final": 0}

        CR = 2
        CR_PS = 3

        def ev_val(u, c):
            return u * NC_ + (c + 1 + CR)

        def ps_val(u, c):
            return u * NC_ + (c + 1 + CR_PS)

        held = {x: sem(f"held_{x}") for x in ("sp", "pe", "dve")}

        def hold(eng, x):
            eng.sem_inc(held[x], 1)

        def w_block(w, row0, kt, col0):
            return w[row0:row0 + kt * P, :].rearrange("(k p) n -> p k n", p=P)[:, :, bass.ds(col0, P)]

        def load_w(sp, raw, j, src, kt=KT):
            sp.wait_ge(raw_free, raw.at(j) + (1 + CR - 2))
            sp.dma_start(wraw[:, j % 2, 0:kt * P].rearrange("p (k n) -> p k n", k=kt), src)\
              .then_inc(w_loaded[j % 2], 16)

        def split_hi(act, unit, raw, j, kt=KT):
            act.wait_ge(w_loaded[j % 2], raw.half(j) * 16 + 16)
            act.wait_ge(unit_ps, ps_val(unit.at(j), 2) - 2 * NC_)
            act.activation(Wh[:, j % 2, 0:kt * P], wraw[:, j % 2, 0:kt * P], ACT.Copy).then_inc(w_hi, 1)

        def split_lo(pool, unit, j, kt=KT):
            pool.wait_ge(w_hi, unit.at(j) + 1)
            pool.tensor_tensor(Wl[:, j % 2, 0:kt * P], wraw[:, j % 2, 0:kt * P],
                               Wh[:, j % 2, 0:kt * P].bitcast(F32), ALU.subtract).then_inc(w_lo, 1)
            pool.wait_ge(w_lo, unit.at(j) + 1)
            pool.sem_inc(raw_free, 1)

        def unit_bank(j, c):
            return bank[(j + c) % 2]

        def unit_chunk(pe, unit, j, c, f, kt=KT):
            c0, w = CHUNKS[c]
            if c == 0:
                pe.wait_ge(w_lo, unit.at(j) + 1)
            pe.wait_ge(h_lo, fill_tiles(f, c) + FILL_K[f])
            pe.wait_ge(unit_ev, ev_val(unit.at(j), c) - 2)
            out = unit_bank(j, c)[:, 0:w]
            for k in range(kt):
                hi, lo = Wh[:, j % 2, k * P:(k + 1) * P], Wl[:, j % 2, k * P:(k + 1) * P]
                xh, xl = Hh[:, k, c0:c0 + w], Hl[:, k, c0:c0 + w]
                nc.tensor.matmul(out, hi, xh, start=(k == 0), stop=False)
                nc.tensor.matmul(out, hi, xl, start=False, stop=False)
                last = nc.tensor.matmul(out, lo, xh, start=False, stop=(k == kt - 1))
            last.then_inc(unit_ps, 1)

        def fill_before(f):
            return {0: 0, 1: 48, 2: 56, 3: 64, 4: UNIT_AT[1] + 32, 5: UNIT_AT[2],
                    6: UNIT_AT[2] + 24, 7: UNIT_AT[2] + 32, 8: UNIT_AT[3], 9: UNIT_AT[3] + 48,
                    10: UNIT_AT[3] + 56}[f]

        def fill_parts(act, dve, pool, f, c):
            c0, w = CHUNKS[c]
            for k in range(FILL_K[f]):
                n = fill_tiles(f, c) + k
                if act is not None:
                    if k == 0 and fill_before(f):
                        act.wait_ge(unit_ps, ps_val(fill_before(f) - 1, c))
                    act.wait_ge(h_raw, n + 1)
                    act.activation(Hh[:, k, c0:c0 + w], hraw[:, n % 2, 0:w], ACT.Copy).then_inc(h_hi, 1)
                if pool is not None:
                    pool.wait_ge(h_hi, n + 1)
                    pool.tensor_tensor(Hl[:, k, c0:c0 + w], hraw[:, n % 2, 0:w],
                                       Hh[:, k, c0:c0 + w].bitcast(F32), ALU.subtract).then_inc(h_lo, 1)

        def norm_index(layer, c):
            return layer * NC_ + c

        NB = bank[7]

        def norm_pe(pe, layer, c):
            c0, w = CHUNKS[c]
            n = norm_index(layer, c)
            pe.wait_ge(ss_done, KT * NC_ * layer + (KT - 1) * NC_ + c + 1)
            if n:
                pe.wait_ge(nrm_sq, n)
            nc.tensor.matmul(NB[:, 0:w], ones[:, :], ss[:, c0:c0 + w], start=True, stop=True).then_inc(nrm_ps, 1)

        def norm_act(act, layer, c):
            c0, w = CHUNKS[c]
            n = norm_index(layer, c)
            f = FILL_AT[layer]
            act.wait_ge(nrm_ps, n + 1)
            if c:
                act.wait_ge(h_raw, fill_tiles(f, c))
            act.activation(rst[:, 0:w], NB[:, 0:w], ACT.Sqrt, bias=eps_t[:, 0:1], scale=1.0 / D_MODEL)\
               .then_inc(nrm_sq, 1)
            fill_parts(act, None, None, f, c)

        def norm_dve(dve, ch, layer, c):
            c0, w = CHUNKS[c]
            f = FILL_AT[layer]
            dve.wait_ge(nrm_sq, norm_index(layer, c) + 1)
            ch.link(nc.vector.reciprocal(rst[:, 0:w], rst[:, 0:w]))
            for k in range(KT):
                n = fill_tiles(f, c) + k
                if n >= 2:
                    dve.wait_ge(h_lo, n - 1)
                nc.vector.scalar_tensor_tensor(hraw[:, n % 2, 0:w], xT[:, k, c0:c0 + w], ng[:, layer, k:k + 1],
                                               rst[:, 0:w], ALU.mult, ALU.mult).then_inc(h_raw, 1)

        def stage_index(f):
            return NC_ * sum(1 for x in range(f) if x not in FILL_AT)

        def stage_load(sp, st, f, k0, c):
            c0, w = CHUNKS[c]
            n = stage_index(f) + c
            for i, src in enumerate((on_d, g_d)):
                sp.dma_start(st[:, n % 2, i, 0:FILL_K[f], 0:w],
                             src[k0:k0 + FILL_K[f], :, c0:c0 + w].rearrange("k p t -> p k t"))\
                  .then_inc(stage_ld[n % 2], 16)

        def stage_dve(dve, st, f, c, scale):
            c0, w = CHUNKS[c]
            m = stage_index(f) + c
            dve.wait_ge(stage_ld[m % 2], 32 * (m // 2 + 1))
            for k in range(FILL_K[f]):
                n = fill_tiles(f, c) + k
                dve.wait_ge(h_lo, n - 1)
                nc.vector.scalar_tensor_tensor(hraw[:, n % 2, 0:w], st[:, m % 2, 0, k, 0:w], scale,
                                               st[:, m % 2, 1, k, 0:w], ALU.mult, ALU.mult).then_inc(h_raw, 1)

        def residual_dve(dve, unit, j, m, c, final, sqb, sqn):
            c0, w = CHUNKS[c]
            dve.wait_ge(unit_ps, ps_val(unit.at(j), c))
            dve.wait_ge(unit_ev, ev_val(unit.at(j), c) - 1)
            x = xT[:, bass.ds(m, 1), c0:c0 + w].rearrange("p a t -> p (a t)")
            nc.vector.tensor_tensor(x, unit_bank(j, c)[:, 0:w], x, ALU.add).then_inc(unit_ev, 1)
            if final:
                dve.wait_ge(sq_done, sqn + 1)
                nc.vector.tensor_tensor(ss[:, c0:c0 + w], ss[:, c0:c0 + w], sqb[:, (j + c) % 2, 0:w], ALU.add)\
                  .then_inc(ss_done, 1)

        def square_act(act, unit, j, m, c, sqb, sqn):
            c0, w = CHUNKS[c]
            act.wait_ge(unit_ev, ev_val(unit.at(j), c))
            act.wait_ge(ss_done, sqn - 1)
            x = xT[:, bass.ds(m, 1), c0:c0 + w].rearrange("p a t -> p (a t)")
            act.activation(sqb[:, (j + c) % 2, 0:w], x, ACT.Square).then_inc(sq_done, 1)

        al = arena()
        xin = al.take(2, D_MODEL)
        sqb0 = al.take(2, WMAX)
        ngr = al.take(P)
        xin_ld, xin_ps = sems("xin_ld", 2), sem("xin_ps")
        xin_a, xin_d = sem("xin_a"), sem("xin_d")

        def xin_bank(b, half):
            return bank[2 + 2 * (b % 2) + half]

        def input_sp(sp):
            sp.sem_inc(raw_free, CR)
            sp.dma_start(ident[:, :], A["c_ident"]).then_inc(const_ld, 16)
            sp.dma_start(ngr[0:32, :], A["norm_g"].rearrange("l (k p) -> (l k) p", p=P)).then_inc(const_ld, 16)
            for b in range(NBLK + 1):
                if b >= 2:
                    sp.wait_ge(xin_ps, 2 * (b - 1))
                src = A["x_prompt"][0, b * P:(b + 1) * P, :] if b < NBLK else A["x_sample"][:, 0, :]
                sp.dma_start(xin[0:P if b < NBLK else NS, b % 2, :], src).then_inc(xin_ld[b % 2], 16)

        def input_pe(pe):
            pe.wait_ge(const_ld, 32)
            nc.tensor.transpose(bank[6][:, 0:32], ngr[0:32, :], ident[0:32, 0:32]).then_inc(const_tr, 1)
            for b in range(NBLK + 1):
                w = P if b < NBLK else NS
                pe.wait_ge(xin_ld[b % 2], 16 * (b // 2 + 1))
                for half, ev in enumerate((xin_a, xin_d)):
                    if b >= 2:
                        pe.wait_ge(ev, b - 1)
                    for k in range(4):
                        last = nc.tensor.transpose(xin_bank(b, half)[:, k * P:k * P + w],
                                                   xin[0:w, b % 2, (4 * half + k) * P:(4 * half + k + 1) * P],
                                                   ident[0:w, 0:w])
                    last.then_inc(xin_ps, 1)

        def input_evac(b, half):
            w = P if b < NBLK else NS
            src = xin_bank(b, half)[:, :].rearrange("p (k t) -> p k t", k=4)[:, :, 0:w]
            return xT[:, 4 * half:4 * half + 4, b * P:b * P + w], src

        def input_act(act):
            for b in range(NBLK + 1):
                act.wait_ge(xin_ps, 2 * b + 1)
                act.activation(*input_evac(b, 0), ACT.Copy).then_inc(xin_a, 1)
            act.wait_ge(xin_a, NBLK + 1)
            act.wait_ge(xin_d, NBLK + 1)
            for n in range(KT * NC_):
                k, (c0, w) = n // NC_, CHUNKS[n % NC_]
                if n >= 2:
                    act.wait_ge(ss_done, n - 1)
                act.activation(sqb0[:, n % 2, 0:w], xT[:, k, c0:c0 + w], ACT.Square).then_inc(sq_done, 1)

        def input_dve(dve, ch):
            nc.vector.memset(ones[:, :], 1.0).then_inc(const_ms, 1)
            nc.vector.memset(eps_t[:, :], EPS).then_inc(const_ms, 1)
            ch.link(nc.vector.memset(ss[:, :], 0.0))
            dve.wait_ge(const_tr, 1)
            ch.link(nc.vector.tensor_copy(ng[:, :, :].rearrange("p l k -> p (l k)"), bank[6][:, 0:32]))
            for b in range(NBLK + 1):
                dve.wait_ge(xin_ps, 2 * b + 2)
                nc.vector.tensor_copy(*input_evac(b, 1)).then_inc(xin_d, 1)
            for n in range(KT * NC_):
                c0, w = CHUNKS[n % NC_]
                dve.wait_ge(sq_done, n + 1)
                if n >= NC_:
                    dve.wait_ge(ss_done, n - NC_ + 1)
                nc.vector.tensor_tensor(ss[:, c0:c0 + w], ss[:, c0:c0 + w], sqb0[:, n % 2, 0:w], ALU.add)\
                  .then_inc(ss_done, 1)

        def output_parts(layers):
            al = arena()
            yo = al.take(2, D_MODEL)
            y_ps, y_a, y_d = sem("y_ps"), sem("y_a"), sem("y_d")
            y_st = sems("y_st", 2)
            q_end = UNIT_AT[layers - 1] + [RET_UNITS, DIFF_IN + DIFF_OUT, LRU_IN + LRU_OUT, RET_UNITS][layers - 1]

            def pe_(pe):
                for b in range(NBLK + 1):
                    w = P if b < NBLK else NS
                    c = min(b // 3, 2)
                    pe.wait_ge(unit_ev, ev_val(q_end - 1, c))
                    for half, ev in enumerate((y_a, y_d)):
                        if b >= 2:
                            pe.wait_ge(ev, b - 1)
                        for k in range(4):
                            last = nc.tensor.transpose(xin_bank(b, half)[0:w, k * P:(k + 1) * P],
                                                       xT[:, 4 * half + k, b * P:b * P + w], ident[:, :])
                        last.then_inc(y_ps, 1)

            def evac(b, half):
                w = P if b < NBLK else NS
                return yo[0:w, b % 2, half * 512:(half + 1) * 512], xin_bank(b, half)[0:w, :]

            def act_(act):
                for b in range(NBLK + 1):
                    if b >= 2:
                        act.wait_ge(y_st[b % 2], 16 * (b // 2))
                    act.wait_ge(y_ps, 2 * b + 1)
                    act.activation(*evac(b, 0), ACT.Copy).then_inc(y_a, 1)

            def dve_(dve):
                for b in range(NBLK + 1):
                    if b >= 2:
                        dve.wait_ge(y_st[b % 2], 16 * (b // 2))
                    dve.wait_ge(y_ps, 2 * b + 2)
                    nc.vector.tensor_copy(*evac(b, 1)).then_inc(y_d, 1)

            def sp_(sp):
                for b in range(NBLK + 1):
                    sp.wait_ge(y_a, b + 1)
                    sp.wait_ge(y_d, b + 1)
                    dst = A["y_prompt"][0, b * P:(b + 1) * P, :] if b < NBLK else A["y_sample"][:, 0, :]
                    sp.dma_start(dst, yo[0:P if b < NBLK else NS, b % 2, :]).then_inc(y_st[b % 2], 16)
                sp.wait_ge(y_st[0], 16 * 5)
                sp.wait_ge(y_st[1], 16 * 4)
            return pe_, act_, dve_, sp_

        al = arena()
        kT, qT = al.take(2, T), al.take(2, T)
        ktok = al.take(NBLK, RDK)
        vtok = al.take(NBLK, RDV)
        vs = al.take(RDV)
        St = al.take(2, RDV)
        qdT = al.take(2, 2, P)
        sdT = al.take(2, P)
        onb = al.take(RDV)
        onst = al.take(2, 4, P)
        kvc = hraw
        gst = al.take(2, WMAX)
        sring = al.take(4, 2, RDV)
        hc = al.take(RHC)
        so, sq_s, rs_s, nt = al.take(4, NS), al.take(4, NS), al.take(NS), al.take(2, NS)
        osq, o_r, nt1 = al.take(1), al.take(1), al.take(2)
        sqj = hraw[:, :, :].rearrange("p a t -> p (a t)")[:, 0:RDV]
        decT, qdec, kdec, gam, gamC = hc[:, 0:P], hc[:, P:2 * P], hc[:, 256:257], hc[:, 257:258], hc[:, 258:259]
        TR, SC, OB, SB0, SB1, VB = bank[2], bank[3], bank[4], bank[5], bank[6], bank[7]
        r_hc = sem("r_hc")
        r_tr, r_te = sem("r_tr"), sem("r_te")
        r_sc, r_sd, r_qd = sem("r_sc"), sem("r_sd"), sem("r_qd")
        r_o, r_st, r_su = sem("r_o"), sem("r_st"), sem("r_su")
        r_sq, r_rs, r_on = sem("r_sq"), sem("r_rs"), sem("r_on")
        r_vb, r_sg, r_sn, r_so = sem("r_vb"), sem("r_sg"), sem("r_sn"), sem("r_so")
        r_sld, r_sst = sems("r_sld", 4), sems("r_sst", 4)
        r_on_st, r_g_st = sems("r_on_st", 2), sems("r_g_st", 2)
        r_fin, r_fs, r_fo = sem("r_fin"), sem("r_fs"), sem("r_fo")
        r_S_st, r_os_st = sem("r_S_st"), sem("r_os_st")

        def rsqrt(dve, ch, x, scale, y, t, last_sem=None):
            a = t[:, 0:1] if len(t.shape) == 2 else t[:, 0, :]
            b = t[:, 1:2] if len(t.shape) == 2 else t[:, 1, :]
            ch.link(nc.vector.tensor_scalar(a, x, scale, EPS, ALU.mult, ALU.add))
            ch.link(nc.vector.tensor_scalar(b.bitcast(I32), a.bitcast(I32), 1, None, ALU.logical_shift_right))
            ch.link(nc.vector.tensor_scalar(y.bitcast(I32), b.bitcast(I32), -1.0, float(0x5F3759DF),
                                            ALU.mult, ALU.add))
            for n in range(3):
                ch.link(nc.vector.tensor_tensor(b, y, y, ALU.mult))
                ch.link(nc.vector.scalar_tensor_tensor(b, b, -0.5, a, ALU.mult, ALU.mult))
                step = nc.vector.scalar_tensor_tensor(y, b, 1.5, y, ALU.add, ALU.mult)
                if n < 2 or last_sem is None:
                    ch.link(step)
                else:
                    step.then_inc(last_sem, 1)

        RTR = 26
        RCH = 8 * 11 + 1 + 12
        CREDITS = [(x, 1) for x in (r_tr, r_te, r_sc, r_sd, r_qd, r_o, r_st, r_su, r_sq, r_rs, r_on, r_vb,
                                    r_sg, r_sn, r_so, r_fin, r_fs, r_fo)] + \
                  [(x, 16) for x in (*r_sst, *r_on_st, *r_g_st, r_S_st, r_os_st)]

        def prior(n):
            return n + 1

        def done(n):
            return n + 2

        def ret_sp(sp, lay):
            j_, U, R = lay // 3, UNIT_AT[lay], RAW_AT[lay]
            win, wout = A["ret_w_in"][j_], A["ret_w_out"][j_]

            def weights(h, js):
                for j in js:
                    col = (h * RDK + (RQK + j * P) if j < 2 else h * RDV + (2 * RQK + (j - 2) * P) if j < 6 else
                           h * RDK + (j - 6) * P if j < 8 else h * RDV + (2 * RQK + RV + (j - 8) * P))
                    load_w(sp, Pos(R, h, RU_IN), j, w_block(win, 0, KT, col))

            def head(h):
                sp.wait_ge(r_fo, h + (RH * j_ + 1))
                sp.dma_start(hc, A["c_ret"][bass.ds(h, 1), :, :].rearrange("a p n -> (a p) n")).then_inc(r_hc, 16)
                weights(h, range(2, RU_IN))

            weights(0, (0, 1))
            if lay:
                sp.wait_ge(h_raw, fill_tiles(FILL_AT[lay] - 1, 2) + FILL_K[FILL_AT[lay] - 1])
                sp.wait_ge(ss_done, KT * NC_ * (lay + 1))
            with sp.Fori(0, RH - 1) as h:
                head(h)
                weights(h + 1, (0, 1))
            head(RH - 1)
            out_sp(sp, lay, wout, U + 48, R + 48, [(FILL_AT[lay] + 1, 0), (FILL_AT[lay] + 2, KT)], ret_stage_wait)

        def ret_stage_wait(sp, lay):
            n = RH * (lay // 3 + 1)
            sp.wait_ge(r_fo, n + 1)
            for i in range(2):
                sp.wait_ge(r_on_st[i], 16 * 4 * n + 16)
                sp.wait_ge(r_g_st[i], 16 * 6 * n + 16)
            sp.wait_ge(r_os_st, 16 * n + 16)
            sp.wait_ge(r_S_st, 16 * n + 16)
            for i in range(4):
                sp.wait_ge(r_sst[i], 16 * 2 * n + 16)
            sp.wait_ge(r_te, RTR * n + 1)

        def out_sp(sp, lay, wout, U, R, fills, stage_wait):
            st = stage_of()
            for x, (f, k0) in enumerate(fills):
                kt = FILL_K[f]
                raw = Pos(R + 8 * x)
                if x == 0:
                    for j in range(2):
                        load_w(sp, raw, j, w_block(wout, k0 * P, kt, j * P), kt)
                    stage_wait(sp, lay)
                    for c in range(2):
                        stage_load(sp, st, f, k0, c)
                for j in range(2 if x == 0 else 0, KT):
                    if j == 2:
                        sp.wait_ge(h_raw, fill_tiles(f, 0) + FILL_K[f])
                        stage_load(sp, st, f, k0, 2)
                        if x + 1 < len(fills):
                            sp.wait_ge(h_raw, fill_tiles(f, 1) + FILL_K[f])
                            stage_load(sp, st, *fills[x + 1], 0)
                            sp.wait_ge(h_raw, fill_tiles(f, 2) + FILL_K[f])
                            stage_load(sp, st, *fills[x + 1], 1)
                    load_w(sp, raw, j, w_block(wout, k0 * P, kt, j * P), kt)

        def stage_of():
            al = arena()
            return al.take(2, 2, KT, WMAX)

        def out_square_buf():
            al = arena()
            al.take(2, 2, KT, WMAX)
            return al.take(2, WMAX)

        def out_pe(pe, lay, U, fills, last_layer):
            for x, (f, k0) in enumerate(fills):
                unit = Pos(U + 8 * x)
                final = x + 1 == len(fills) and not last_layer
                for j in range(KT):
                    for c in range(NC_):
                        unit_chunk(pe, unit, j, c, f, FILL_K[f])
                        if final and j == KT - 1 and c:
                            norm_pe(pe, lay + 1, c - 1)
                if final:
                    norm_pe(pe, lay + 1, 2)

        def out_act(act, lay, U, R, fills, last_layer, next_split=True):
            sqb = out_square_buf()
            sqn = KT * NC_ * (lay + 1)
            for x, (f, k0) in enumerate(fills):
                unit, raw = Pos(U + 8 * x), Pos(R + 8 * x)
                final = x + 1 == len(fills) and not last_layer
                if x == 0:
                    for c in range(NC_):
                        fill_parts(act, None, None, f, c)
                for j in range(KT):
                    if j < KT - 1:
                        split_hi(act, unit, raw, j + 1, FILL_K[f])
                    elif x + 1 < len(fills):
                        split_hi(act, unit, raw, j + 1, FILL_K[fills[x + 1][0]])
                    elif not last_layer and next_split:
                        split_hi(act, unit, raw, j + 1)
                    for c in range(NC_):
                        if final:
                            square_act(act, unit, j, j, c, sqb, sqn)
                            sqn += 1
                        if j == KT - 1 and x + 1 < len(fills):
                            fill_parts(act, None, None, fills[x + 1][0], c)
                        elif final and j == KT - 1 and c:
                            norm_act(act, lay + 1, c - 1)
                if final:
                    norm_act(act, lay + 1, 2)

        def out_dve(dve, ch, lay, U, fills, last_layer, scale):
            st, sqb = stage_of(), out_square_buf()
            sqn = KT * NC_ * (lay + 1)
            dve.wait_ge(nrm_ps, NC_ * (lay + 1))
            ch.link(nc.vector.memset(ss[:, :], 0.0))
            for x, (f, k0) in enumerate(fills):
                unit = Pos(U + 8 * x)
                final = x + 1 == len(fills) and not last_layer
                if x == 0:
                    for c in range(NC_):
                        stage_dve(dve, st, f, c, scale)
                for j in range(KT):
                    for c in range(NC_):
                        residual_dve(dve, unit, j, j, c, final, sqb, sqn)
                        sqn += final
                        if j == KT - 1 and x + 1 < len(fills):
                            stage_dve(dve, st, fills[x + 1][0], c, scale)
                        elif final and j == KT - 1 and c:
                            norm_dve(dve, ch, lay + 1, c - 1)
                if final:
                    norm_dve(dve, ch, lay + 1, 2)

        def out_pool(pool, lay, U, fills, last_layer, next_split=True):
            for x, (f, k0) in enumerate(fills):
                unit = Pos(U + 8 * x)
                if x == 0:
                    for c in range(NC_):
                        fill_parts(None, None, pool, f, c)
                for j in range(KT):
                    if j < KT - 1:
                        split_lo(pool, unit, j + 1, FILL_K[f])
                    elif x + 1 < len(fills):
                        split_lo(pool, unit, j + 1, FILL_K[fills[x + 1][0]])
                    elif not last_layer and next_split:
                        split_lo(pool, unit, j + 1)
                    if j == KT - 1:
                        for c in range(NC_):
                            if x + 1 < len(fills):
                                fill_parts(None, None, pool, fills[x + 1][0], c)
                            elif not last_layer:
                                fill_parts(None, None, pool, FILL_AT[lay + 1], c)

        def ret_places(lay, h):
            g = RH * (lay // 3)
            return (Pos(UNIT_AT[lay], h, RU_IN), Pos(RAW_AT[lay], h, RU_IN), Pos(g, h, 1), Pos(8 * g, h, 8),
                    Pos(RTR * g, h, RTR))

        def ret_pe(pe, lay):
            f = FILL_AT[lay]
            with pe.Fori(0, RH) as h:
                unit, raw, n1, n8, ntr = ret_places(lay, h)
                for s in range(36):
                    j, c = divmod(s, NC_)
                    unit_chunk(pe, unit, j, c, f)
                    if 1 <= s <= 18:
                        js, cs = divmod(s - 1, NC_)
                        c0 = CHUNKS[cs][0]
                        pe.wait_ge(unit_ev, ev_val(unit.at(js), cs))
                        pe.wait_ge(r_te, prior(ntr.at(s - 1)))
                        for b, w in blocks_of(cs):
                            if js < 2 and b == NBLK:
                                continue
                            src = kT[:, js, b * P:b * P + w] if js < 2 else kvc[:, (s - 1) % 2, b * P - c0:b * P - c0 + w]
                            last = nc.tensor.transpose(TR[0:w, b * P - c0:b * P - c0 + P], src, ident[:, :])
                        last.then_inc(r_tr, 1)
                    t = s - 24
                    if 0 <= t - 2 < NBLK:
                        r = t - 2
                        pe.wait_ge(r_on, done(n8.at(r)))
                        pe.wait_ge(r_te, prior(ntr.at(18 + r)))
                        for x in range(4):
                            last = nc.tensor.transpose(TR[:, x * P:(x + 1) * P], onb[:, x * P:(x + 1) * P], ident[:, :])
                        last.then_inc(r_tr, 1)
                    if 0 <= t - 1 < NBLK:
                        r = t - 1
                        if r == 0:
                            pe.wait_ge(r_te, done(ntr.at(17)))
                        pe.wait_ge(r_sd, done(n8.at(r)))
                        pe.wait_ge(r_on, prior(n8.at(r)))
                        pe.wait_ge(r_su, prior(n8.at(r)))
                        last = nc.tensor.matmul(OB[:, :], sdT[:, r % 2, :], vtok[:, r, :], start=True, stop=(r == 0))
                        if r:
                            pe.wait_ge(r_qd, done(n8.at(r)))
                            for x in range(2):
                                last = nc.tensor.matmul(OB[:, :], qdT[:, r % 2, x, :], St[:, x, :], start=False,
                                                        stop=(x == 1))
                        last.then_inc(r_o, 1)
                        for x, sbk in enumerate((SB0, SB1)):
                            last = nc.tensor.matmul(sbk[:, :], ktok[:, r, x * P:(x + 1) * P], vtok[:, r, :],
                                                    start=True, stop=True)
                        last.then_inc(r_st, 1)
                    if 0 <= t - 2 < NS:
                        b = t - 2
                        pe.wait_ge(r_sd, prior(n8.at(min(t, NBLK))))
                        pe.wait_ge(r_sn, done(n8.at(b)))
                        for d in range(4):
                            for x in range(2):
                                last = nc.tensor.matmul(SC[:, P + d * NS + b:P + d * NS + b + 1],
                                                        sring[:, b % 4, x, d * P:(d + 1) * P],
                                                        qT[:, x, SEQ + b:SEQ + b + 1], start=(x == 0), stop=(x == 1))
                        last.then_inc(r_so, 1)
                    if 0 <= t < NBLK:
                        if t == 0:
                            pe.wait_ge(unit_ev, ev_val(unit.at(7), 2))
                        pe.wait_ge(r_sd, prior(n8.at(t)))
                        for x in range(2):
                            last = nc.tensor.matmul(SC[:, 0:P], kT[:, x, t * P:(t + 1) * P], qT[:, x, t * P:(t + 1) * P],
                                                    start=(x == 0), stop=(x == 1))
                        last.then_inc(r_sc, 1)
                    if 0 <= t - 1 < NS:
                        b = t - 1
                        pe.wait_ge(r_sn, prior(n8.at(b)))
                        nc.tensor.matmul(VB[:, :], ident[0:NS, b:b + 1].to_broadcast([NS, P]), vs[0:NS, :],
                                         start=True, stop=True).then_inc(r_vb, 1)
                    if t == 10:
                        pe.wait_ge(r_fs, done(n1.at(0)))
                        for d in range(4):
                            last = nc.tensor.matmul(SC[:, 160:160 + NS], ones[:, :], sq_s[:, d, :], start=(d == 0),
                                                    stop=(d == 3))
                        last.then_inc(r_fin, 1)

        def ret_act(act, lay):
            j_ = lay // 3
            with act.Fori(0, RH) as h:
                unit, raw, n1, n8, ntr = ret_places(lay, h)
                n2, n4, n6 = (Pos(x * RH * j_, h, x) for x in (2, 4, 6))
                for s in range(36):
                    j, c = divmod(s, NC_)
                    c0, w = CHUNKS[c]
                    if c == 0:
                        split_hi(act, unit, raw, j + 1)
                    src = unit_bank(j, c)[:, 0:w]
                    act.wait_ge(unit_ps, ps_val(unit.at(j), c))
                    if j < 2:
                        if s == 0:
                            act.wait_ge(r_fo, prior(n1.at(0)))
                        act.activation(kT[:, j, c0:c0 + w], src, ACT.Copy, scale=RDK ** -0.5).then_inc(unit_ev, 1)
                    elif j < 6:
                        act.wait_ge(r_tr, done(ntr.at(s - 2)))
                        act.activation(kvc[:, s % 2, 0:w], src, ACT.Copy).then_inc(unit_ev, 1)
                    elif j < 8:
                        act.activation(qT[:, j - 6, c0:c0 + w], src, ACT.Copy).then_inc(unit_ev, 1)
                    else:
                        t = s - 24
                        act.wait_ge(r_g_st[t % 2], n6.at(t // 2) * 16 + 16)
                        act.activation(gst[:, t % 2, 0:w], src, ACT.Silu).then_inc(unit_ev, 1)
                        act.wait_ge(unit_ev, ev_val(unit.at(j), c))
                        act.dma_start(g_d[bass.ds(h * 4 + (j - 8), 1), :, c0:c0 + w].rearrange("a p t -> (a p) t"),
                                      gst[:, t % 2, 0:w]).then_inc(r_g_st[t % 2], 16)
                    t = s - 24
                    for b in (range(4) if s == 12 else [t] if 4 <= t < NS else []):
                        act.wait_ge(r_sst[b % 4], n2.at(b // 4) * 16 + 16)
                        act.wait_ge(r_so, prior(n8.at(0)) if b < 4 else done(n8.at(b - 4)))
                        act.dma_start(sring[:, b % 4, :, :],
                                      A["state_ret"][j_, b, bass.ds(h, 1), :, :]
                                      .rearrange("a (x p) v -> p (a x) v", p=P)).then_inc(r_sld[b % 4], 16)
                    if 0 <= t - 2 < NBLK:
                        r = t - 2
                        act.wait_ge(r_tr, done(ntr.at(18 + r)))
                        act.wait_ge(r_on_st[r % 2], n4.at(r // 2) * 16 + 16)
                        act.activation(onst[:, r % 2, :, :].rearrange("p d t -> p (d t)"), TR[:, :], ACT.Copy)\
                           .then_inc(r_te, 1)
                        act.wait_ge(r_te, done(ntr.at(18 + r)))
                        act.dma_start(on_d[bass.ds(h * 4, 4), :, r * P:(r + 1) * P].rearrange("d p t -> p d t"),
                                      onst[:, r % 2, :, :]).then_inc(r_on_st[r % 2], 16)
                    if 0 <= t - 1 < NBLK:
                        r = t - 1
                        act.wait_ge(r_o, done(n8.at(r)))
                        act.wait_ge(r_rs, prior(n8.at(r)))
                        act.activation(sqj[:, :], OB[:, :], ACT.Square, accum_out=osq[:, 0:1]).then_inc(r_sq, 1)
                    if 0 <= t - 1 < NS:
                        b = t - 1
                        act.wait_ge(r_hc, n1.at(0) * 16 + 16)
                        act.wait_ge(r_sld[b % 4], n2.at(b // 4) * 16 + 16)
                        sx = sring[:, b % 4, :, :].rearrange("p x v -> p (x v)")
                        act.activation(sx, sx, ACT.Copy, scale=gam).then_inc(r_sg, 1)
                    if 0 <= t - 1 < NBLK:
                        r = t - 1
                        act.wait_ge(r_rs, done(n8.at(r)))
                        act.wait_ge(r_tr, done(ntr.at(17 + r)))
                        act.activation(onb[:, :], OB[:, :], ACT.Copy, scale=o_r[:, 0:1]).then_inc(r_on, 1)
                    if 0 <= t - 2 < NS:
                        b = t - 2
                        act.wait_ge(r_sn, done(n8.at(b)))
                        act.dma_start(A["ret_state_sample"][j_, b, bass.ds(h, 1), :, :]
                                      .rearrange("a (x p) v -> p (a x) v", p=P), sring[:, b % 4, :, :])\
                           .then_inc(r_sst[b % 4], 16)
                    if t == 9:
                        act.wait_ge(r_su, done(n8.at(7)))
                        act.dma_start(A["ret_state_prompt"][j_, 0, bass.ds(h, 1), :, :]
                                      .rearrange("a (x p) v -> p (a x) v", p=P), St[:, :, :]).then_inc(r_S_st, 16)
                act.wait_ge(r_fo, done(n1.at(0)))
                act.dma_start(on_d[bass.ds(h * 4, 4), :, SEQ:T].rearrange("d p t -> p d t"), so[:, :, :])\
                   .then_inc(r_os_st, 16)

        def ret_dve(dve, ch, lay):
            with dve.Fori(0, RH) as h:
                unit, raw, n1, n8, ntr = ret_places(lay, h)
                ch.loop(h, 0, RCH)
                for s in range(36):
                    if 1 <= s <= 18:
                        js, cs = divmod(s - 1, NC_)
                        blks = [b for b, w in blocks_of(cs) if b < NBLK]
                        b0, nb = blks[0], len(blks)
                        if s == 1:
                            dve.wait_ge(r_hc, n1.at(0) * 16 + 16)
                        dve.wait_ge(r_tr, done(ntr.at(s - 1)))
                        src = TR[:, 0:nb * P].rearrange("p (b n) -> p b n", b=nb)
                        if js < 2:
                            nc.vector.tensor_scalar(ktok[:, b0:b0 + nb, js * P:(js + 1) * P], src, kdec, None,
                                                    ALU.mult).then_inc(r_te, 1)
                        else:
                            if cs == NC_ - 1:
                                nc.vector.tensor_copy(vs[0:NS, (js - 2) * P:(js - 1) * P], TR[0:NS, 256:384])
                            nc.vector.tensor_copy(vtok[:, b0:b0 + nb, (js - 2) * P:(js - 1) * P], src)\
                              .then_inc(r_te, 1)
                    t = s - 24
                    if 0 <= t - 1 < NBLK:
                        r = t - 1
                        dve.wait_ge(r_st, done(n8.at(r)))
                        if r == 0:
                            dve.wait_ge(r_S_st, n1.at(0) * 16 + 16)
                            nc.vector.tensor_copy(St[:, 0, :], SB0[:, :])
                            nc.vector.tensor_copy(St[:, 1, :], SB1[:, :]).then_inc(r_su, 1)
                        else:
                            dve.wait_ge(r_su, prior(n8.at(r)))
                            nc.vector.scalar_tensor_tensor(St[:, 0, :], St[:, 0, :], gamC, SB0[:, :], ALU.mult, ALU.add)
                            nc.vector.scalar_tensor_tensor(St[:, 1, :], St[:, 1, :], gamC, SB1[:, :], ALU.mult,
                                                           ALU.add).then_inc(r_su, 1)
                        dve.wait_ge(r_sq, done(n8.at(r)))
                        dve.wait_ge(r_on, prior(n8.at(r)))
                        rsqrt(dve, ch, osq[:, 0:1], 1.0 / RDV, o_r[:, 0:1], nt1, r_rs)
                    if 0 <= t < NBLK:
                        dve.wait_ge(r_sc, done(n8.at(t)))
                        nc.vector.tensor_tensor(sdT[:, t % 2, :], SC[:, 0:P], decT, ALU.mult).then_inc(r_sd, 1)
                        if t == 0:
                            dve.wait_ge(unit_ev, ev_val(unit.at(7), 2))
                        nc.vector.tensor_tensor(qdT[:, t % 2, :, :], qT[:, :, t * P:(t + 1) * P],
                                                qdec.rearrange("p (x n) -> p x n", x=1).to_broadcast([P, 2, P]),
                                                ALU.mult).then_inc(r_qd, 1)
                    if 0 <= t - 1 < NS:
                        b = t - 1
                        dve.wait_ge(r_vb, done(n8.at(b)))
                        dve.wait_ge(r_sg, done(n8.at(b)))
                        for x in range(2):
                            last = nc.vector.scalar_tensor_tensor(sring[:, b % 4, x, :], VB[:, :],
                                                                  kT[:, x, SEQ + b:SEQ + b + 1], sring[:, b % 4, x, :],
                                                                  ALU.mult, ALU.add)
                        last.then_inc(r_sn, 1)
                    if t == 10:
                        dve.wait_ge(r_so, done(n8.at(7)))
                        dve.wait_ge(r_os_st, n1.at(0) * 16 + 16)
                        ch.link(nc.vector.tensor_copy(so[:, :, :].rearrange("p d b -> p (d b)"), SC[:, P:P + 4 * NS]))
                        nc.vector.tensor_tensor(sq_s[:, :, :], so[:, :, :], so[:, :, :], ALU.mult).then_inc(r_fs, 1)
                    if t == 11:
                        dve.wait_ge(r_fin, done(n1.at(0)))
                        rsqrt(dve, ch, SC[:, 160:160 + NS], 1.0 / RDV, rs_s[:, :], nt)
                        nc.vector.tensor_tensor(so[:, :, :], so[:, :, :],
                                                rs_s[:, :].rearrange("p (x n) -> p x n", x=1).to_broadcast([P, 4, NS]),
                                                ALU.mult).then_inc(r_fo, 1)
            ch.done(RH)

        def ret_pool(pool, lay):
            with pool.Fori(0, RH) as h:
                unit = Pos(UNIT_AT[lay], h, RU_IN)
                for j in range(RU_IN):
                    split_lo(pool, unit, j + 1)

        PG = PAGES * P
        TX = SEQ + P
        al = arena()
        qf, kf = al.take(SEQ), al.take(SEQ)
        qtk, ktk = al.take(TX), al.take(TX)
        vf = al.take(NBLK, DV)
        strip = al.take(SEQ)
        sc2 = al.take(2, 2, SEQ)
        pT = al.take(2, NBLK, P)
        kring, vring = al.take(2, PG), al.take(2, PG)
        prod = pT.rearrange("p a b t -> p (a b t)")[:, 0:TX]
        dgst = al.take(2, WMAX)
        donst = al.take(2, P)
        donb = al.take(P)
        sb8 = al.take(SEQ)
        vs8 = al.take(P)
        gqb, gkb = al.take(64), al.take(64)
        sgf = al.take(1)
        lamv, lam2, negl = al.take(4, 64), al.take(2), al.take(1)
        ptab = al.take(NS * PAGES)
        rsk, rsn, ktmp = al.take(18), al.take(18), al.take(2, 18)
        stok = al.take(2, PAGES, NS)
        pTs = al.take(9 * NS)
        sself, smx, snm, sl, sef = (al.take(2) for _ in range(5))
        wself, diagw = al.take(1), al.take(NS)
        vsf, osm, osq2, ors, ont = al.take(NS), al.take(NS), al.take(NS), al.take(NS), al.take(2, NS)
        mx2, nm2, l2 = al.take(2, 2), al.take(2, 2), al.take(2, 2)
        rl0, ratio = al.take(2), al.take(1)
        dsq, dx, drs, rnt = al.take(1), al.take(1), al.take(1), al.take(2)
        es = sc2[:, 0, :, :]
        DTR, DOB, SOB = bank[4], bank[5], bank[1]
        DSC = [psum[:, 2:4, :].rearrange("p a n -> p (a n)"), psum[:, 6:8, :].rearrange("p a n -> p (a n)")]
        QB = DSC[1]
        d_ld, d_tab, d_set = sem("d_ld"), sem("d_tab"), sem("d_set")
        d_tr, d_te = sem("d_tr"), sem("d_te")
        d_kn = sem("d_kn")
        d_qb = sem("d_qb")
        d_kld, d_vld = sems("d_kld", 2), sems("d_vld", 2)
        d_ku, d_vu = sem("d_ku"), sem("d_vu")
        d_st, d_snm, d_sex, d_spc = sem("d_st"), sem("d_snm"), sem("d_sex"), sem("d_spc")
        d_so, d_ssq, d_sfin, d_sfo = sem("d_so"), sem("d_ssq"), sem("d_sfin"), sem("d_sfo")
        d_sc, d_mx, d_nm, d_ex, d_pc = sem("d_sc"), sem("d_mx"), sem("d_nm"), sem("d_ex"), sem("d_pc")
        d_o, d_sq, d_rs, d_on = sem("d_o"), sem("d_sq"), sem("d_rs"), sem("d_on")
        d_th = sem("d_th")
        d_gst, d_ost = sems("d_gst", 2), sems("d_ost", 2)
        d_kst, d_vst, d_sst, d_rows = sem("d_kst"), sem("d_vst"), sem("d_sst"), sem("d_rows")
        CREDITS += [(x, 1) for x in (d_tr, d_te, d_kn, d_qb, d_st, d_snm, d_sex, d_spc, d_so, d_ssq, d_sfin, d_sfo,
                                     d_sc, d_mx, d_nm, d_ex, d_pc, d_o, d_sq, d_rs, d_on, d_th)]
        CREDITS += [(x, 2) for x in (d_ku, d_vu)]
        CREDITS += [(x, 16) for x in (*d_gst, *d_ost, d_kst, d_vst, d_sst, d_rows)]

        DUSES = ([("T1", 0), ("T1", 1), ("T1", 2), ("T1", 3), ("T1", 4), ("T2q", 0), ("T2q", 1), ("T1", 5), ("T1", 6),
                  ("T1", 7), ("T2k", 0), ("T2k", 1), ("T1", 8), ("P", 0)])
        for t in range(1, 10):
            if t - 1 < NBLK:
                DUSES += [("B", t - 1, x) for x in range((t - 1) // 4 + 1)]
            if t >= 2:
                DUSES.append(("D", t - 2))
        DN = len(DUSES)
        T2_AT = {5: "T2q", 8: "T2k"}
        SLABS = {5: [0], 7: [1], 8: [2, 3], 9: [4], 10: [5, 6], 11: [7]}

        def diff_at(h):
            tr = Pos(0, h, DN)
            return (Pos(UNIT_AT[1], h, 4), Pos(RAW_AT[1], h, 4), Pos(0, h, 1), Pos(0, h, 2), Pos(0, h, 3), Pos(0, h, 4),
                    Pos(0, h, 8), Pos(0, h, 16), lambda *use: tr.at(DUSES.index(use)))

        def diff_sp(sp):
            win, wout = A["diff_w_in"][0], A["diff_w_out"][0]

            def slab(cache, ring, ld, used, n8, n4, h, b):
                sp.wait_ge(used, n8.at(b) + 1)
                hold(sp, "sp")
                for p in range(PAGES):
                    reg = sp.value_load(ptab[0:1, b * PAGES + p:b * PAGES + p + 1].bitcast(I32), min_val=0,
                                        max_val=A["cache_k"].shape[1] - 1)
                    sp.dma_start(ring[:, b % 2, p * P:(p + 1) * P],
                                 cache[0, bass.ds(reg, 1), :, bass.ds(h, 1), :].rearrange("a t c d -> (a t) (c d)"))\
                      .then_inc(ld[b % 2], 16)

            def weights(h, js):
                for j in js:
                    load_w(sp, Pos(RAW_AT[1], h, 4), j, w_block(win, 0, KT, h * P + j * D_MODEL))

            weights(0, (0, 1))
            sp.wait_ge(h_raw, fill_tiles(2, 2) + KT)
            sp.wait_ge(ss_done, KT * NC_ * 2)
            sp.dma_start(ptab[0:1, :].bitcast(I32), A["page_table"].rearrange("(a b) p -> a (b p)", a=1))\
              .then_inc(d_tab, 16)
            with nc.allow_non_contiguous_dma(reason="a gain by partition"):
                sp.dma_start(sgf, A["diff_sub_gain"].rearrange("a d -> d a")).then_inc(d_ld, 16)
            sp.dma_start(gqb, A["diff_q_gain"].to_broadcast([P, 64])).then_inc(d_ld, 16)
            sp.dma_start(gkb, A["diff_k_gain"].to_broadcast([P, 64])).then_inc(d_ld, 16)
            for x, name in enumerate(("diff_lam_q1", "diff_lam_k1", "diff_lam_q2", "diff_lam_k2")):
                sp.dma_start(lamv[:, x, :], A[name].to_broadcast([P, 64])).then_inc(d_ld, 16)
            sp.dma_start(strip, A["c_dist"]).then_inc(d_ld, 16)
            sp.dma_start(sb8[0:NS, :], A["c_sdist"]).then_inc(d_ld, 16)
            sp.wait_ge(d_tab, 16)

            def head(h):
                unit, raw, n1, n2, n3, n4, n8, n16, tr = diff_at(h)
                for b in range(NS):
                    if b == 2:
                        weights(h, (2, 3))
                    slab(A["cache_k"], kring, d_kld, d_ku, n8, n4, h, b)
                for b in range(NS):
                    slab(A["cache_v"], vring, d_vld, d_vu, n8, n4, h, b)

            with sp.Fori(0, DH - 1) as h:
                head(h)
                weights(h + 1, (0, 1))
            head(DH - 1)
            out_sp(sp, 1, wout, UNIT_AT[1] + 32, RAW_AT[1] + 32, [(4, 0)], diff_stage_wait)

        def diff_stage_wait(sp, lay):
            for x in range(2):
                sp.wait_ge(d_gst[x], 16 * DH * (2 - x) + 16)
                sp.wait_ge(d_ost[x], 16 * 4 * DH + 16)
            for x in (d_kst, d_vst, d_sst):
                sp.wait_ge(x, 16 * DH + 16)
            sp.wait_ge(d_rows, 32 * DH + 16)
            sp.wait_ge(d_sfo, done(DH - 1))
            sp.wait_ge(d_te, done(DN * DH - 1))

        def diff_pe(pe):
            f = FILL_AT[1]
            with pe.Fori(0, DH) as h:
                unit, raw, n1, n2, n3, n4, n8, n16, tr = diff_at(h)

                def transposes(*use):
                    pe.wait_ge(d_te, prior(tr(*use)))

                for s in range(13):
                    j, c = divmod(s, NC_)
                    if s < 12:
                        unit_chunk(pe, unit, j, c, f)
                    if 1 <= s <= 9:
                        js, cs = divmod(s - 1, NC_)
                        c0 = CHUNKS[cs][0]
                        pe.wait_ge(unit_ev, ev_val(unit.at(js), cs))
                        transposes("T1", s - 1)
                        for b, w in blocks_of(cs):
                            o = b * P - c0
                            last = nc.tensor.transpose(DTR[0:w, o:o + P], hraw[:, (s - 1) % 2, o:o + w], ident[:, :])
                        last.then_inc(d_tr, 1)
                    if s == 5:
                        pe.wait_ge(d_kn, done(n2.at(0)))
                        pe.wait_ge(d_mx, prior(n16.at(0)))
                        for b in range(NS):
                            last = nc.tensor.matmul(QB[:, b * P:(b + 1) * P], ident[0:NS, b:b + 1].to_broadcast([NS, P]),
                                                    qtk[0:NS, SEQ:TX], start=True, stop=True)
                        last.then_inc(d_qb, 1)
                    if s in T2_AT:
                        x = (5, 8).index(s)
                        src = (qtk, ktk)[x]
                        pe.wait_ge(d_kn, done(n2.at(x)))
                        for half in range(2):
                            transposes(T2_AT[s], half)
                            for y in range(4):
                                b = 4 * half + y
                                last = nc.tensor.transpose(DTR[:, y * P:(y + 1) * P], src[:, b * P:(b + 1) * P],
                                                           ident[:, :])
                            last.then_inc(d_tr, 1)
                pe.wait_ge(d_ku, n8.at(7) + 3)
                hold(pe, "pe")
                for m in range(2):
                    for p in range(PAGES):
                        last = nc.tensor.transpose(DSC[m][0:NS, p * P:(p + 1) * P], stok[:, m, p, :], ident[:, :])
                last.then_inc(d_st, 1)
                pe.wait_ge(d_spc, done(n1.at(0)))
                transposes("P", 0)
                hold(pe, "pe")
                for p in range(PAGES):
                    nc.tensor.transpose(DTR[:, p * NS:(p + 1) * NS], es[0:NS, 0, p * P:(p + 1) * P], ident[0:NS, 0:NS])
                nc.tensor.matmul(DTR[:, 64:72], ones[0:NS, :], diagw[0:NS, :], start=True, stop=True).then_inc(d_tr, 1)
                for t in range(10):
                    if t < NBLK:
                        W = (t + 1) * P
                        for m in range(2):
                            pe.wait_ge(d_mx, prior(n16.at(2 * t + m)) - (1 if (t, m) != (0, 0) else 0))
                            if t == 0:
                                pe.wait_ge(d_snm, done(n1.at(0)))
                                pe.wait_ge(d_te, done(tr("T2k", 1)))
                            for a in range(0, W, 512):
                                e = min(W, a + 512)
                                last = nc.tensor.matmul(DSC[m][:, a:e], qf[64 * m:64 * m + 64, t * P:(t + 1) * P],
                                                        kf[64 * m:64 * m + 64, a:e], start=True, stop=True)
                            last.then_inc(d_sc, 1)
                    if 1 <= t <= NBLK:
                        tb = t - 1
                        pe.wait_ge(d_pc, done(n8.at(tb)))
                        for half in range(tb // 4 + 1):
                            transposes("B", tb, half)
                            for y in range(min(4, tb + 1 - 4 * half)):
                                b = 4 * half + y
                                last = nc.tensor.transpose(DTR[:, y * P:(y + 1) * P],
                                                           sc2[:, tb % 2, 0, b * P:(b + 1) * P], ident[:, :])
                            last.then_inc(d_tr, 1)
                    if t < NS:
                        if t == 0:
                            pe.wait_ge(d_te, done(tr("P", 0)))
                            pe.wait_ge(unit_ev, ev_val(unit.at(3), 2))
                        pe.wait_ge(d_vld[t % 2], (n4.at(t // 2) * PAGES) * 16 + 16 * PAGES)
                        for p in range(PAGES):
                            last = nc.tensor.matmul(SOB[:, t:t + 1], vring[:, t % 2, p * P:(p + 1) * P],
                                                    pTs[:, p * NS + t:p * NS + t + 1], start=(p == 0),
                                                    stop=(p == PAGES - 1))
                        last.then_inc(d_vu, 1)
                    if 1 <= t <= NBLK:
                        tb = t - 1
                        if tb == 0:
                            pe.wait_ge(d_te, done(tr("T1", 8)))
                        pe.wait_ge(d_te, done(tr("B", tb, tb // 4)))
                        pe.wait_ge(d_on, prior(n8.at(tb)))
                        for b in range(tb + 1):
                            last = nc.tensor.matmul(DOB[:, 0:P], pT[:, tb % 2, b, :], vf[:, b, :], start=(b == 0),
                                                    stop=(b == tb))
                        last.then_inc(d_o, 1)
                    if t >= 2:
                        pe.wait_ge(d_on, done(n8.at(t - 2)))
                        transposes("D", t - 2)
                        nc.tensor.transpose(DTR[:, 0:P], donb, ident[:, :]).then_inc(d_tr, 1)
                pe.wait_ge(d_ssq, done(n1.at(0)))
                nc.tensor.matmul(SOB[:, 16:16 + NS], ones[:, :], osq2, start=True, stop=True).then_inc(d_sfin, 1)
                pe.wait_ge(d_sfo, done(n1.at(0)))
            out_pe(pe, 1, UNIT_AT[1] + 32, [(4, 0)], LAST == 1)

        def diff_act(act):
            act.wait_ge(d_set, 1)
            act.activation(lam2, lam2, ACT.Exp).then_inc(d_set, 1)
            act.wait_ge(h_lo, fill_tiles(FILL_AT[1], 2) + KT)
            with act.Fori(0, DH) as h:
                unit, raw, n1, n2, n3, n4, n8, n16, tr = diff_at(h)
                for s in range(12):
                    j, c = divmod(s, NC_)
                    c0, w = CHUNKS[c]
                    if c == 0 and j < 3:
                        split_hi(act, unit, raw, j + 1)
                    src = unit_bank(j, c)[:, 0:w]
                    act.wait_ge(unit_ps, ps_val(unit.at(j), c))
                    if j < 3:
                        if s >= 2:
                            act.wait_ge(d_tr, done(tr("T1", s - 2)))
                        act.activation(hraw[:, s % 2, 0:w], src, ACT.Copy).then_inc(unit_ev, 1)
                    else:
                        act.wait_ge(d_gst[0] if c != 1 else d_gst[1],
                                    (n2.at(0) if c == 0 else n1.at(0) if c == 1 else n2.at(1)) * 16 + 16)
                        act.activation(dgst[:, c % 2, 0:w], src, ACT.Tanh, scale=0.5).then_inc(d_th, 1)
                        act.wait_ge(unit_ev, ev_val(unit.at(j), c))
                        act.dma_start(g_d[bass.ds(h, 1), :, c0:c0 + w].rearrange("a p t -> (a p) t"),
                                      dgst[:, c % 2, 0:w]).then_inc(d_gst[c % 2], 16)
                    if s in T2_AT:
                        dst = (qf, kf)[(5, 8).index(s)]
                        for half in range(2):
                            act.wait_ge(d_tr, done(tr(T2_AT[s], half)))
                            act.activation(dst[:, half * 512:(half + 1) * 512], DTR[:, :], ACT.Copy).then_inc(d_te, 1)
                    if s == 8:
                        act.wait_ge(d_kn, done(n2.at(1)))
                        act.dma_start(A["k_rows_prompt"][0, 0, :, bass.ds(h, 1), :]
                                      .rearrange("(b p) a d -> p b (a d)", p=P),
                                      ktk[:, 0:SEQ].rearrange("p (b d) -> p b d", b=NBLK)).then_inc(d_kst, 16)
                        act.dma_start(A["k_rows_sample"][0, :, 0, bass.ds(h, 1), :].rearrange("b a d -> b (a d)"),
                                      ktk[0:NS, SEQ:TX]).then_inc(d_rows, 16)
                    if s == 10:
                        act.wait_ge(d_te, done(tr("T1", 8)))
                        act.dma_start(A["v_rows_prompt"][0, 0, :, bass.ds(h, 1), :]
                                      .rearrange("(b p) a d -> p b (a d)", p=P), vf).then_inc(d_vst, 16)
                        act.dma_start(A["v_rows_sample"][0, :, 0, bass.ds(h, 1), :].rearrange("b a d -> b (a d)"),
                                      vs8[0:NS, :]).then_inc(d_rows, 16)
                act.wait_ge(d_snm, done(n1.at(0)))
                for m in range(2):
                    act.activation(es[0:NS, m, :], es[0:NS, m, :], ACT.Exp, bias=snm[0:NS, m:m + 1],
                                   accum_out=sl[0:NS, m:m + 1])
                for m in range(2):
                    last = act.activation(sef[0:NS, m:m + 1], sself[0:NS, m:m + 1], ACT.Exp, bias=snm[0:NS, m:m + 1])
                last.then_inc(d_sex, 1)
                for t in range(10):
                    if t < NBLK:
                        W = (t + 1) * P
                        act.wait_ge(d_nm, done(n8.at(t)))
                        for m in range(2):
                            act.activation(sc2[:, t % 2, m, 0:W], sc2[:, t % 2, m, 0:W], ACT.Exp,
                                           bias=nm2[:, t % 2, m:m + 1], accum_out=l2[:, t % 2, m:m + 1]).then_inc(d_ex, 1)
                    if t >= 2:
                        act.wait_ge(d_rs, done(n8.at(t - 2)))
                        if t == 2:
                            act.wait_ge(d_tr, tr("D", 0))
                        else:
                            act.wait_ge(d_tr, done(tr("D", t - 3)))
                        act.activation(donb, DOB[:, 0:P], ACT.Copy, scale=drs).then_inc(d_on, 1)
                    if 1 <= t <= NBLK:
                        tb = t - 1
                        for half in range(tb // 4 + 1):
                            act.wait_ge(d_tr, done(tr("B", tb, half)))
                            nb = min(4, tb + 1 - 4 * half)
                            act.activation(pT[:, tb % 2, 4 * half:4 * half + nb, :].rearrange("p b t -> p (b t)"),
                                           DTR[:, 0:nb * P], ACT.Copy).then_inc(d_te, 1)
                        act.wait_ge(d_o, done(n8.at(tb)))
                        act.activation(hraw[:, 0, 0:P], DOB[:, 0:P], ACT.Square, accum_out=dsq).then_inc(d_sq, 1)
                    if t >= 2:
                        tb = t - 2
                        act.wait_ge(d_tr, done(tr("D", tb)))
                        act.wait_ge(d_ost[tb % 2], n4.at(tb // 2) * 16 + 16)
                        act.activation(donst[:, tb % 2, :], DTR[:, 0:P], ACT.Copy, scale=sgf).then_inc(d_te, 1)
                        act.wait_ge(d_te, done(tr("D", tb)))
                        act.dma_start(on_d[bass.ds(h, 1), :, tb * P:(tb + 1) * P].rearrange("a p t -> (a p) t"),
                                      donst[:, tb % 2, :]).then_inc(d_ost[tb % 2], 16)
                split_hi(act, unit, raw, 4)
                act.wait_ge(d_sfo, done(n1.at(0)))
                act.dma_start(on_d[bass.ds(h, 1), :, SEQ:T].rearrange("a p t -> (a p) t"), osm).then_inc(d_sst, 16)
            out_act(act, 1, UNIT_AT[1] + 32, RAW_AT[1] + 32, [(4, 0)], LAST == 1)

        DCH_PER = 191

        def diff_dve(dve, ch):
            dve.wait_ge(d_ld, 16 * 9)
            ch.link(nc.vector.tensor_tensor(prod[:, 0:P].rearrange("p (a d) -> p a d", a=2), lamv[:, 0:4:2, :],
                                            lamv[:, 1:4:2, :], ALU.mult))
            nc.vector.tensor_reduce(lam2, prod[:, 0:P].rearrange("p (a d) -> p a d", a=2), AX.X, ALU.add)\
              .then_inc(d_set, 1)
            nc.vector.tensor_scalar(gqb, gqb, 0.125, None, ALU.mult)
            nc.vector.tensor_scalar(sgf, sgf, 1.0 - LAM_INIT, None, ALU.mult)
            ch.link(nc.vector.memset(qtk, 0.0))
            ch.link(nc.vector.memset(ktk, 0.0))
            dve.wait_ge(d_set, 2)
            ch.link(nc.vector.scalar_tensor_tensor(negl, lam2[:, 1:2], -LAM_INIT, lam2[:, 0:1], ALU.add, ALU.subtract))

            with dve.Fori(0, DH) as h:
                unit, raw, n1, n2, n3, n4, n8, n16, tr = diff_at(h)
                ch.loop(h, 0, DCH_PER)
                ch.link(nc.vector.tensor_scalar(strip, strip, 0.5, None, ALU.mult))
                ch.link(nc.vector.tensor_scalar(sb8[0:NS, :], sb8[0:NS, :], 0.5, None, ALU.mult))
                for s in range(12):
                    if 1 <= s <= 9:
                        js, cs = divmod(s - 1, NC_)
                        c0 = CHUNKS[cs][0]
                        dst = (qtk, ktk, vf.rearrange("p b d -> p (b d)"))[js]
                        nb = 3 if cs < 2 else 2
                        dve.wait_ge(d_tr, done(tr("T1", s - 1)))
                        if s == 4:
                            dve.wait_ge(d_kst, n1.at(0) * 16 + 16)
                            dve.wait_ge(d_rows, n2.at(0) * 16 + 16)
                        if s == 7:
                            dve.wait_ge(d_vst, n1.at(0) * 16 + 16)
                        if cs == 2:
                            x = (qtk[0:NS, SEQ:TX], ktk[0:NS, SEQ:TX], vs8[0:NS, :])[js]
                            nc.vector.tensor_copy(x, DTR[0:NS, 256:384])
                        if s == 9:
                            nc.vector.tensor_copy(vsf, hraw[:, 0, 256:264])
                        ins = nc.vector.tensor_copy(dst[:, c0:c0 + nb * P], DTR[:, 0:nb * P])
                        ins.then_inc(d_te, 1)
                    if s in (3, 6):
                        x = s // 3 - 1
                        v, gain = ((qtk, gqb), (ktk, gkb))[x]
                        dve.wait_ge(d_te, done(tr("T1", s - 1)))
                        g3 = v.rearrange("p (g d) -> p g d", d=64)
                        ch.link(nc.vector.tensor_tensor(prod, v, v, ALU.mult))
                        ch.link(nc.vector.tensor_reduce(rsk, prod.rearrange("p (g d) -> p g d", d=64), AX.X, ALU.add))
                        rsqrt(dve, ch, rsk, 1.0 / 64, rsn, ktmp)
                        ch.link(nc.vector.tensor_tensor(g3, g3, rsn.rearrange("p (g a) -> p g a", a=1)
                                                        .to_broadcast([P, 18, 64]), ALU.mult))
                        ins = nc.vector.tensor_tensor(g3, g3, gain.rearrange("p (a d) -> p a d", a=1)
                                                      .to_broadcast([P, 18, 64]), ALU.mult)
                        ins.then_inc(d_kn, 1)
                        if x == 1:
                            dve.wait_ge(d_kn, done(n2.at(1)))
                            ch.link(nc.vector.tensor_tensor(prod[0:NS, 0:P], qtk[0:NS, SEQ:TX], ktk[0:NS, SEQ:TX],
                                                            ALU.mult))
                            ch.link(nc.vector.tensor_reduce(sself[0:NS, :],
                                                            prod[0:NS, 0:P].rearrange("p (g d) -> p g d", d=64),
                                                            AX.X, ALU.add))
                    if s >= 9:
                        c = s - 9
                        w = CHUNKS[c][1]
                        dve.wait_ge(d_th, done(n3.at(c)))
                        dve.wait_ge(unit_ev, ev_val(unit.at(3), c) - 1)
                        nc.vector.scalar_tensor_tensor(dgst[:, c % 2, 0:w], dgst[:, c % 2, 0:w], 1.0,
                                                       unit_bank(3, c)[:, 0:w], ALU.add, ALU.mult).then_inc(unit_ev, 1)
                    for b in SLABS.get(s, []):
                        if b == 0:
                            dve.wait_ge(d_qb, done(n1.at(0)))
                        dve.wait_ge(d_kld[b % 2], (n4.at(b // 2) * PAGES) * 16 + 16 * PAGES)
                        ch.link(nc.vector.tensor_tensor(
                            prod[:, 0:PG].rearrange("p (g d) -> p g d", g=PAGES),
                            kring[:, b % 2, :].rearrange("p (g d) -> p g d", g=PAGES),
                            QB[:, b * P:(b + 1) * P].rearrange("p (a d) -> p a d", a=1).to_broadcast([P, PAGES, P]),
                            ALU.mult))
                        nc.vector.tensor_reduce(stok[:, :, :, b].rearrange("p m g -> p g m"),
                                                prod[:, 0:PG].rearrange("p (g m d) -> p g m d", g=PAGES, m=2),
                                                AX.X, ALU.add).then_inc(d_ku, 1)
                        dve.wait_ge(d_ku, n8.at(b) + 3)
                dve.wait_ge(d_st, done(n1.at(0)))
                hold(dve, "dve")
                for m in range(2):
                    last = nc.vector.tensor_tensor_reduce(
                        out=es[0:NS, m, :], in0=DSC[m][0:NS, :], in1=sb8[0:NS, :], scale=1.0, scalar=-1e30, op0=ALU.add,
                        op1=ALU.max, accum_out=smx[0:NS, m:m + 1])
                ch.link(last)
                ch.link(nc.vector.tensor_tensor(smx[0:NS, :], smx[0:NS, :], sself[0:NS, :], ALU.max))
                nc.vector.tensor_scalar(snm[0:NS, :], smx[0:NS, :], -1.0, None, ALU.mult).then_inc(d_snm, 1)
                dve.wait_ge(d_sex, done(n1.at(0)))
                ch.link(nc.vector.tensor_tensor(sl[0:NS, :], sl[0:NS, :], sef[0:NS, :], ALU.add))
                ch.link(nc.vector.reciprocal(sl[0:NS, :], sl[0:NS, :]))
                ch.link(nc.vector.tensor_tensor(sl[0:NS, 1:2], sl[0:NS, 1:2], negl[0:NS, :], ALU.mult))
                nc.vector.tensor_scalar(es[0:NS, 1, :], es[0:NS, 1, :], sl[0:NS, 1:2], None, ALU.mult)
                ch.link(nc.vector.tensor_scalar(wself[0:NS, :], sef[0:NS, 1:2], sl[0:NS, 1:2], None, ALU.mult))
                ch.link(nc.vector.scalar_tensor_tensor(wself[0:NS, :], sef[0:NS, 0:1], sl[0:NS, 0:1], wself[0:NS, :],
                                                       ALU.mult, ALU.add))
                nc.vector.tensor_scalar(diagw[0:NS, :], ident[0:NS, 0:NS], wself[0:NS, :], None, ALU.mult)
                nc.vector.scalar_tensor_tensor(es[0:NS, 0, :], es[0:NS, 0, :], sl[0:NS, 0:1], es[0:NS, 1, :],
                                               ALU.mult, ALU.add).then_inc(d_spc, 1)
                dve.wait_ge(d_tr, done(tr("P", 0)))
                nc.vector.tensor_copy(pTs, DTR[:, 0:72]).then_inc(d_te, 1)
                dve.wait_ge(d_te, done(tr("P", 0)))
                for t in range(10):
                    if t >= 2:
                        tb = t - 2
                        dve.wait_ge(d_sq, done(n8.at(tb)))
                        r = rl0[:, tb % 2:tb % 2 + 1]
                        ch.link(nc.vector.scalar_tensor_tensor(dx, dsq, r, r, ALU.mult, ALU.mult))
                        if tb:
                            dve.wait_ge(d_on, done(n8.at(tb - 1)))
                        rsqrt(dve, ch, dx, 1.0 / DV, drs, rnt)
                        nc.vector.tensor_tensor(drs, drs, r, ALU.mult).then_inc(d_rs, 1)
                    if t < NBLK:
                        W = (t + 1) * P
                        for m in range(2):
                            dve.wait_ge(d_sc, done(n16.at(2 * t + m)))
                            if t >= 2 and m == 0:
                                dve.wait_ge(d_tr, done(tr("B", t - 2, (t - 2) // 4)))
                            hold(dve, "dve")
                            nc.vector.tensor_tensor_reduce(
                                out=sc2[:, t % 2, m, 0:W], in0=DSC[m][:, 0:W], in1=strip[:, SEQ - W:SEQ], scale=1.0,
                                scalar=-1e30, op0=ALU.add, op1=ALU.max, accum_out=mx2[:, t % 2, m:m + 1])\
                              .then_inc(d_mx, 1)
                        dve.wait_ge(d_mx, done(n16.at(2 * t + 1)))
                        nc.vector.tensor_scalar(nm2[:, t % 2, :], mx2[:, t % 2, :], -1.0, None, ALU.mult)\
                          .then_inc(d_nm, 1)
                    if 1 <= t <= NBLK:
                        tb = t - 1
                        W = t * P
                        dve.wait_ge(d_ex, done(n16.at(2 * tb + 1)))
                        ch.link(nc.vector.reciprocal(ratio, l2[:, tb % 2, 1:2]))
                        nc.vector.reciprocal(rl0[:, tb % 2:tb % 2 + 1], l2[:, tb % 2, 0:1])
                        ch.link(nc.vector.tensor_tensor(ratio, ratio, l2[:, tb % 2, 0:1], ALU.mult))
                        ch.link(nc.vector.tensor_tensor(ratio, ratio, negl, ALU.mult))
                        nc.vector.scalar_tensor_tensor(sc2[:, tb % 2, 0, 0:W], sc2[:, tb % 2, 1, 0:W], ratio,
                                                       sc2[:, tb % 2, 0, 0:W], ALU.mult, ALU.add).then_inc(d_pc, 1)
                dve.wait_ge(d_vu, n8.at(7) + 3)
                dve.wait_ge(d_sst, n1.at(0) * 16 + 16)
                ch.link(nc.vector.tensor_tensor(osm, vsf, pTs[:, 64:72], ALU.mult))
                ch.link(nc.vector.tensor_tensor(osm, osm, SOB[:, 0:NS], ALU.add))
                nc.vector.tensor_tensor(osq2, osm, osm, ALU.mult).then_inc(d_ssq, 1)
                dve.wait_ge(d_sfin, done(n1.at(0)))
                rsqrt(dve, ch, SOB[:, 16:16 + NS], 1.0 / DV, ors, ont)
                nc.vector.scalar_tensor_tensor(osm, osm, sgf, ors, ALU.mult, ALU.mult).then_inc(d_sfo, 1)
            ch.done(DH)
            out_dve(dve, ch, 1, UNIT_AT[1] + 32, [(4, 0)], LAST == 1, 0.5)

        def diff_pool(pool):
            with pool.Fori(0, DH) as h:
                unit = Pos(UNIT_AT[1], h, 4)
                for j in range(4):
                    split_lo(pool, unit, j + 1)
            out_pool(pool, 1, UNIT_AT[1] + 32, [(4, 0)], LAST == 1)

        LC0, LH0, LW, LB, LBA, LBX, LY, LNY = 0, 24, 32, 36, 37, 38, 39, 40
        NPAR, NOUT = 40, 36
        OH, OC, OHS, OCS = 0, 1, 4, 12
        al = arena()
        lrow = al.take(LRU_W)
        lpar = al.take(LRU_B, NPAR + 1)
        lout = al.take(LRU_B, NOUT)
        lrow2 = al.take(LRU_W)
        lp, lo = al.take(NPAR + 1), al.take(NOUT)
        xpad = al.take(3 + SEQ)
        xs8 = al.take(NS)
        xcv, gtr, gti, ga, gm, hb = (al.take(T) for _ in range(6))
        lgst = al.take(2, WMAX)
        wax = al.take(2, 2, P)
        sp_ = [al.take(LRU_B) for _ in range(6)]
        tmp_s = al.take(NS)
        LTR = bank[2]
        l_ld, l_set, l_ptr, l_z = sem("l_ld"), sem("l_set"), sem("l_ptr"), sem("l_z")
        l_xc = sem("l_xc")
        l_gt, l_tg = sem("l_gt"), sem("l_tg")
        l_at, l_m, l_sq, l_h = sem("l_at"), sem("l_m"), sem("l_sq"), sem("l_h")
        l_th = sem("l_th")
        l_wl = sems("l_wl", 2)
        l_gst, l_hst, l_ost = sems("l_gst", 2), sem("l_hst"), sem("l_ost")
        l_otr, l_oev = sem("l_otr"), sem("l_oev")
        CREDITS += [(x, 1) for x in (l_xc, l_tg, l_at, l_m, l_sq, l_h, l_th)] + [(l_gt, 12)]
        CREDITS += [(x, 16) for x in (*l_gst, l_hst)]
        LU, LF = UNIT_AT[2], FILL_AT[2]

        def lru_at(n):
            return (Pos(LU, n, 2), Pos(0, n, 1), Pos(0, n, 2), Pos(0, n, 3), Pos(0, n, 6))

        def store_states(sp, n):
            sp.wait_ge(l_h, n + 2)
            sp.dma_start(on_d[bass.ds(n, 1), :, :].rearrange("a p t -> (a p) t"), hb).then_inc(l_hst, 16)

        def lru_sp(sp):
            win, wout = A["lru_w_in"][0], A["lru_w_out"][0]

            def weights(n):
                for j in range(2):
                    load_w(sp, Pos(LU, n, 2), j, w_block(win, 0, KT, n * P + j * LRU_W))

            def gates(n, slot):
                for x, name in enumerate(("lru_wa", "lru_wx")):
                    sp.dma_start(wax[:, slot, x, :], A[name][0, bass.ds(n, 1), :, :].rearrange("a c d -> (a c) d"))\
                      .then_inc(l_wl[slot], 16)

            weights(0)
            sp.wait_ge(h_raw, fill_tiles(4, 2) + KT)
            sp.wait_ge(ss_done, KT * NC_ * 3)
            rows = 0
            for name in ("state_lru_conv", "state_lru_h", "lru_conv_w", "lru_conv_b", "lru_ba", "lru_bx", "lru_lambda"):
                src = {"state_lru_conv": lambda a: a[0].rearrange("b r w -> (b r) w"),
                       "state_lru_h": lambda a: a[0], "lru_conv_w": lambda a: a[0]}.get(name, lambda a: a)(A[name])
                sp.dma_start(lrow[rows:rows + src.shape[0], :], src).then_inc(l_ld, 16)
                rows += src.shape[0]
            gates(0, 0)
            gates(1, 1)

            def block_pair(n, more):
                for x in range(2):
                    if more or x == 0:
                        weights(n + (x + 1))
                        store_states(sp, n + x)
                    if more:
                        gates(n + (x + 2), x)

            with sp.Fori(0, LRU_B // 2 - 1) as i:
                block_pair(i * 2, True)
            block_pair(LRU_B - 2, False)
            out_sp(sp, 2, wout, LU + LRU_IN, LU + LRU_IN, [(6, 0), (7, KT)], lru_stage_wait)

        def lru_stage_wait(sp, lay):
            store_states(sp, LRU_B - 1)
            sp.wait_ge(l_hst, 16 * LRU_B + 16)
            for x in range(2):
                sp.wait_ge(l_gst[x], 16 * LRU_B * (2 - x) + 16)
            sp.wait_ge(l_ost, 16 * 4)

        def lru_pe(pe):
            pe.wait_ge(l_ld, 16 * 7)
            for n in range(LRU_B):
                last = nc.tensor.transpose(LTR[:, n * NPAR:(n + 1) * NPAR], lrow[0:NPAR, n * P:(n + 1) * P],
                                           ident[0:NPAR, 0:NPAR])
            last.then_inc(l_ptr, 1)
            pe.wait_ge(l_set, 1)

            def block(n, slot, pair):
                unit, n1, n2, n3, n6 = lru_at(n)
                for s in range(6):
                    unit_chunk(pe, unit, s // NC_, s % NC_, LF)
                    if s == 4:
                        pe.wait_ge(l_xc, done(n1.at(0)))
                        pe.wait_ge(l_wl[slot], pair * 32 + 32)
                        pe.wait_ge(l_tg, prior(n6.at(0)))
                        for c in range(NC_):
                            c0, w = CHUNKS[c]
                            for x in range(2):
                                nc.tensor.matmul(bank[2 + 3 * x + c][:, 0:w], wax[:, slot, x, :], xcv[:, c0:c0 + w],
                                                 start=True, stop=True).then_inc(l_gt, 1)

            with pe.Fori(0, LRU_B // 2) as i:
                block(i * 2, 0, i)
                block(i * 2 + 1, 1, i)
            pe.wait_ge(l_h, done(LRU_B - 1))
            pe.wait_ge(l_tg, done(6 * LRU_B - 1))
            pe.wait_ge(l_oev, 1)
            for n in range(LRU_B):
                last = nc.tensor.transpose(bank[2 + n // 4][0:NOUT, (n % 4) * P:(n % 4 + 1) * P], lout[:, n, :], ident[:, :])
            last.then_inc(l_otr, 1)
            out_pe(pe, 2, LU + LRU_IN, [(6, 0), (7, KT)], LAST == 2)

        def lru_act(act):
            act.wait_ge(l_z, 1)
            act.activation(sp_[1], sp_[1], ACT.Exp).then_inc(l_z, 1)

            def block(n):
                unit, n1, n2, n3, n6 = lru_at(n)

                def g_tanh(c):
                    w = CHUNKS[c][1]
                    act.wait_ge(unit_ps, ps_val(unit.at(1), c))
                    act.wait_ge(l_gst[c % 2], (n1.at(0) if c == 1 else n2.at(c // 2)) * 16 + 16)
                    act.activation(lgst[:, c % 2, 0:w], unit_bank(1, c)[:, 0:w], ACT.Tanh, scale=0.5).then_inc(l_th, 1)

                def g_store(c):
                    c0, w = CHUNKS[c]
                    act.wait_ge(unit_ev, ev_val(unit.at(1), c))
                    act.dma_start(g_d[bass.ds(n, 1), :, c0:c0 + w].rearrange("a p t -> (a p) t"), lgst[:, c % 2, 0:w])\
                       .then_inc(l_gst[c % 2], 16)

                split_hi(act, unit, unit, 1)
                act.wait_ge(l_xc, prior(n1.at(0)))
                for c in range(NC_):
                    c0, w = CHUNKS[c]
                    act.wait_ge(unit_ps, ps_val(unit.at(0), c))
                    wp = min(w, SEQ - c0)
                    if wp < w:
                        act.activation(xs8, unit_bank(0, c)[:, wp:w], ACT.Copy)
                    act.activation(xpad[:, 3 + c0:3 + c0 + wp], unit_bank(0, c)[:, 0:wp], ACT.Copy).then_inc(unit_ev, 1)
                split_hi(act, unit, unit, 2)
                g_tanh(0)
                g_tanh(1)
                g_store(0)
                g_store(1)
                for c in range(NC_):
                    c0, w = CHUNKS[c]
                    for x in range(2):
                        act.wait_ge(l_gt, n6.at(2 * c + x) + 13)
                        act.activation((gtr, gti)[x][:, c0:c0 + w], bank[2 + 3 * x + c][:, 0:w], ACT.Tanh, scale=0.5,
                                       bias=lp[:, LBA + x:LBA + x + 1]).then_inc(l_tg, 1)
                act.wait_ge(l_tg, done(n6.at(5)))
                act.wait_ge(l_h, prior(n1.at(0)))
                act.activation(ga, gtr, ACT.Exp, scale=lp[:, LNY:LNY + 1], bias=lp[:, LNY:LNY + 1])
                act.activation(gtr, gtr, ACT.Tanh, scale=lp[:, LY:LY + 1], bias=lp[:, LY:LY + 1]).then_inc(l_at, 1)
                g_tanh(2)
                act.wait_ge(l_m, done(n1.at(0)))
                act.activation(gm, gm, ACT.Sqrt, scale=0.25).then_inc(l_sq, 1)
                g_store(2)

            with act.Fori(0, LRU_B) as n:
                block(n)
            act.wait_ge(l_otr, 1)
            for x in range(3):
                last = act.activation(lrow2[0:NOUT, x * 512:(x + 1) * 512], bank[2 + x][0:NOUT, :], ACT.Copy)
            last.then_inc(l_otr, 1)
            act.wait_ge(l_otr, 2)
            for name, at, n in (("lru_h_prompt", OH, 1), ("lru_conv_prompt", OC, 3), ("lru_h_sample", OHS, NS),
                                ("lru_conv_sample", OCS, 3 * NS)):
                dst = A[name][0] if len(A[name].shape) == 3 else A[name] if n == 1 else A[name][0]
                if name == "lru_conv_prompt":
                    dst = A[name][0, 0]
                if name == "lru_conv_sample":
                    dst = A[name][0].rearrange("b r w -> (b r) w")
                act.dma_start(dst, lrow2[at:at + n, :]).then_inc(l_ost, 16)
            out_act(act, 2, LU + LRU_IN, LU + LRU_IN, [(6, 0), (7, KT)], LAST == 2)

        LCH_PER = 9

        def lru_dve(dve, ch):
            dve.wait_ge(l_ptr, 1)
            nc.vector.memset(xpad[:, 0:3], 0.0)
            ch.link(nc.vector.tensor_copy(lpar[:, :, 0:NPAR], LTR[:, 0:LRU_B * NPAR].rearrange("p (n c) -> p n c", n=LRU_B)))
            lam, z, s, q, p, neg = sp_
            ch.link(nc.vector.tensor_copy(lam, lpar[:, :, LY]))
            ch.link(nc.vector.tensor_scalar(neg, lam, -1.0, None, ALU.mult))
            nc.vector.tensor_tensor(z, lam, neg, ALU.min).then_inc(l_z, 1)
            dve.wait_ge(l_z, 2)
            ch.link(nc.vector.tensor_scalar(s, z, 2.0, None, ALU.add))
            ch.link(nc.vector.reciprocal(s, s))
            ch.link(nc.vector.tensor_tensor(s, s, z, ALU.mult))
            ch.link(nc.vector.tensor_tensor(q, s, s, ALU.mult))
            ch.link(nc.vector.tensor_scalar(p, q, 1.0 / 19, None, ALU.mult))
            for k in range(17, 2, -2):
                ch.link(nc.vector.scalar_tensor_tensor(p, p, 1.0 / k, q, ALU.add, ALU.mult))
            ch.link(nc.vector.scalar_tensor_tensor(p, p, 1.0, s, ALU.add, ALU.mult))
            ch.link(nc.vector.tensor_scalar(neg, neg, 0.0, 0.5, ALU.max, ALU.mult))
            ch.link(nc.vector.tensor_tensor(p, p, neg, ALU.add))
            nc.vector.tensor_scalar(lpar[:, :, LY], p, 8.0, None, ALU.mult)
            nc.vector.tensor_scalar(lpar[:, :, LNY], p, -8.0, None, ALU.mult)
            ch.link(nc.vector.tensor_scalar(lpar[:, :, LBA:LBX + 1], lpar[:, :, LBA:LBX + 1], 0.5, None, ALU.mult))
            dve.sem_inc(l_set, 1)

            def block(n):
                unit, n1, n2, n3, n6 = lru_at(n)
                ch.link(nc.vector.tensor_copy(lp, lpar[:, bass.ds(n, 1), :].rearrange("p a c -> p (a c)")))
                dve.wait_ge(unit_ev, ev_val(unit.at(0), 2))
                dve.wait_ge(l_gt, n6.at(0) + 12)
                cs = lp[:, LC0:LC0 + 24].rearrange("p (b r) -> p b r", r=3)
                oc = lo[:, OCS:OCS + 24].rearrange("p (b r) -> p b r", r=3)
                nc.vector.tensor_copy(lo[:, OC:OC + 3], xpad[:, SEQ:SEQ + 3])
                nc.vector.tensor_copy(oc[:, :, 0:2], cs[:, :, 1:3])
                nc.vector.tensor_copy(oc[:, :, 2], xs8)
                for k in range(4):
                    tap = lp[:, LW + k:LW + k + 1]
                    src_s = cs[:, :, k] if k < 3 else xs8
                    if k == 0:
                        nc.vector.tensor_scalar(xcv[:, SEQ:T], src_s, tap, lp[:, LB:LB + 1], ALU.mult, ALU.add)
                        ins = nc.vector.tensor_scalar(xcv[:, 0:SEQ], xpad[:, 0:SEQ], tap, lp[:, LB:LB + 1], ALU.mult,
                                                      ALU.add)
                    else:
                        nc.vector.scalar_tensor_tensor(xcv[:, SEQ:T], src_s, tap, xcv[:, SEQ:T], ALU.mult, ALU.add)
                        ins = nc.vector.scalar_tensor_tensor(xcv[:, 0:SEQ], xpad[:, k:k + SEQ], tap, xcv[:, 0:SEQ],
                                                             ALU.mult, ALU.add)
                    if k < 3:
                        ch.link(ins)
                ins.then_inc(l_xc, 1)

                def g_mul(c):
                    w = CHUNKS[c][1]
                    dve.wait_ge(l_th, done(n3.at(c)))
                    dve.wait_ge(unit_ev, ev_val(unit.at(1), c) - 1)
                    nc.vector.scalar_tensor_tensor(lgst[:, c % 2, 0:w], lgst[:, c % 2, 0:w], 1.0,
                                                   unit_bank(1, c)[:, 0:w], ALU.add, ALU.mult).then_inc(unit_ev, 1)

                g_mul(0)
                g_mul(1)
                dve.wait_ge(l_at, done(n1.at(0)))
                ch.link(nc.vector.tensor_tensor(gm, ga, ga, ALU.mult))
                nc.vector.scalar_tensor_tensor(gm, gm, 1.0, gtr, ALU.add, ALU.mult).then_inc(l_m, 1)
                ch.link(nc.vector.scalar_tensor_tensor(gti, gti, 1.0, xcv, ALU.add, ALU.mult))
                g_mul(2)
                dve.wait_ge(l_sq, done(n1.at(0)))
                dve.wait_ge(l_hst, n1.at(0) * 16 + 16)
                nc.vector.tensor_tensor(tmp_s, ga[:, SEQ:T], lp[:, LH0:LH0 + NS], ALU.mult)
                ch.link(nc.vector.tensor_tensor(gti, gti, gm, ALU.mult))
                nc.vector.tensor_tensor(hb[:, SEQ:T], tmp_s, gti[:, SEQ:T], ALU.add)
                nc.vector.tensor_tensor_scan(hb[:, 0:SEQ], ga[:, 0:SEQ], gti[:, 0:SEQ], 0.0, ALU.mult, ALU.add)\
                  .then_inc(l_h, 1)
                dve.wait_ge(l_h, done(n1.at(0)))
                nc.vector.tensor_copy(lo[:, OHS:OHS + NS], hb[:, SEQ:T])
                ch.link(nc.vector.tensor_copy(lo[:, OH:OH + 1], hb[:, SEQ - 1:SEQ]))
                ch.link(nc.vector.tensor_copy(lout[:, bass.ds(n, 1), :].rearrange("p a c -> p (a c)"), lo))

            with dve.Fori(0, LRU_B) as n:
                ch.loop(n, 0, LCH_PER)
                block(n)
            ch.done(LRU_B)
            dve.sem_inc(l_oev, 1)
            out_dve(dve, ch, 2, LU + LRU_IN, [(6, 0), (7, KT)], LAST == 2, 0.5)

        def lru_pool(pool):
            with pool.Fori(0, LRU_B) as n:
                unit = Pos(LU, n, 2)
                for j in range(2):
                    split_lo(pool, unit, j + 1)
            out_pool(pool, 2, LU + LRU_IN, [(6, 0), (7, KT)], LAST == 2)

        block = ctx.enter_context(nc.Block())
        LAST = LAYERS - 1
        outp = output_parts(LAYERS)
        ret_fills = {lay: [(FILL_AT[lay] + 1, 0), (FILL_AT[lay] + 2, KT)] for lay in (0, 3)}

        @block.sync
        def _(sp):
            for x, n in CREDITS:
                sp.sem_inc(x, n)
            sp.sem_inc(unit_ps, CR_PS)
            sp.sem_inc(unit_ev, CR)
            input_sp(sp)
            ret_sp(sp, 0)
            if LAYERS > 1:
                diff_sp(sp)
            if LAYERS > 2:
                lru_sp(sp)
            if LAYERS > 3:
                ret_sp(sp, 3)
            outp[3](sp)

        @block.tensor
        def _(pe):
            pe.wait_ge(const_ms, 2)
            input_pe(pe)
            for c in range(NC_):
                norm_pe(pe, 0, c)
            for lay in range(LAYERS):
                if lay in (0, 3):
                    ret_pe(pe, lay)
                    out_pe(pe, lay, UNIT_AT[lay] + 48, ret_fills[lay], LAST == lay)
                else:
                    (diff_pe, lru_pe)[lay - 1](pe)
            outp[0](pe)

        @block.scalar
        def _(act):
            act.wait_ge(const_ms, 2)
            input_act(act)
            split_hi(act, Pos(0), Pos(0), 0)
            for c in range(NC_):
                norm_act(act, 0, c)
            for lay in range(LAYERS):
                if lay in (0, 3):
                    ret_act(act, lay)
                    out_act(act, lay, UNIT_AT[lay] + 48, RAW_AT[lay] + 48, ret_fills[lay], LAST == lay)
                else:
                    (diff_act, lru_act)[lay - 1](act)
            outp[1](act)

        @block.vector
        def _(dve):
            ch = Chain(dve, dve_own)
            input_dve(dve, ch)
            for c in range(NC_):
                norm_dve(dve, ch, 0, c)
            for lay in range(LAYERS):
                if lay in (0, 3):
                    ret_dve(dve, ch, lay)
                    out_dve(dve, ch, lay, UNIT_AT[lay] + 48, ret_fills[lay], LAST == lay, 1.0)
                else:
                    (diff_dve, lru_dve)[lay - 1](dve, ch)
            outp[2](dve)

        @block.gpsimd
        def _(pool):
            split_lo(pool, Pos(0), 0)
            for c in range(NC_):
                fill_parts(None, None, pool, 0, c)
            for lay in range(LAYERS):
                if lay in (0, 3):
                    ret_pool(pool, lay)
                    out_pool(pool, lay, UNIT_AT[lay] + 48, ret_fills[lay], LAST == lay)
                else:
                    (diff_pool, lru_pool)[lay - 1](pool)


_OUTS = (("y_prompt", (1, SEQ, D_MODEL)), ("y_sample", (NS, 1, D_MODEL)),
         ("ret_state_prompt", (2, 1, RH, RDK, RDV)), ("ret_state_sample", (2, NS, RH, RDK, RDV)),
         ("k_rows_prompt", (1, 1, SEQ, DH, DV)), ("v_rows_prompt", (1, 1, SEQ, DH, DV)),
         ("k_rows_sample", (1, NS, 1, DH, DV)), ("v_rows_sample", (1, NS, 1, DH, DV)),
         ("lru_h_prompt", (1, 1, LRU_W)), ("lru_conv_prompt", (1, 1, 3, LRU_W)),
         ("lru_h_sample", (1, NS, LRU_W)), ("lru_conv_sample", (1, NS, 3, LRU_W)))


def kernel(**inputs):
    import numpy as _np
    import concourse.bacc as _bacc
    from concourse import mybir as _mybir
    from concourse.bass_utils import run_bass_kernel_spmd as _run

    nc = _bacc.Bacc("TRN2", target_bir_lowering=False, num_devices=1)
    arrays, A = {}, {}
    for name, value in {**inputs, **constants()}.items():
        a = _np.ascontiguousarray(value)
        arrays[f"in_{name}"] = a
        A[name] = nc.dram_tensor(f"in_{name}", a.shape, _mybir.dt.from_np(a.dtype), kind="ExternalInput").ap()
    for name, shape in _OUTS:
        A[name] = nc.dram_tensor(f"out_{name}", shape, _mybir.dt.float32, kind="ExternalOutput").ap()
    trunk(nc, A)
    r = _run(nc, [arrays], core_ids=[0])
    return tuple(r.results[0][f"out_{name}"] for name, _ in _OUTS)
```

```python
from contextlib import ExitStack
import math

import numpy as np
import concourse.bass as bass
from concourse import mybir

P = 128
D_MODEL = 1024
SEQ = 1024
NS = 8
T = SEQ + NS
KT = D_MODEL // P
CHUNKS = [(0, 384), (384, 384), (768, 264)]
NC_ = len(CHUNKS)
WMAX = 384
NBLK = SEQ // P
EPS = 1e-6
UNIT = KT * P

RH, RDK, RDV = 4, 256, 512
RQK, RV = RH * RDK, RH * RDV
RU_IN = 12
RU_OUT = 16
RET_UNITS = RH * RU_IN + RU_OUT

DH, DV = 8, 128
PAGES = 8
LAM_INIT = 0.8 - 0.6 * math.exp(-0.3 * 1)
DIFF_IN, DIFF_OUT = 32, 8
LRU_W, LRU_B = 1536, 12
LRU_IN, LRU_OUT = 24, 16

F32 = mybir.dt.float32
F32R = mybir.dt.float32r
I32 = mybir.dt.int32
ALU = mybir.AluOpType
ACT = mybir.ActivationFunctionType
AX = mybir.AxisListType

RHC = 128 + 128 + 3


def blocks_of(c):
    c0, w = CHUNKS[c]
    return [(b, min(P, c0 + w - b * P)) for b in range(c0 // P, (c0 + w + P - 1) // P)]


def constants():
    ident = np.eye(P, dtype=np.float32)
    lg = np.log1p(-np.exp2(-5.0 - np.arange(RH)))
    idx = np.arange(P, dtype=np.float64)
    rel = idx[None, :] - idx[:, None]
    ret = np.zeros((RH, P, RHC), np.float32)
    for h in range(RH):
        ret[h, :, 0:P] = np.where(rel >= 0, np.exp(np.maximum(rel, 0) * lg[h]), 0.0)
        ret[h, :, P:2 * P] = np.exp((idx + 1.0) * lg[h])[None, :]
        ret[h, :, 2 * P] = np.exp((P - 1.0 - idx) * lg[h])
        ret[h, :, 2 * P + 1] = np.exp(lg[h])
        ret[h, :, 2 * P + 2] = np.exp(P * lg[h])
    dist = np.arange(SEQ)[None, :] - (SEQ - P) - idx[:, None]
    dist = np.where(dist <= 0, dist, -1e32).astype(np.float32)
    sdist = (idx[:, None] + P * np.arange(PAGES)[None, :] - SEQ).astype(np.float32)
    return {"c_ident": ident, "c_ret": ret, "c_dist": dist, "c_sdist": sdist}


class Chain:

    def __init__(self, eng, sem):
        self.eng, self.sem, self.n, self.off = eng, sem, 0, 0

    def link(self, ins):
        self.n += 1
        ins.then_inc(self.sem, 1)
        self.eng.wait_ge(self.sem, self.n + self.off)

    def loop(self, i, start, per):
        self.at, self.per = self.n, per
        self.off = (i - start) * per

    def done(self, rounds):
        assert self.n - self.at == self.per, (self.n - self.at, self.per)
        self.n = self.at + self.per * rounds
        self.off = 0


class Pos:

    def __init__(self, base, i=0, per=0):
        self.base, self.i, self.per = base, i, per

    def at(self, k):
        return self.base + k if self.per == 0 else self.i * self.per + (self.base + k)

    def half(self, k):
        return (self.base + k) // 2 if self.per == 0 else self.i * (self.per // 2) + (self.base + k) // 2


class Arena:

    def __init__(self, ap, size):
        self.ap, self.size, self.at = ap, size, 0

    def take(self, *shape):
        n = int(np.prod(shape))
        assert self.at + n <= self.size, f"arena: {self.at + n} of {self.size}"
        v = self.ap[:, self.at:self.at + n]
        self.at += n
        names = "abcd"[:len(shape)]
        if len(shape) > 1:
            kw = {names[i]: shape[i] for i in range(1, len(shape))}
            v = v.rearrange(f"p ({' '.join(names)}) -> p {' '.join(names)}", **kw)
        return v



UNIT_AT = [0, RET_UNITS, RET_UNITS + DIFF_IN + DIFF_OUT, RET_UNITS + DIFF_IN + DIFF_OUT + LRU_IN + LRU_OUT]
RAW_AT = UNIT_AT
FILL_AT = [0, 3, 5, 8]
FILL_K = [8, 8, 8, 8, 8, 8, 8, 4, 8, 8, 8]


def fill_tiles(f, c):
    return sum(FILL_K[:f]) * NC_ + c * FILL_K[f]


def trunk(nc, A, LAYERS=4):
    ctx = ExitStack()
    with ctx:
        def sb(name, shape, dt=F32):
            return ctx.enter_context(nc.sbuf_tensor(name, shape, dt))

        def sem(name):
            return ctx.enter_context(nc.semaphore(name))

        def sems(name, n):
            return [sem(f"{name}{i}") for i in range(n)]

        xT = sb("xT", [P, KT, T])
        Hh, Hl = sb("Hh", [P, KT, T], F32R), sb("Hl", [P, KT, T], F32R)
        wraw = sb("wraw", [P, 2, UNIT])
        Wh, Wl = sb("Wh", [P, 2, UNIT], F32R), sb("Wl", [P, 2, UNIT], F32R)
        ident, ones = sb("ident", [P, P]), sb("ones", [P, P])
        ss = sb("ss", [P, T])
        rst = sb("rst", [P, WMAX])
        hraw = sb("hraw", [P, 2, WMAX])
        ng = sb("ng", [P, 4, KT])
        eps_t = sb("eps_t", [P, 1])
        ASZ = 19808
        arena_t = sb("arena", [P, ASZ])
        psum = ctx.enter_context(nc.psum_tensor("psum", [P, 8, 512], F32))
        bank = [psum[:, i, :] for i in range(8)]
        on_d = nc.dram_tensor("scratch_on", (2 * KT, P, T), F32, kind="Internal").ap()
        g_d = nc.dram_tensor("scratch_g", (2 * KT, P, T), F32, kind="Internal").ap()

        def arena():
            return Arena(arena_t[:, :], ASZ)

        w_loaded = sems("w_loaded", 2)
        raw_free = sem("raw_free")
        w_hi, w_lo = sem("w_hi"), sem("w_lo")
        unit_ps = sem("unit_ps")
        unit_ev = sem("unit_ev")
        h_raw, h_hi, h_lo = sem("h_raw"), sem("h_hi"), sem("h_lo")
        sq_done, ss_done = sem("sq_done"), sem("ss_done")
        nrm_ps, nrm_sq = sem("nrm_ps"), sem("nrm_sq")
        const_ld, const_ms, const_tr, const_ev = sem("const_ld"), sem("const_ms"), sem("const_tr"), sem("const_ev")
        dve_own = sem("dve_own")
        stage_ld = sems("stage_ld", 4)

        CR = 2
        CR_PS = 3

        def ev_val(u, c):
            return u * NC_ + (c + 1 + CR)

        def ps_val(u, c):
            return u * NC_ + (c + 1 + CR_PS)

        held = {x: sem(f"held_{x}") for x in ("sp", "pe", "dve")}

        def hold(eng, x):
            eng.sem_inc(held[x], 1)

        def w_block(w, row0, kt, col0):
            return w[row0:row0 + kt * P, :].rearrange("(k p) n -> p k n", p=P)[:, :, bass.ds(col0, P)]

        def load_w(sp, raw, j, src, kt=KT):
            sp.wait_ge(raw_free, raw.at(j) + (1 + CR - 2))
            sp.dma_start(wraw[:, j % 2, 0:kt * P].rearrange("p (k n) -> p k n", k=kt), src)\
              .then_inc(w_loaded[j % 2], 16)

        def split_hi(act, unit, raw, j, kt=KT):
            act.wait_ge(w_loaded[j % 2], raw.half(j) * 16 + 16)
            act.wait_ge(unit_ps, ps_val(unit.at(j), 2) - 2 * NC_)
            act.activation(Wh[:, j % 2, 0:kt * P], wraw[:, j % 2, 0:kt * P], ACT.Copy).then_inc(w_hi, 1)

        def split_lo(pool, unit, j, kt=KT):
            pool.wait_ge(w_hi, unit.at(j) + 1)
            pool.tensor_tensor(Wl[:, j % 2, 0:kt * P], wraw[:, j % 2, 0:kt * P],
                               Wh[:, j % 2, 0:kt * P].bitcast(F32), ALU.subtract).then_inc(w_lo, 1)
            pool.wait_ge(w_lo, unit.at(j) + 1)
            pool.sem_inc(raw_free, 1)

        def unit_bank(j, c):
            return bank[(j + c) % 2]

        def unit_chunk(pe, unit, j, c, f, kt=KT, ks=None, new_h=False):
            c0, w = CHUNKS[c]
            ks = ks or range(kt)
            if not new_h and f in FILL_AT and ks[0] == 0:
                pe.wait_ge(h_lo, fill_tiles(f, c) + FILL_K[f])
            if ks[0] == 0:
                if c == 0:
                    pe.wait_ge(w_lo, unit.at(j) + 1)
                pe.wait_ge(unit_ev, ev_val(unit.at(j), c) - 2)
            out = unit_bank(j, c)[:, 0:w]
            for k in ks:
                if new_h:
                    pe.wait_ge(h_lo, fill_tiles(f, c) + k + 1)
                hi, lo = Wh[:, j % 2, k * P:(k + 1) * P], Wl[:, j % 2, k * P:(k + 1) * P]
                xh, xl = Hh[:, k, c0:c0 + w], Hl[:, k, c0:c0 + w]
                nc.tensor.matmul(out, hi, xh, start=(k == 0), stop=False)
                nc.tensor.matmul(out, hi, xl, start=False, stop=False)
                last = nc.tensor.matmul(out, lo, xh, start=False, stop=(k == kt - 1))
            if ks[-1] == kt - 1:
                last.then_inc(unit_ps, 1)

        def fill_before(f):
            return {0: 0, 1: 48, 2: 56, 3: 64, 4: UNIT_AT[1] + 32, 5: UNIT_AT[2],
                    6: UNIT_AT[2] + 24, 7: UNIT_AT[2] + 32, 8: UNIT_AT[3], 9: UNIT_AT[3] + 48,
                    10: UNIT_AT[3] + 56}[f]

        def fill_parts(act, dve, pool, f, c):
            c0, w = CHUNKS[c]
            for k in range(FILL_K[f]):
                n = fill_tiles(f, c) + k
                if act is not None:
                    if k == 0 and fill_before(f):
                        act.wait_ge(unit_ps, ps_val(fill_before(f) - 1, c))
                    act.wait_ge(h_raw, n + 1)
                    act.activation(Hh[:, k, c0:c0 + w], hraw[:, n % 2, 0:w], ACT.Copy).then_inc(h_hi, 1)
                if pool is not None:
                    pool.wait_ge(h_hi, n + 1)
                    pool.tensor_tensor(Hl[:, k, c0:c0 + w], hraw[:, n % 2, 0:w],
                                       Hh[:, k, c0:c0 + w].bitcast(F32), ALU.subtract).then_inc(h_lo, 1)

        def norm_index(layer, c):
            return layer * NC_ + c

        NB = bank[7]

        def norm_pe(pe, layer, c):
            c0, w = CHUNKS[c]
            n = norm_index(layer, c)
            pe.wait_ge(ss_done, KT * NC_ * layer + (KT - 1) * NC_ + c + 1 if layer else KT * (c + 1))
            if n:
                pe.wait_ge(nrm_sq, n)
            nc.tensor.matmul(NB[:, 0:w], ones[:, :], ss[:, c0:c0 + w], start=True, stop=True).then_inc(nrm_ps, 1)

        def norm_act(act, layer, c):
            c0, w = CHUNKS[c]
            n = norm_index(layer, c)
            f = FILL_AT[layer]
            act.wait_ge(nrm_ps, n + 1)
            if c:
                act.wait_ge(h_raw, fill_tiles(f, c))
            act.activation(rst[:, 0:w], NB[:, 0:w], ACT.Sqrt, bias=eps_t[:, 0:1], scale=1.0 / D_MODEL)\
               .then_inc(nrm_sq, 1)
            fill_parts(act, None, None, f, c)

        def norm_dve(dve, ch, layer, c):
            c0, w = CHUNKS[c]
            f = FILL_AT[layer]
            dve.wait_ge(nrm_sq, norm_index(layer, c) + 1)
            ch.link(nc.vector.reciprocal(rst[:, 0:w], rst[:, 0:w]))
            for k in range(KT):
                n = fill_tiles(f, c) + k
                if n >= 2:
                    dve.wait_ge(h_lo, n - 1)
                nc.vector.scalar_tensor_tensor(hraw[:, n % 2, 0:w], xT[:, k, c0:c0 + w], ng[:, layer, k:k + 1],
                                               rst[:, 0:w], ALU.mult, ALU.mult).then_inc(h_raw, 1)

        def stage_index(f):
            return NC_ * sum(1 for x in range(f) if x not in FILL_AT)

        LRU_STAGE = 9500

        def stage_parts(f):
            return [(0, FILL_K[f] // 2), (FILL_K[f] // 2, FILL_K[f])]

        def stage_load(sp, st, f, k0, c):
            c0, w = CHUNKS[c]
            n = stage_index(f) + c
            for x, (ka, ke) in enumerate(stage_parts(f)):
                if f in (6, 7):
                    for a, e in ((ka, (ka + ke) // 2), ((ka + ke) // 2, ke)):
                        sp.dma_start(st[:, n % 2, a:e, 0:w], on_d[k0 + a:k0 + e, :, c0:c0 + w].rearrange("k p t -> p k t"))\
                          .then_inc(stage_ld[2 * (n % 2) + x], 16)
                    continue
                for i, src in enumerate((on_d, g_d)):
                    sp.dma_start(st[:, n % 2, i, ka:ke, 0:w],
                                 src[k0 + ka:k0 + ke, :, c0:c0 + w].rearrange("k p t -> p k t"))\
                      .then_inc(stage_ld[2 * (n % 2) + x], 16)

        def stage_dve(dve, st, f, c, scale):
            c0, w = CHUNKS[c]
            m = stage_index(f) + c
            for x, (ka, ke) in enumerate(stage_parts(f)):
                dve.wait_ge(stage_ld[2 * (m % 2) + x], 32 * (m // 2 + 1))
                for k in range(ka, ke):
                    n = fill_tiles(f, c) + k
                    dve.wait_ge(h_lo, n - 1)
                    if f in (6, 7):
                        nc.vector.tensor_scalar(hraw[:, n % 2, 0:w], st[:, m % 2, k, 0:w], scale, None, ALU.mult)\
                          .then_inc(h_raw, 1)
                        continue
                    nc.vector.scalar_tensor_tensor(hraw[:, n % 2, 0:w], st[:, m % 2, 0, k, 0:w], scale,
                                                   st[:, m % 2, 1, k, 0:w], ALU.mult, ALU.mult).then_inc(h_raw, 1)

        def residual_dve(dve, unit, j, m, c, final, sqb, sqn):
            c0, w = CHUNKS[c]
            dve.wait_ge(unit_ps, ps_val(unit.at(j), c))
            dve.wait_ge(unit_ev, ev_val(unit.at(j), c) - 1)
            x = xT[:, bass.ds(m, 1), c0:c0 + w].rearrange("p a t -> p (a t)")
            nc.vector.tensor_tensor(x, unit_bank(j, c)[:, 0:w], x, ALU.add).then_inc(unit_ev, 1)
            if final:
                dve.wait_ge(sq_done, sqn + 1)
                nc.vector.tensor_tensor(ss[:, c0:c0 + w], ss[:, c0:c0 + w], sqb[:, (j + c) % 2, 0:w], ALU.add)\
                  .then_inc(ss_done, 1)

        def square_act(act, unit, j, m, c, sqb, sqn):
            c0, w = CHUNKS[c]
            act.wait_ge(unit_ev, ev_val(unit.at(j), c))
            act.wait_ge(ss_done, sqn - 1)
            x = xT[:, bass.ds(m, 1), c0:c0 + w].rearrange("p a t -> p (a t)")
            act.activation(sqb[:, (j + c) % 2, 0:w], x, ACT.Square).then_inc(sq_done, 1)

        al = arena()
        xin = al.take(2, D_MODEL)
        sqb0 = al.take(2, WMAX)
        ngr = al.take(P)
        xin_ld, xin_ps = sems("xin_ld", 2), sem("xin_ps")
        xin_a, xin_d = sem("xin_a"), sem("xin_d")

        def xin_bank(b, half):
            return bank[2 + 2 * (b % 2) + half]

        def input_sp(sp):
            sp.sem_inc(raw_free, CR)
            sp.dma_start(ident[:, :], A["c_ident"]).then_inc(const_ld, 16)
            sp.dma_start(ngr[0:32, :], A["norm_g"].rearrange("l (k p) -> (l k) p", p=P)).then_inc(const_ld, 16)
            for b in range(NBLK + 1):
                if b >= 2:
                    sp.wait_ge(xin_ps, 2 * (b - 1))
                src = A["x_prompt"][0, b * P:(b + 1) * P, :] if b < NBLK else A["x_sample"][:, 0, :]
                sp.dma_start(xin[0:P if b < NBLK else NS, b % 2, :], src).then_inc(xin_ld[b % 2], 16)
                if b == 4:
                    load_w(sp, Pos(0), 0, w_block(A["ret_w_in"][0], 0, KT, RQK))

        def input_blocks(c):
            return [(0, 1, 2), (3, 4, 5), (6, 7, 8)][c]

        def input_pe(pe):
            pe.wait_ge(const_ld, 32)
            nc.tensor.transpose(bank[6][:, 0:32], ngr[0:32, :], ident[0:32, 0:32]).then_inc(const_tr, 1)
            for c in range(NC_):
                for b in input_blocks(c):
                    w = P if b < NBLK else NS
                    pe.wait_ge(xin_ld[b % 2], 16 * (b // 2 + 1))
                    for half, ev in enumerate((xin_a, xin_d)):
                        if b >= 2:
                            pe.wait_ge(ev, b - 1)
                        for k in range(4):
                            last = nc.tensor.transpose(xin_bank(b, half)[:, k * P:k * P + w],
                                                       xin[0:w, b % 2, (4 * half + k) * P:(4 * half + k + 1) * P],
                                                       ident[0:w, 0:w])
                        last.then_inc(xin_ps, 1)
                if c:
                    norm_pe(pe, 0, c - 1)
            norm_pe(pe, 0, NC_ - 1)

        def input_evac(b, half):
            w = P if b < NBLK else NS
            src = xin_bank(b, half)[:, :].rearrange("p (k t) -> p k t", k=4)[:, :, 0:w]
            return xT[:, 4 * half:4 * half + 4, b * P:b * P + w], src

        def input_act(act):
            for c in range(NC_):
                c0, w = CHUNKS[c]
                for b in input_blocks(c):
                    act.wait_ge(xin_ps, 2 * b + 1)
                    act.activation(*input_evac(b, 0), ACT.Copy).then_inc(xin_a, 1)
                act.wait_ge(xin_a, input_blocks(c)[-1] + 1)
                act.wait_ge(xin_d, input_blocks(c)[-1] + 1)
                for k in range(KT):
                    n = KT * c + k
                    if n >= 2:
                        act.wait_ge(ss_done, n - 1)
                    act.activation(sqb0[:, n % 2, 0:w], xT[:, k, c0:c0 + w], ACT.Square).then_inc(sq_done, 1)
                if c:
                    norm_act(act, 0, c - 1)
                if c == 1:
                    split_hi(act, Pos(0), Pos(0), 0)
            norm_act(act, 0, NC_ - 1)

        def input_dve(dve, ch):
            nc.vector.memset(ones[:, :], 1.0).then_inc(const_ms, 1)
            nc.vector.memset(eps_t[:, :], EPS).then_inc(const_ms, 1)
            ch.link(nc.vector.memset(ss[:, :], 0.0))
            dve.wait_ge(const_tr, 1)
            ch.link(nc.vector.tensor_copy(ng[:, :, :].rearrange("p l k -> p (l k)"), bank[6][:, 0:32]))
            for c in range(NC_):
                c0, w = CHUNKS[c]
                for b in input_blocks(c):
                    dve.wait_ge(xin_ps, 2 * b + 2)
                    nc.vector.tensor_copy(*input_evac(b, 1)).then_inc(xin_d, 1)
                for k in range(KT):
                    n = KT * c + k
                    dve.wait_ge(sq_done, n + 1)
                    if n:
                        dve.wait_ge(ss_done, n)
                    nc.vector.tensor_tensor(ss[:, c0:c0 + w], ss[:, c0:c0 + w], sqb0[:, n % 2, 0:w], ALU.add)\
                      .then_inc(ss_done, 1)
                if c:
                    norm_dve(dve, ch, 0, c - 1)
            norm_dve(dve, ch, 0, NC_ - 1)

        def output_parts(layers):
            al = arena()
            yo = al.take(2, D_MODEL)
            y_ps, y_a, y_d = sem("y_ps"), sem("y_a"), sem("y_d")
            y_st = sems("y_st", 2)
            q_end = UNIT_AT[layers - 1] + [RET_UNITS, DIFF_IN + DIFF_OUT, LRU_IN + LRU_OUT, RET_UNITS][layers - 1]

            def pe_(pe):
                for b in range(NBLK + 1):
                    w = P if b < NBLK else NS
                    c = min(b // 3, 2)
                    pe.wait_ge(unit_ev, ev_val(q_end - 1, c))
                    for half, ev in enumerate((y_a, y_d)):
                        if b >= 2:
                            pe.wait_ge(ev, b - 1)
                        for k in range(4):
                            last = nc.tensor.transpose(xin_bank(b, half)[0:w, k * P:(k + 1) * P],
                                                       xT[:, 4 * half + k, b * P:b * P + w], ident[:, :])
                        last.then_inc(y_ps, 1)

            def evac(b, half):
                w = P if b < NBLK else NS
                return yo[0:w, b % 2, half * 512:(half + 1) * 512], xin_bank(b, half)[0:w, :]

            def act_(act):
                for b in range(NBLK + 1):
                    if b >= 2:
                        act.wait_ge(y_st[b % 2], 16 * (b // 2))
                    act.wait_ge(y_ps, 2 * b + 1)
                    act.activation(*evac(b, 0), ACT.Copy).then_inc(y_a, 1)

            def dve_(dve):
                for b in range(NBLK + 1):
                    if b >= 2:
                        dve.wait_ge(y_st[b % 2], 16 * (b // 2))
                    dve.wait_ge(y_ps, 2 * b + 2)
                    nc.vector.tensor_copy(*evac(b, 1)).then_inc(y_d, 1)

            def sp_(sp):
                for b in range(NBLK + 1):
                    sp.wait_ge(y_a, b + 1)
                    sp.wait_ge(y_d, b + 1)
                    dst = A["y_prompt"][0, b * P:(b + 1) * P, :] if b < NBLK else A["y_sample"][:, 0, :]
                    sp.dma_start(dst, yo[0:P if b < NBLK else NS, b % 2, :]).then_inc(y_st[b % 2], 16)
                sp.wait_ge(y_st[0], 16 * 5)
                sp.wait_ge(y_st[1], 16 * 4)
            return pe_, act_, dve_, sp_

        al = arena()
        kT, qT = al.take(2, T), al.take(2, T)
        ktok = al.take(NBLK, RDK)
        vtok = al.take(NBLK, RDV)
        vs = al.take(RDV)
        St = al.take(2, RDV)
        qdT = al.take(2, 2, P)
        sdT = al.take(2, P)
        onb = al.take(RDV)
        onst = al.take(2, 4, P)
        kvc = hraw
        gst = al.take(2, WMAX)
        sring = al.take(4, 2, RDV)
        hc = al.take(RHC)
        so, sq_s, rs_s, nt = al.take(4, NS), al.take(4, NS), al.take(NS), al.take(2, NS)
        osq, o_r, nt1 = al.take(1), al.take(1), al.take(2)
        sqj = hraw[:, :, :].rearrange("p a t -> p (a t)")[:, 0:RDV]
        decT, qdec, kdec, gam, gamC = hc[:, 0:P], hc[:, P:2 * P], hc[:, 256:257], hc[:, 257:258], hc[:, 258:259]
        TR, SC, OB, SB0, SB1, VB = bank[2], bank[3], bank[4], bank[5], bank[6], bank[7]
        r_hc = sem("r_hc")
        r_tr, r_te = sem("r_tr"), sem("r_te")
        r_sc, r_sd, r_qd = sem("r_sc"), sem("r_sd"), sem("r_qd")
        r_o, r_st, r_su = sem("r_o"), sem("r_st"), sem("r_su")
        r_sq, r_rs, r_on = sem("r_sq"), sem("r_rs"), sem("r_on")
        r_vb, r_sg, r_sn, r_so = sem("r_vb"), sem("r_sg"), sem("r_sn"), sem("r_so")
        r_sld, r_sst = sems("r_sld", 4), sems("r_sst", 4)
        r_on_st, r_g_st = sems("r_on_st", 2), sems("r_g_st", 2)
        r_fs, r_fin, r_fo = sem("r_fs"), sem("r_fin"), sem("r_fo")
        r_S_st, r_os_st = sem("r_S_st"), sem("r_os_st")

        def rsqrt(dve, ch, x, scale, y, t, last_sem=None):
            a = t[:, 0:1] if len(t.shape) == 2 else t[:, 0, :]
            b = t[:, 1:2] if len(t.shape) == 2 else t[:, 1, :]
            ch.link(nc.vector.tensor_scalar(a, x, scale, EPS, ALU.mult, ALU.add))
            ch.link(nc.vector.tensor_scalar(b.bitcast(I32), a.bitcast(I32), 1, None, ALU.logical_shift_right))
            ch.link(nc.vector.tensor_scalar(y.bitcast(I32), b.bitcast(I32), -1.0, float(0x5F3759DF),
                                            ALU.mult, ALU.add))
            for n in range(3):
                ch.link(nc.vector.tensor_tensor(b, y, y, ALU.mult))
                ch.link(nc.vector.scalar_tensor_tensor(b, b, -0.5, a, ALU.mult, ALU.mult))
                step = nc.vector.scalar_tensor_tensor(y, b, 1.5, y, ALU.add, ALU.mult)
                if n < 2 or last_sem is None:
                    ch.link(step)
                else:
                    step.then_inc(last_sem, 1)

        RTR = 26
        RCH = 8 * 11 + 1 + 12
        CREDITS = [(x, 1) for x in (r_tr, r_te, r_sc, r_sd, r_qd, r_o, r_st, r_su, r_sq, r_rs, r_on, r_vb,
                                    r_sg, r_sn, r_so, r_fin, r_fs, r_fo)] + \
                  [(x, 16) for x in (*r_sst, *r_on_st, *r_g_st, r_S_st, r_os_st)]

        def prior(n):
            return n + 1

        def done(n):
            return n + 2

        def ret_sp(sp, lay):
            j_, U, R = lay // 3, UNIT_AT[lay], RAW_AT[lay]
            win, wout = A["ret_w_in"][j_], A["ret_w_out"][j_]

            def weights(h, js):
                for j in js:
                    col = (h * RDK + (RQK + j * P) if j < 2 else h * RDV + (2 * RQK + (j - 2) * P) if j < 6 else
                           h * RDK + (j - 6) * P if j < 8 else h * RDV + (2 * RQK + RV + (j - 8) * P))
                    load_w(sp, Pos(R, h, RU_IN), j, w_block(win, 0, KT, col))

            def head(h):
                sp.wait_ge(r_fo, h + (RH * j_ + 1))
                sp.dma_start(hc, A["c_ret"][bass.ds(h, 1), :, :].rearrange("a p n -> (a p) n")).then_inc(r_hc, 16)
                weights(h, range(2, RU_IN))

            weights(0, (0, 1) if lay else (1,))
            if lay:
                sp.wait_ge(h_raw, fill_tiles(FILL_AT[lay] - 1, 2) + FILL_K[FILL_AT[lay] - 1])
                sp.wait_ge(ss_done, KT * NC_ * (lay + 1))
            with sp.Fori(0, RH - 1) as h:
                head(h)
                weights(h + 1, (0, 1))
            head(RH - 1)
            out_sp(sp, lay, wout, U + 48, R + 48, [(FILL_AT[lay] + 1, 0), (FILL_AT[lay] + 2, KT)], ret_stage_wait,
                   late_wait=ret_end_wait)

        def ret_stage_wait(sp, lay):
            n = RH * (lay // 3 + 1)
            for x in (r_so, r_o, r_st, r_su, r_vb):
                sp.wait_ge(x, done(8 * n - 1))
            sp.wait_ge(r_S_st, 16 * n + 16)
            for i in range(2):
                sp.wait_ge(r_on_st[i], 16 * 4 * (n - 1) + 16)
                sp.wait_ge(r_g_st[i], 16 * 6 * (n - 1) + 16)
            sp.wait_ge(r_os_st, 16 * (n - 1) + 16)

        def ret_end_wait(sp, lay):
            n = RH * (lay // 3 + 1)
            sp.wait_ge(r_fo, n + 1)
            for i in range(2):
                sp.wait_ge(r_on_st[i], 16 * 4 * n + 16)
                sp.wait_ge(r_g_st[i], 16 * 6 * n + 16)
            sp.wait_ge(r_os_st, 16 * n + 16)
            sp.wait_ge(r_S_st, 16 * n + 16)
            for i in range(4):
                sp.wait_ge(r_sst[i], 16 * 2 * n + 16)
            sp.wait_ge(r_te, RTR * n + 1)

        def out_sp(sp, lay, wout, U, R, fills, stage_wait, loaded=0, after=None, late_wait=None):
            st = stage_of(lay)
            for x, (f, k0) in enumerate(fills):
                kt = FILL_K[f]
                raw = Pos(R + 8 * x)
                if x == 0:
                    for j in range(loaded, 2):
                        load_w(sp, raw, j, w_block(wout, k0 * P, kt, j * P), kt)
                    stage_wait(sp, lay)
                    for c in range(2) if lay != 2 else ():
                        stage_load(sp, st, f, k0, c)
                    if after is not None:
                        after(sp)
                for j in range(2 if x == 0 else 0, KT):
                    if j == 2:
                        sp.wait_ge(h_raw, fill_tiles(f, 0) + FILL_K[f])
                        stage_load(sp, st, f, k0, 2)
                        if x + 1 < len(fills):
                            sp.wait_ge(h_raw, fill_tiles(f, 1) + FILL_K[f])
                            if late_wait is not None:
                                late_wait(sp, lay)
                            stage_load(sp, st, *fills[x + 1], 0)
                            sp.wait_ge(h_raw, fill_tiles(f, 2) + FILL_K[f])
                            stage_load(sp, st, *fills[x + 1], 1)
                    load_w(sp, raw, j, w_block(wout, k0 * P, kt, j * P), kt)

        def stage_of(lay):
            al = arena()
            if lay == 2:
                al.at = LRU_STAGE
                return al.take(2, KT, WMAX)
            return al.take(2, 2, KT, WMAX)

        def out_square_buf(lay):
            al = arena()
            if lay != 2:
                al.take(2, 2, KT, WMAX)
            return al.take(2, WMAX)

        def out_pe(pe, lay, U, fills, last_layer):
            for x, (f, k0) in enumerate(fills):
                unit = Pos(U + 8 * x)
                final = x + 1 == len(fills) and not last_layer
                for j in range(KT):
                    for c in range(NC_):
                        unit_chunk(pe, unit, j, c, f, FILL_K[f], new_h=(j == 0))
                        if final and j == KT - 1 and c:
                            norm_pe(pe, lay + 1, c - 1)
                if final:
                    norm_pe(pe, lay + 1, 2)

        def out_act(act, lay, U, R, fills, last_layer, next_split=True):
            sqb = out_square_buf(lay)
            sqn = KT * NC_ * (lay + 1)
            for x, (f, k0) in enumerate(fills):
                unit, raw = Pos(U + 8 * x), Pos(R + 8 * x)
                final = x + 1 == len(fills) and not last_layer
                if x == 0:
                    for c in range(NC_):
                        fill_parts(act, None, None, f, c)
                for j in range(KT):
                    if j < KT - 1:
                        split_hi(act, unit, raw, j + 1, FILL_K[f])
                    elif x + 1 < len(fills):
                        split_hi(act, unit, raw, j + 1, FILL_K[fills[x + 1][0]])
                    elif not last_layer and next_split:
                        split_hi(act, unit, raw, j + 1)
                    for c in range(NC_):
                        if final:
                            square_act(act, unit, j, j, c, sqb, sqn)
                            sqn += 1
                        if j == KT - 1 and x + 1 < len(fills):
                            fill_parts(act, None, None, fills[x + 1][0], c)
                        elif final and j == KT - 1 and c:
                            norm_act(act, lay + 1, c - 1)
                if final:
                    norm_act(act, lay + 1, 2)

        def out_dve(dve, ch, lay, U, fills, last_layer, scale):
            st, sqb = stage_of(lay), out_square_buf(lay)
            sqn = KT * NC_ * (lay + 1)
            dve.wait_ge(nrm_ps, NC_ * (lay + 1))
            ch.link(nc.vector.memset(ss[:, :], 0.0))
            for x, (f, k0) in enumerate(fills):
                unit = Pos(U + 8 * x)
                final = x + 1 == len(fills) and not last_layer
                if x == 0:
                    for c in range(NC_):
                        stage_dve(dve, st, f, c, scale)
                for j in range(KT):
                    for c in range(NC_):
                        residual_dve(dve, unit, j, j, c, final, sqb, sqn)
                        sqn += final
                        if j == KT - 1 and x + 1 < len(fills):
                            stage_dve(dve, st, fills[x + 1][0], c, scale)
                        elif final and j == KT - 1 and c:
                            norm_dve(dve, ch, lay + 1, c - 1)
                if final:
                    norm_dve(dve, ch, lay + 1, 2)

        def out_pool(pool, lay, U, fills, last_layer, next_split=True):
            for x, (f, k0) in enumerate(fills):
                unit = Pos(U + 8 * x)
                if x == 0:
                    for c in range(NC_):
                        fill_parts(None, None, pool, f, c)
                for j in range(KT):
                    if j < KT - 1:
                        split_lo(pool, unit, j + 1, FILL_K[f])
                    elif x + 1 < len(fills):
                        split_lo(pool, unit, j + 1, FILL_K[fills[x + 1][0]])
                    elif not last_layer and next_split:
                        split_lo(pool, unit, j + 1)
                    if j == KT - 1:
                        for c in range(NC_):
                            if x + 1 < len(fills):
                                fill_parts(None, None, pool, fills[x + 1][0], c)
                            elif not last_layer:
                                fill_parts(None, None, pool, FILL_AT[lay + 1], c)

        def ret_places(lay, h):
            g = RH * (lay // 3)
            return (Pos(UNIT_AT[lay], h, RU_IN), Pos(RAW_AT[lay], h, RU_IN), Pos(g, h, 1), Pos(8 * g, h, 8),
                    Pos(RTR * g, h, RTR))

        def ret_pe(pe, lay):
            f = FILL_AT[lay]
            with pe.Fori(0, RH) as h:
                unit, raw, n1, n8, ntr = ret_places(lay, h)
                for s in range(36):
                    j, c = divmod(s, NC_)
                    unit_chunk(pe, unit, j, c, f)
                    if 1 <= s <= 18:
                        js, cs = divmod(s - 1, NC_)
                        c0 = CHUNKS[cs][0]
                        pe.wait_ge(unit_ev, ev_val(unit.at(js), cs))
                        pe.wait_ge(r_te, prior(ntr.at(s - 1)))
                        for b, w in blocks_of(cs):
                            if js < 2 and b == NBLK:
                                continue
                            src = kT[:, js, b * P:b * P + w] if js < 2 else kvc[:, (s - 1) % 2, b * P - c0:b * P - c0 + w]
                            last = nc.tensor.transpose(TR[0:w, b * P - c0:b * P - c0 + P], src, ident[:, :])
                        last.then_inc(r_tr, 1)
                    t = s - 24
                    if 0 <= t - 2 < NBLK:
                        r = t - 2
                        pe.wait_ge(r_on, done(n8.at(r)))
                        pe.wait_ge(r_te, prior(ntr.at(18 + r)))
                        for x in range(4):
                            last = nc.tensor.transpose(TR[:, x * P:(x + 1) * P], onb[:, x * P:(x + 1) * P], ident[:, :])
                        last.then_inc(r_tr, 1)
                    if 0 <= t - 1 < NBLK:
                        r = t - 1
                        if r == 0:
                            pe.wait_ge(r_te, done(ntr.at(17)))
                        pe.wait_ge(r_sd, done(n8.at(r)))
                        pe.wait_ge(r_on, prior(n8.at(r)))
                        pe.wait_ge(r_su, prior(n8.at(r)))
                        last = nc.tensor.matmul(OB[:, :], sdT[:, r % 2, :], vtok[:, r, :], start=True, stop=(r == 0))
                        if r:
                            pe.wait_ge(r_qd, done(n8.at(r)))
                            for x in range(2):
                                last = nc.tensor.matmul(OB[:, :], qdT[:, r % 2, x, :], St[:, x, :], start=False,
                                                        stop=(x == 1))
                        last.then_inc(r_o, 1)
                        for x, sbk in enumerate((SB0, SB1)):
                            last = nc.tensor.matmul(sbk[:, :], ktok[:, r, x * P:(x + 1) * P], vtok[:, r, :],
                                                    start=True, stop=True)
                        last.then_inc(r_st, 1)
                    if 0 <= t - 2 < NS:
                        b = t - 2
                        pe.wait_ge(r_sd, prior(n8.at(min(t, NBLK))))
                        pe.wait_ge(r_sn, done(n8.at(b)))
                        for d in range(4):
                            for x in range(2):
                                last = nc.tensor.matmul(SC[:, P + d * NS + b:P + d * NS + b + 1],
                                                        sring[:, b % 4, x, d * P:(d + 1) * P],
                                                        qT[:, x, SEQ + b:SEQ + b + 1], start=(x == 0), stop=(x == 1))
                        last.then_inc(r_so, 1)
                    if 0 <= t < NBLK:
                        if t == 0:
                            pe.wait_ge(unit_ev, ev_val(unit.at(7), 2))
                        pe.wait_ge(r_sd, prior(n8.at(t)))
                        for x in range(2):
                            last = nc.tensor.matmul(SC[:, 0:P], kT[:, x, t * P:(t + 1) * P], qT[:, x, t * P:(t + 1) * P],
                                                    start=(x == 0), stop=(x == 1))
                        last.then_inc(r_sc, 1)
                    if 0 <= t - 1 < NS:
                        b = t - 1
                        pe.wait_ge(r_sn, prior(n8.at(b)))
                        nc.tensor.matmul(VB[:, :], ident[0:NS, b:b + 1].to_broadcast([NS, P]), vs[0:NS, :],
                                         start=True, stop=True).then_inc(r_vb, 1)
                    if t == 10:
                        pe.wait_ge(r_fs, done(n1.at(0)))
                        for d in range(4):
                            last = nc.tensor.matmul(SC[:, 160:160 + NS], ones[:, :], sq_s[:, d, :], start=(d == 0),
                                                    stop=(d == 3))
                        last.then_inc(r_fin, 1)

        def ret_act(act, lay):
            j_ = lay // 3
            with act.Fori(0, RH) as h:
                unit, raw, n1, n8, ntr = ret_places(lay, h)
                n2, n4, n6 = (Pos(x * RH * j_, h, x) for x in (2, 4, 6))
                for s in range(36):
                    j, c = divmod(s, NC_)
                    c0, w = CHUNKS[c]
                    if c == 0:
                        split_hi(act, unit, raw, j + 1)
                    src = unit_bank(j, c)[:, 0:w]
                    act.wait_ge(unit_ps, ps_val(unit.at(j), c))
                    if j < 2:
                        if s == 0:
                            act.wait_ge(r_fo, prior(n1.at(0)))
                        act.activation(kT[:, j, c0:c0 + w], src, ACT.Copy, scale=RDK ** -0.5).then_inc(unit_ev, 1)
                    elif j < 6:
                        act.wait_ge(r_tr, done(ntr.at(s - 2)))
                        act.activation(kvc[:, s % 2, 0:w], src, ACT.Copy).then_inc(unit_ev, 1)
                    elif j < 8:
                        act.activation(qT[:, j - 6, c0:c0 + w], src, ACT.Copy).then_inc(unit_ev, 1)
                    else:
                        t = s - 24
                        act.wait_ge(r_g_st[t % 2], n6.at(t // 2) * 16 + 16)
                        act.activation(gst[:, t % 2, 0:w], src, ACT.Silu).then_inc(unit_ev, 1)
                        act.wait_ge(unit_ev, ev_val(unit.at(j), c))
                        act.dma_start(g_d[bass.ds(h * 4 + (j - 8), 1), :, c0:c0 + w].rearrange("a p t -> (a p) t"),
                                      gst[:, t % 2, 0:w]).then_inc(r_g_st[t % 2], 16)
                    t = s - 24
                    for b in (range(4) if s == 12 else [t] if 4 <= t < NS else []):
                        act.wait_ge(r_sst[b % 4], n2.at(b // 4) * 16 + 16)
                        act.wait_ge(r_so, prior(n8.at(0)) if b < 4 else done(n8.at(b - 4)))
                        act.dma_start(sring[:, b % 4, :, :],
                                      A["state_ret"][j_, b, bass.ds(h, 1), :, :]
                                      .rearrange("a (x p) v -> p (a x) v", p=P)).then_inc(r_sld[b % 4], 16)
                    if 0 <= t - 2 < NBLK:
                        r = t - 2
                        act.wait_ge(r_tr, done(ntr.at(18 + r)))
                        act.wait_ge(r_on_st[r % 2], n4.at(r // 2) * 16 + 16)
                        act.activation(onst[:, r % 2, :, :].rearrange("p d t -> p (d t)"), TR[:, :], ACT.Copy)\
                           .then_inc(r_te, 1)
                        act.wait_ge(r_te, done(ntr.at(18 + r)))
                        act.dma_start(on_d[bass.ds(h * 4, 4), :, r * P:(r + 1) * P].rearrange("d p t -> p d t"),
                                      onst[:, r % 2, :, :]).then_inc(r_on_st[r % 2], 16)
                    if 0 <= t - 1 < NBLK:
                        r = t - 1
                        act.wait_ge(r_o, done(n8.at(r)))
                        act.wait_ge(r_rs, prior(n8.at(r)))
                        act.activation(sqj[:, :], OB[:, :], ACT.Square, accum_out=osq[:, 0:1]).then_inc(r_sq, 1)
                    if 0 <= t - 1 < NS:
                        b = t - 1
                        act.wait_ge(r_hc, n1.at(0) * 16 + 16)
                        act.wait_ge(r_sld[b % 4], n2.at(b // 4) * 16 + 16)
                        sx = sring[:, b % 4, :, :].rearrange("p x v -> p (x v)")
                        act.activation(sx, sx, ACT.Copy, scale=gam).then_inc(r_sg, 1)
                    if 0 <= t - 1 < NBLK:
                        r = t - 1
                        act.wait_ge(r_rs, done(n8.at(r)))
                        act.wait_ge(r_tr, done(ntr.at(17 + r)))
                        act.activation(onb[:, :], OB[:, :], ACT.Copy, scale=o_r[:, 0:1]).then_inc(r_on, 1)
                    if 0 <= t - 2 < NS:
                        b = t - 2
                        act.wait_ge(r_sn, done(n8.at(b)))
                        act.dma_start(A["ret_state_sample"][j_, b, bass.ds(h, 1), :, :]
                                      .rearrange("a (x p) v -> p (a x) v", p=P), sring[:, b % 4, :, :])\
                           .then_inc(r_sst[b % 4], 16)
                    if t == 9:
                        act.wait_ge(r_su, done(n8.at(7)))
                        act.dma_start(A["ret_state_prompt"][j_, 0, bass.ds(h, 1), :, :]
                                      .rearrange("a (x p) v -> p (a x) v", p=P), St[:, :, :]).then_inc(r_S_st, 16)
                act.wait_ge(r_fo, done(n1.at(0)))
                act.dma_start(on_d[bass.ds(h * 4, 4), :, SEQ:T].rearrange("d p t -> p d t"), so[:, :, :])\
                   .then_inc(r_os_st, 16)

        def ret_dve(dve, ch, lay):
            with dve.Fori(0, RH) as h:
                unit, raw, n1, n8, ntr = ret_places(lay, h)
                ch.loop(h, 0, RCH)
                for s in range(36):
                    if 1 <= s <= 18:
                        js, cs = divmod(s - 1, NC_)
                        blks = [b for b, w in blocks_of(cs) if b < NBLK]
                        b0, nb = blks[0], len(blks)
                        if s == 1:
                            dve.wait_ge(r_hc, n1.at(0) * 16 + 16)
                        dve.wait_ge(r_tr, done(ntr.at(s - 1)))
                        src = TR[:, 0:nb * P].rearrange("p (b n) -> p b n", b=nb)
                        if js < 2:
                            nc.vector.tensor_scalar(ktok[:, b0:b0 + nb, js * P:(js + 1) * P], src, kdec, None,
                                                    ALU.mult).then_inc(r_te, 1)
                        else:
                            if cs == NC_ - 1:
                                nc.vector.tensor_copy(vs[0:NS, (js - 2) * P:(js - 1) * P], TR[0:NS, 256:384])
                            nc.vector.tensor_copy(vtok[:, b0:b0 + nb, (js - 2) * P:(js - 1) * P], src)\
                              .then_inc(r_te, 1)
                    t = s - 24
                    if 0 <= t - 1 < NBLK:
                        r = t - 1
                        dve.wait_ge(r_st, done(n8.at(r)))
                        if r == 0:
                            dve.wait_ge(r_S_st, n1.at(0) * 16 + 16)
                            nc.vector.tensor_copy(St[:, 0, :], SB0[:, :])
                            nc.vector.tensor_copy(St[:, 1, :], SB1[:, :]).then_inc(r_su, 1)
                        else:
                            dve.wait_ge(r_su, prior(n8.at(r)))
                            nc.vector.scalar_tensor_tensor(St[:, 0, :], St[:, 0, :], gamC, SB0[:, :], ALU.mult, ALU.add)
                            nc.vector.scalar_tensor_tensor(St[:, 1, :], St[:, 1, :], gamC, SB1[:, :], ALU.mult,
                                                           ALU.add).then_inc(r_su, 1)
                        dve.wait_ge(r_sq, done(n8.at(r)))
                        dve.wait_ge(r_on, prior(n8.at(r)))
                        rsqrt(dve, ch, osq[:, 0:1], 1.0 / RDV, o_r[:, 0:1], nt1, r_rs)
                    if 0 <= t < NBLK:
                        dve.wait_ge(r_sc, done(n8.at(t)))
                        nc.vector.tensor_tensor(sdT[:, t % 2, :], SC[:, 0:P], decT, ALU.mult).then_inc(r_sd, 1)
                        if t == 0:
                            dve.wait_ge(unit_ev, ev_val(unit.at(7), 2))
                        nc.vector.tensor_tensor(qdT[:, t % 2, :, :], qT[:, :, t * P:(t + 1) * P],
                                                qdec.rearrange("p (x n) -> p x n", x=1).to_broadcast([P, 2, P]),
                                                ALU.mult).then_inc(r_qd, 1)
                    if 0 <= t - 1 < NS:
                        b = t - 1
                        dve.wait_ge(r_vb, done(n8.at(b)))
                        dve.wait_ge(r_sg, done(n8.at(b)))
                        for x in range(2):
                            last = nc.vector.scalar_tensor_tensor(sring[:, b % 4, x, :], VB[:, :],
                                                                  kT[:, x, SEQ + b:SEQ + b + 1], sring[:, b % 4, x, :],
                                                                  ALU.mult, ALU.add)
                        last.then_inc(r_sn, 1)
                    if t == 10:
                        dve.wait_ge(r_so, done(n8.at(7)))
                        dve.wait_ge(r_os_st, n1.at(0) * 16 + 16)
                        ch.link(nc.vector.tensor_copy(so[:, :, :].rearrange("p d b -> p (d b)"), SC[:, P:P + 4 * NS]))
                        nc.vector.tensor_tensor(sq_s[:, :, :], so[:, :, :], so[:, :, :], ALU.mult).then_inc(r_fs, 1)
                    if t == 11:
                        dve.wait_ge(r_fin, done(n1.at(0)))
                        rsqrt(dve, ch, SC[:, 160:160 + NS], 1.0 / RDV, rs_s[:, :], nt)
                        nc.vector.tensor_tensor(so[:, :, :], so[:, :, :],
                                                rs_s[:, :].rearrange("p (x n) -> p x n", x=1).to_broadcast([P, 4, NS]),
                                                ALU.mult).then_inc(r_fo, 1)
            ch.done(RH)

        def ret_pool(pool, lay):
            with pool.Fori(0, RH) as h:
                unit = Pos(UNIT_AT[lay], h, RU_IN)
                for j in range(RU_IN):
                    split_lo(pool, unit, j + 1)

        PG = PAGES * P
        TX = SEQ + P
        al = arena()
        qf, kf = al.take(SEQ), al.take(SEQ)
        qtk, ktk = al.take(TX), al.take(TX)
        vf = al.take(NBLK, DV)
        strip = al.take(SEQ)
        sc2 = al.take(2, 2, SEQ)
        pT = al.take(2, NBLK, P)
        kring, vring = al.take(2, PG), al.take(2, PG)
        prod = al.take(TX)
        dgst = al.take(2, WMAX)
        donst = al.take(2, P)
        donb, junk = al.take(P), al.take(P)
        vs8 = al.take(P)
        gqb, gkb = al.take(64), al.take(64)
        sgf = al.take(1)
        lamv = sc2[:, 0, 0, 0:256].rearrange("p (a d) -> p a d", a=4)
        lam2, negl = al.take(2), al.take(1)
        ptab = al.take(NS * PAGES)
        ppk = al.take(3 * NS)
        assert A["cache_k"].shape[1] <= 128 and PAGES <= 9
        rsk, rsn, ktmp = al.take(18), al.take(18), al.take(2, 18)
        stok, sbt = al.take(2, PAGES, NS), al.take(PAGES)
        pTs = al.take(9 * NS)
        sself, smx, snm, sl, sef = (al.take(2) for _ in range(5))
        wself, diagw = al.take(1), al.take(NS)
        vsf, osm, osq2, fsum, ors, ont = (*(al.take(NS) for _ in range(5)), al.take(2, NS))
        mx2, nm2, l2 = al.take(2, 2), al.take(2, 2), al.take(2, 2)
        rl0, ratio = al.take(2), al.take(1)
        dsq, dx, drs, rnt = al.take(1), al.take(1), al.take(1), al.take(2)
        es = sc2[:, 0, :, :]
        nsq = [ss[:, 0:SEQ], rst[:, 0:P]]
        DTR, DOB = bank[4], bank[5]
        SCB = psum[:, 2:4, :].rearrange("p a n -> p (a n)")
        QB = psum[:, 6:8, :].rearrange("p a n -> p (a n)")
        SSC = [SCB, QB]
        d_ld, d_tab, d_pk, d_set = sem("d_ld"), sem("d_tab"), sem("d_pk"), sem("d_set")
        d_tr, d_te = sem("d_tr"), sem("d_te")
        d_kn = sem("d_kn")
        d_qs = sem("d_qs")
        d_t3, d_ns, d_nr, d_nn, d_ng = (sem(x) for x in ("d_t3", "d_ns", "d_nr", "d_nn", "d_ng"))
        d_qb = sem("d_qb")
        d_kld, d_vld = sems("d_kld", 2), sems("d_vld", 2)
        d_ku, d_vu = sem("d_ku"), sem("d_vu")
        d_sb, d_st, d_snm, d_sex, d_spc = sem("d_sb"), sem("d_st"), sem("d_snm"), sem("d_sex"), sem("d_spc")
        d_ssq, d_sfo = sem("d_ssq"), sem("d_sfo")
        d_sc, d_mx, d_nm, d_ex, d_pc = sem("d_sc"), sem("d_mx"), sem("d_nm"), sem("d_ex"), sem("d_pc")
        d_o, d_sq, d_rs, d_on = sem("d_o"), sem("d_sq"), sem("d_rs"), sem("d_on")
        d_th = sem("d_th")
        d_gst, d_ost = sems("d_gst", 2), sems("d_ost", 2)
        d_kst, d_vst, d_sst, d_rows = sem("d_kst"), sem("d_vst"), sem("d_sst"), sem("d_rows")
        CREDITS += [(x, 1) for x in (d_qs, d_t3, d_ns, d_nr, d_nn, d_ng, d_tr, d_te, d_kn, d_qb, d_sb, d_st, d_snm, d_sex, d_spc, d_ssq, d_sfo,
                                     d_sc, d_mx, d_nm, d_ex, d_pc, d_o, d_sq, d_rs, d_on, d_th)]
        CREDITS += [(x, 2) for x in (d_ku, d_vu)]
        CREDITS += [(x, 16) for x in (*d_gst, *d_ost, d_kst, d_vst, d_sst, d_rows)]
        Q0, K0, G0, V0 = 0, 3, 6, 9
        COLS = (0, 1, 3, 2)
        SLABS = {5: [0], 6: [1, 2], 7: [3, 4], 8: [5], 9: [6, 7]}
        T1_AT = {1: [0], 2: [1], 3: [2], 4: [3], 5: [4], 6: [5], 10: [9], 11: [10, 11]}
        EARLY = 5
        NORM_AT, QB_AT = (4, 7), 5
        V_AT = {0: [0], 1: [1], 2: [2], 3: [3], 4: [4], 5: [5], 6: [6], 7: [7]}
        T2_AT = {8: "T2q", 9: "T2k"}

        def diff_uses(proj, attn):
            out = []
            for s in range(12):
                if attn:
                    out += [("V", x) for x in V_AT.get(s, [])]
                if attn and 1 <= s <= 8:
                    out += [("B", s - 1, x) for x in range((s - 1) // 4 + 1)]
                if proj:
                    out += [("T1", x) for x in T1_AT.get(s, [])]
                    out += [(T2_AT[s], x) for x in range(2) if s in T2_AT]
                if attn and 2 <= s <= 9:
                    out.append(("D", s - 2))
                if attn and s == 9:
                    out.append(("F",))
            return out + [("P",)] * proj

        DN0, DN = len(diff_uses(True, False)), len(diff_uses(True, True))

        class Round:

            def __init__(self, i, proj, attn, dyn):
                uses = diff_uses(proj, attn)
                self.i, self.proj, self.attn = i, proj, attn

                def pos(base, per):
                    return Pos(base, i, per) if dyn else Pos(base + per * i)
                self.unit = pos(UNIT_AT[1], 4)
                self.n1, self.n2, self.n3, self.n4, self.n8 = (pos(0, x) for x in (1, 2, 3, 4, 8))
                self.p1, self.p4, self.p8, self.p16 = (pos(-x, x) for x in (1, 4, 8, 16))
                self.base = Pos(DN0 - DN, i, DN) if dyn else Pos(0 if i == 0 else DN0 + (i - 1) * DN)
                self.tr = lambda *use: self.base.at(uses.index(use))

        def diff_rounds(eng, body, ch=None):
            body(Round(0, True, False, False))
            with eng.Fori(1, DH) as i:
                if ch is not None:
                    ch.loop(i, 1, DCH_PER)
                body(Round(i, True, True, True))
            if ch is not None:
                ch.done(DH - 1)
            body(Round(DH, False, True, False))

        def diff_sp(sp):
            win, wout = A["diff_w_in"][0], A["diff_w_out"][0]

            def weights(h, j):
                load_w(sp, Pos(RAW_AT[1], h, 4), j, w_block(win, 0, KT, h * P + COLS[j] * D_MODEL))

            def slab(cache, ring, ld, used, n8, h, b):
                sp.wait_ge(used, n8.at(b) + 1)
                hold(sp, "sp")
                for p in range(PAGES):
                    if p % 3 == 0:
                        ids = sp.value_load(ppk[0:1, b * 3 + p // 3:b * 3 + p // 3 + 1].bitcast(I32))
                    reg = nc.s_assert_within((ids >> (7 * (p % 3))) & 127, 0, cache.shape[1] - 1,
                                             skip_runtime_bounds_check_because="page ids are rows of the cache")
                    sp.dma_start(ring[:, b % 2, p * P:(p + 1) * P],
                                 cache[0, bass.ds(reg, 1), :, bass.ds(h, 1), :].rearrange("a t c d -> (a t) (c d)"))\
                      .then_inc(ld[b % 2], 16)

            def body(r, last_proj=False):
                i = r.i
                for what, x in (("V", 0), ("V", 1), ("K", 0), ("K", 1), ("W", 2), ("V", 2), ("W", 3), ("V", 3), ("V", 4), ("V", 5), ("V", 6), ("N", 0), ("V", 7), ("K", 2), ("K", 3), ("K", 4), ("K", 5), ("K", 6), ("N", 1), ("K", 7)):
                    if what == "V" and r.attn:
                        slab(A["cache_v"], vring, d_vld, d_vu, r.p8, i - 1, x)
                    if what == "K" and r.proj:
                        slab(A["cache_k"], kring, d_kld, d_ku, r.n8, i, x)
                    if what == "W" and r.proj:
                        weights(i, x)
                    if what == "N" and r.proj and not last_proj:
                        weights(i + 1, x)
                    if what == "N" and last_proj:
                        load_w(sp, Pos(RAW_AT[1] + 32), x, w_block(wout, 0, KT, x * P))

            weights(0, 0)
            weights(0, 1)
            sp.wait_ge(h_raw, fill_tiles(2, 2) + KT)
            sp.wait_ge(ss_done, KT * NC_ * 2)
            sp.dma_start(ptab[0:1, :].bitcast(I32), A["page_table"].rearrange("(a b) p -> a (b p)", a=1))\
              .then_inc(d_tab, 16)
            with nc.allow_non_contiguous_dma(reason="a gain by partition"):
                sp.dma_start(sgf, A["diff_sub_gain"].rearrange("a d -> d a")).then_inc(d_ld, 16)
            sp.dma_start(gqb, A["diff_q_gain"].to_broadcast([P, 64])).then_inc(d_ld, 16)
            sp.dma_start(gkb, A["diff_k_gain"].to_broadcast([P, 64])).then_inc(d_ld, 16)
            for x, name in enumerate(("diff_lam_q1", "diff_lam_k1", "diff_lam_q2", "diff_lam_k2")):
                sp.dma_start(lamv[:, x, :], A[name].to_broadcast([P, 64])).then_inc(d_ld, 16)
            sp.dma_start(strip, A["c_dist"]).then_inc(d_ld, 16)
            sp.dma_start(sbt, A["c_sdist"]).then_inc(d_ld, 16)
            sp.wait_ge(d_pk, 1)
            body(Round(0, True, False, False))
            with sp.Fori(1, DH - 1) as i:
                body(Round(i, True, True, True))
            body(Round(DH - 1, True, True, False), True)
            body(Round(DH, False, True, False))
            out_sp(sp, 1, wout, UNIT_AT[1] + 32, RAW_AT[1] + 32, [(4, 0)], diff_stage_wait, loaded=2,
                   after=lru_setup_sp if LAYERS > 2 else None)

        def diff_stage_wait(sp, lay):
            for x in range(2):
                sp.wait_ge(d_gst[x], 16 * DH * (2 - x) + 16)
                sp.wait_ge(d_ost[x], 16 * 4 * DH + 16)
            for x in (d_kst, d_vst, d_sst):
                sp.wait_ge(x, 16 * DH + 16)
            sp.wait_ge(d_rows, 32 * DH + 16)
            sp.wait_ge(d_sfo, done(DH - 1))
            sp.wait_ge(d_te, done(DN0 + (DH - 1) * DN + len(diff_uses(False, True)) - 1))

        def diff_pe(pe):
            def body(r):
                def bank_free(*use):
                    pe.wait_ge(d_te, prior(r.tr(*use)))

                def scores(t, m):
                    pe.wait_ge(d_mx, prior(r.p16.at(2 * t + m)))
                    W = (t + 1) * P
                    for a in range(0, W, 512):
                        e = min(W, a + 512)
                        last = nc.tensor.matmul(SCB[:, a:e], qf[64 * m:64 * m + 64, t * P:(t + 1) * P],
                                                kf[64 * m:64 * m + 64, a:e], start=True, stop=True)
                    last.then_inc(d_sc, 1)

                def probs(tb, half):
                    bank_free("B", tb, half)
                    for y in range(min(4, tb + 1 - 4 * half)):
                        b = 4 * half + y
                        last = nc.tensor.transpose(DTR[:, y * P:(y + 1) * P], sc2[:, tb % 2, 0, b * P:(b + 1) * P],
                                                   ident[:, :])
                    last.then_inc(d_tr, 1)

                for s in range(12):
                    if r.attn and s < NBLK:
                        if s == 0:
                            pe.wait_ge(d_te, r.base.at(0) + 1)
                        scores(s, 0)
                    for x in V_AT.get(s, []) if r.attn else []:
                        pe.wait_ge(d_vld[x % 2], (r.p4.at(x // 2) * PAGES) * 16 + 16 * PAGES)
                        bank_free("V", x)
                        for p in range(PAGES):
                            last = nc.tensor.matmul(DTR[:, 0:1], vring[:, x % 2, p * P:(p + 1) * P],
                                                    pTs[:, p * NS + x:p * NS + x + 1], start=(p == 0),
                                                    stop=(p == PAGES - 1))
                        last.then_inc(d_tr, 1)
                    if r.proj:
                        unit_chunk(pe, r.unit, s // NC_, s % NC_, FILL_AT[1], ks=range(0, KT // 2))
                    if r.attn and 1 <= s <= NBLK:
                        pe.wait_ge(d_pc, done(r.p8.at(s - 1)))
                        probs(s - 1, 0)
                    if r.attn and s < NBLK:
                        scores(s, 1)
                    if r.attn and NBLK // 2 < s <= NBLK:
                        probs(s - 1, 1)
                    if r.proj:
                        unit_chunk(pe, r.unit, s // NC_, s % NC_, FILL_AT[1], ks=range(KT // 2, KT))
                        for x in T1_AT.get(s, []):
                            js, cs = divmod(x, NC_)
                            c0 = CHUNKS[cs][0]
                            pe.wait_ge(unit_ev, ev_val(r.unit.at(js), cs))
                            bank_free("T1", x)
                            for b, w in blocks_of(cs):
                                o = b * P - c0
                                last = nc.tensor.transpose(DTR[0:w, o:o + P], hraw[:, x % 2, o:o + w], ident[:, :])
                            last.then_inc(d_tr, 1)
                        if s == QB_AT:
                            pe.wait_ge(d_qs, done(r.n2.at(0)))
                            for b in range(NS):
                                last = nc.tensor.matmul(QB[:, b * P:(b + 1) * P],
                                                        ident[0:NS, b:b + 1].to_broadcast([NS, P]),
                                                        qtk[0:NS, SEQ:TX], start=True, stop=True)
                            last.then_inc(d_qb, 1)
                        if s in T2_AT:
                            x = (8, 9).index(s)
                            pe.wait_ge(d_kn, done(r.n2.at(x)))
                            for half in range(2):
                                bank_free(T2_AT[s], half)
                                for y in range(4):
                                    b = 4 * half + y
                                    last = nc.tensor.transpose(DTR[:, y * P:(y + 1) * P],
                                                               (qtk, ktk)[x][:, b * P:(b + 1) * P], ident[:, :])
                                last.then_inc(d_tr, 1)
                    if r.attn and 1 <= s <= NBLK:
                        tb = s - 1
                        pe.wait_ge(d_te, done(r.tr("B", tb, tb // 4)))
                        pe.wait_ge(d_on, prior(r.p8.at(tb)))
                        for b in range(tb + 1):
                            last = nc.tensor.matmul(DOB[:, 0:P], pT[:, tb % 2, b, :], vf[:, b, :], start=(b == 0),
                                                    stop=(b == tb))
                        last.then_inc(d_o, 1)
                    if r.attn and 2 <= s <= 9:
                        pe.wait_ge(d_on, done(r.p8.at(s - 2)))
                        bank_free("D", s - 2)
                        nc.tensor.transpose(DTR[:, 0:P], donb, ident[:, :]).then_inc(d_tr, 1)
                    if r.attn and s == 9:
                        pe.wait_ge(d_ssq, done(r.p1.at(0)))
                        bank_free("F")
                        nc.tensor.matmul(DTR[:, 0:NS], ones[:, :], osq2, start=True, stop=True).then_inc(d_tr, 1)
                    if r.proj and s == 9:
                        if r.attn:
                            pe.wait_ge(d_mx, done(r.p16.at(15)))
                        pe.wait_ge(d_sb, done(r.n1.at(0)))
                        hold(pe, "pe")
                        for m in range(2):
                            for p in range(PAGES):
                                last = nc.tensor.transpose(SSC[m][0:NS, p * P:(p + 1) * P], stok[:, m, p, :],
                                                           ident[:, :])
                        last.then_inc(d_st, 1)
                if r.proj:
                    pe.wait_ge(d_spc, done(r.n1.at(0)))
                    bank_free("P")
                    hold(pe, "pe")
                    for p in range(PAGES):
                        nc.tensor.transpose(DTR[:, p * NS:(p + 1) * NS], es[0:NS, 0, p * P:(p + 1) * P],
                                            ident[0:NS, 0:NS])
                    nc.tensor.matmul(DTR[:, 64:72], ones[0:NS, :], diagw[0:NS, :], start=True, stop=True)\
                      .then_inc(d_tr, 1)

            diff_rounds(pe, body)
            out_pe(pe, 1, UNIT_AT[1] + 32, [(4, 0)], LAST == 1)

        def diff_act(act):
            act.wait_ge(d_set, 1)
            act.activation(lam2, lam2, ACT.Exp).then_inc(d_set, 1)
            act.wait_ge(h_lo, fill_tiles(FILL_AT[1], 2) + KT)
            act.wait_ge(d_set, 3)

            def t1_copy(r, x):
                js, cs = divmod(x, NC_)
                c0 = CHUNKS[cs][0]
                dst = {0: qtk, 1: ktk, 3: vf.rearrange("p b d -> p (b d)")}[js]
                nb = 3 if cs < 2 else 2
                act.wait_ge(d_tr, done(r.tr("T1", x)))
                if x == K0:
                    act.wait_ge(d_kst, r.n1.at(0) * 16 + 16)
                    act.wait_ge(d_rows, r.n2.at(0) * 16 + 16)
                if x == V0:
                    act.wait_ge(d_vst, r.n1.at(0) * 16 + 16)
                if cs == 2:
                    rows = {0: qtk[0:NS, SEQ:TX], 1: ktk[0:NS, SEQ:TX], 3: vs8[0:NS, :]}[js]
                    act.activation(rows, DTR[0:NS, 256:384], ACT.Copy)
                if x == 11:
                    act.activation(vsf, hraw[:, 1, 256:264], ACT.Copy)
                act.activation(dst[:, c0:c0 + nb * P], DTR[:, 0:nb * P], ACT.Copy).then_inc(d_te, 1)
                if x in (2, 5):
                    act.wait_ge(d_te, done(r.tr("T1", x)))
                    act.sem_inc(d_t3, 1)

            def body(r):
                i = r.i

                def g_store(c):
                    c0, w = CHUNKS[c]
                    act.wait_ge(unit_ev, ev_val(r.unit.at(2), c))
                    act.dma_start(g_d[bass.ds(i, 1), :, c0:c0 + w].rearrange("a p t -> (a p) t"),
                                  dgst[:, c % 2, 0:w]).then_inc(d_gst[c % 2], 16)

                for s in range(12):
                    j, c = divmod(s, NC_)
                    c0, w = CHUNKS[c]
                    for x in V_AT.get(s, []) if r.attn else []:
                        act.wait_ge(d_tr, done(r.tr("V", x)))
                        if x == 0:
                            act.wait_ge(d_sst, r.p1.at(0) * 16 + 16)
                        act.activation(osm[:, x:x + 1], DTR[:, 0:1], ACT.Copy).then_inc(d_te, 1)
                        act.sem_inc(d_vu, 1)
                    if r.attn and 1 <= s <= NBLK:
                        tb = s - 1
                        for half in range(tb // 4 + 1):
                            act.wait_ge(d_tr, done(r.tr("B", tb, half)))
                            nb = min(4, tb + 1 - 4 * half)
                            act.activation(pT[:, tb % 2, 4 * half:4 * half + nb, :].rearrange("p b t -> p (b t)"),
                                           DTR[:, 0:nb * P], ACT.Copy).then_inc(d_te, 1)
                    if r.attn and 2 <= s <= 9:
                        act.wait_ge(d_rs, done(r.p8.at(s - 2)))
                        if s > 2:
                            act.wait_ge(d_tr, done(r.tr("D", s - 3)))
                        act.activation(donb, DOB[:, 0:P], ACT.Copy, scale=drs).then_inc(d_on, 1)
                    if r.attn and s < NBLK:
                        W = (s + 1) * P
                        act.wait_ge(d_nm, done(r.p8.at(s)))
                        for m in range(2):
                            act.activation(sc2[:, s % 2, m, 0:W], sc2[:, s % 2, m, 0:W], ACT.Exp,
                                           bias=nm2[:, s % 2, m:m + 1], accum_out=l2[:, s % 2, m:m + 1]).then_inc(d_ex, 1)
                    if r.proj:
                        if c == 0:
                            split_hi(act, r.unit, r.unit, j + 1)
                        src = unit_bank(j, c)[:, 0:w]
                        act.wait_ge(unit_ps, ps_val(r.unit.at(j), c))
                        if j != 2:
                            if s == 9:
                                act.wait_ge(unit_ev, ev_val(r.unit.at(2), 2))
                            if s < 2:
                                act.wait_ge(d_tr, r.base.at(0) + 1)
                            else:
                                act.wait_ge(d_tr, done(r.tr("T1", {9: 5, 10: 5}.get(s, s - 2))))
                            act.activation(hraw[:, s % 2, 0:w], src, ACT.Copy).then_inc(unit_ev, 1)
                        else:
                            act.wait_ge(d_gst[c % 2], (r.n1.at(0) if c == 1 else r.n2.at(c // 2)) * 16 + 16)
                            act.activation(dgst[:, c % 2, 0:w], src, ACT.Tanh, scale=0.5).then_inc(d_th, 1)
                        for x in T1_AT.get(s, []):
                            if x != 11:
                                t1_copy(r, x)
                        if s in (7, 8, 9):
                            g_store(s - 7)
                        if s in T2_AT:
                            dst = (qf, kf)[(8, 9).index(s)]
                            for half in range(2):
                                act.wait_ge(d_tr, done(r.tr(T2_AT[s], half)))
                                act.activation(dst[:, half * 512:(half + 1) * 512], DTR[:, :], ACT.Copy)\
                                   .then_inc(d_te, 1)
                        if s == 9:
                            act.wait_ge(d_kn, done(r.n2.at(1)))
                            act.dma_start(A["k_rows_prompt"][0, 0, :, bass.ds(i, 1), :]
                                          .rearrange("(b p) a d -> p b (a d)", p=P),
                                          ktk[:, 0:SEQ].rearrange("p (b d) -> p b d", b=NBLK)).then_inc(d_kst, 16)
                            act.dma_start(A["k_rows_sample"][0, :, 0, bass.ds(i, 1), :].rearrange("b a d -> b (a d)"),
                                          ktk[0:NS, SEQ:TX]).then_inc(d_rows, 16)
                    if r.attn and 1 <= s <= NBLK:
                        act.wait_ge(d_o, done(r.p8.at(s - 1)))
                        act.activation(junk, DOB[:, 0:P], ACT.Square, accum_out=dsq).then_inc(d_sq, 1)
                    if r.attn and 2 <= s <= 9:
                        tb = s - 2
                        act.wait_ge(d_tr, done(r.tr("D", tb)))
                        act.wait_ge(d_ost[tb % 2], r.p4.at(tb // 2) * 16 + 16)
                        act.activation(donst[:, tb % 2, :], DTR[:, 0:P], ACT.Copy, scale=sgf).then_inc(d_te, 1)
                        act.wait_ge(d_te, done(r.tr("D", tb)))
                        act.dma_start(on_d[bass.ds(i - 1, 1), :, tb * P:(tb + 1) * P].rearrange("a p t -> (a p) t"),
                                      donst[:, tb % 2, :]).then_inc(d_ost[tb % 2], 16)
                    if r.proj and s == 10:
                        act.wait_ge(d_snm, done(r.n1.at(0)))
                        for m in range(2):
                            act.activation(es[0:NS, m, :], SSC[m][0:NS, :], ACT.Exp, bias=snm[0:NS, m:m + 1],
                                           accum_out=sl[0:NS, m:m + 1])
                        for m in range(2):
                            last = act.activation(sef[0:NS, m:m + 1], sself[0:NS, m:m + 1], ACT.Exp,
                                                  bias=snm[0:NS, m:m + 1])
                        last.then_inc(d_sex, 1)
                    if r.attn and s == 10:
                        act.wait_ge(d_sfo, done(r.p1.at(0)))
                        act.dma_start(on_d[bass.ds(i - 1, 1), :, SEQ:T].rearrange("a p t -> (a p) t"), osm)\
                           .then_inc(d_sst, 16)
                if r.proj:
                    t1_copy(r, 11)
                    act.wait_ge(d_te, done(r.tr("T1", 11)))
                    act.dma_start(A["v_rows_prompt"][0, 0, :, bass.ds(i, 1), :]
                                  .rearrange("(b p) a d -> p b (a d)", p=P), vf).then_inc(d_vst, 16)
                    act.dma_start(A["v_rows_sample"][0, :, 0, bass.ds(i, 1), :].rearrange("b a d -> b (a d)"),
                                  vs8[0:NS, :]).then_inc(d_rows, 16)

            diff_rounds(act, body)
            out_act(act, 1, UNIT_AT[1] + 32, RAW_AT[1] + 32, [(4, 0)], LAST == 1)

        DCH_PER = 183

        def diff_dve(dve, ch):
            dve.wait_ge(d_tab, 16)
            ids = ptab[0:1, :].bitcast(I32).rearrange("o (b p) -> o b p", b=NS)
            pk = ppk[0:1, :].bitcast(I32).rearrange("o (b x) -> o b x", b=NS)
            ch.link(nc.vector.tensor_copy(pk, ids[:, :, 0:PAGES:3]))
            for y in (1, 2):
                n = (PAGES - y + 2) // 3
                last = nc.vector.scalar_tensor_tensor(pk[:, :, 0:n], ids[:, :, y:PAGES:3], float(128 ** y), pk[:, :, 0:n],
                                                      ALU.mult, ALU.add)
                if y == 1:
                    ch.link(last)
            last.then_inc(d_pk, 1)
            dve.wait_ge(d_ld, 16 * 9)
            ch.link(nc.vector.tensor_tensor(prod[:, 0:P].rearrange("p (a d) -> p a d", a=2), lamv[:, 0:4:2, :],
                                            lamv[:, 1:4:2, :], ALU.mult))
            nc.vector.tensor_reduce(lam2, prod[:, 0:P].rearrange("p (a d) -> p a d", a=2), AX.X, ALU.add)\
              .then_inc(d_set, 1)
            nc.vector.tensor_scalar(gqb, gqb, 0.125, None, ALU.mult)
            nc.vector.tensor_scalar(sgf, sgf, 1.0 - LAM_INIT, None, ALU.mult)
            ch.link(nc.vector.memset(qtk, 0.0))
            ch.link(nc.vector.memset(ktk, 0.0))
            dve.wait_ge(d_set, 2)
            ch.link(nc.vector.scalar_tensor_tensor(negl, lam2[:, 1:2], -LAM_INIT, lam2[:, 0:1], ALU.add, ALU.subtract))
            dve.sem_inc(d_set, 1)

            def max_scores(r, t, m):
                W = (t + 1) * P
                dve.wait_ge(d_sc, done(r.p16.at(2 * t + m)))
                if m == 0 and t >= 2:
                    dve.wait_ge(d_tr, done(r.tr("B", t - 2, (t - 2) // 4)))
                hold(dve, "dve")
                nc.vector.tensor_tensor_reduce(
                    out=sc2[:, t % 2, m, 0:W], in0=SCB[:, 0:W], in1=strip[:, SEQ - W:SEQ], scale=1.0,
                    scalar=-1e30, op0=ALU.add, op1=ALU.max, accum_out=mx2[:, t % 2, m:m + 1]).then_inc(d_mx, 1)

            def combine(r, tb):
                W = (tb + 1) * P
                dve.wait_ge(d_ex, done(r.p16.at(2 * tb + 1)))
                ch.link(nc.vector.reciprocal(ratio, l2[:, tb % 2, 1:2]))
                nc.vector.reciprocal(rl0[:, tb % 2:tb % 2 + 1], l2[:, tb % 2, 0:1])
                ch.link(nc.vector.tensor_tensor(ratio, ratio, l2[:, tb % 2, 0:1], ALU.mult))
                ch.link(nc.vector.tensor_tensor(ratio, ratio, negl, ALU.mult))
                nc.vector.scalar_tensor_tensor(sc2[:, tb % 2, 0, 0:W], sc2[:, tb % 2, 1, 0:W], ratio,
                                               sc2[:, tb % 2, 0, 0:W], ALU.mult, ALU.add).then_inc(d_pc, 1)

            def norm(r, x):
                dve.wait_ge(d_ns, done(r.n2.at(x)))
                nc.vector.tensor_reduce(rsk[:, 0:16], nsq[0].rearrange("p (g d) -> p g d", d=64), AX.X, ALU.add)
                nc.vector.tensor_reduce(rsk[:, 16:18], nsq[1].rearrange("p (g d) -> p g d", d=64), AX.X, ALU.add)\
                  .then_inc(d_nr, 1)
                dve.wait_ge(d_nr, done(r.n2.at(x)))
                dve.wait_ge(d_kn, prior(r.n2.at(x)))
                rsqrt(dve, ch, rsk, 1.0 / 64, rsn, ktmp, d_nn)

            def body(r):
                if r.attn:
                    ch.link(nc.vector.tensor_scalar(strip, strip, 0.5, None, ALU.mult))
                if r.proj:
                    ch.link(nc.vector.tensor_scalar(sbt, sbt, 0.5, None, ALU.mult))
                for s in range(12):
                    if r.attn and s < NBLK:
                        max_scores(r, s, 0)
                    if r.attn and 1 <= s <= EARLY:
                        combine(r, s - 1)
                    if r.attn and 2 <= s <= 9:
                        tb = s - 2
                        dve.wait_ge(d_sq, done(r.p8.at(tb)))
                        d0 = rl0[:, tb % 2:tb % 2 + 1]
                        ch.link(nc.vector.scalar_tensor_tensor(dx, dsq, d0, d0, ALU.mult, ALU.mult))
                        dve.wait_ge(d_on, prior(r.p8.at(tb)))
                        rsqrt(dve, ch, dx, 1.0 / DV, drs, rnt)
                        nc.vector.tensor_tensor(drs, drs, d0, ALU.mult).then_inc(d_rs, 1)
                    if r.attn and s < NBLK:
                        max_scores(r, s, 1)
                        dve.wait_ge(d_mx, done(r.p16.at(2 * s + 1)))
                        nc.vector.tensor_scalar(nm2[:, s % 2, :], mx2[:, s % 2, :], -1.0, None, ALU.mult)\
                          .then_inc(d_nm, 1)
                    if r.attn and s == 8:
                        dve.wait_ge(d_te, done(r.tr("V", 7)))
                        ch.link(nc.vector.tensor_tensor(vsf, vsf, pTs[:, 64:72], ALU.mult))
                        ch.link(nc.vector.tensor_tensor(osm, osm, vsf, ALU.add))
                        nc.vector.tensor_tensor(osq2, osm, osm, ALU.mult).then_inc(d_ssq, 1)
                    if r.proj:
                        if 6 <= s <= 8:
                            c = s - 6
                            w = CHUNKS[c][1]
                            dve.wait_ge(d_th, done(r.n3.at(c)))
                            dve.wait_ge(unit_ev, ev_val(r.unit.at(2), c) - 1)
                            nc.vector.scalar_tensor_tensor(dgst[:, c % 2, 0:w], dgst[:, c % 2, 0:w], 1.0,
                                                           unit_bank(2, c)[:, 0:w], ALU.add, ALU.mult)\
                              .then_inc(unit_ev, 1)
                    if r.attn and EARLY <= s < NBLK:
                        combine(r, s)
                    if r.proj:
                        if s == 8:
                            dve.wait_ge(d_kn, done(r.n2.at(1)))
                            ch.link(nc.vector.tensor_tensor(prod[0:NS, 0:P], qtk[0:NS, SEQ:TX], ktk[0:NS, SEQ:TX],
                                                            ALU.mult))
                            ch.link(nc.vector.tensor_reduce(sself[0:NS, :],
                                                            prod[0:NS, 0:P].rearrange("p (g d) -> p g d", d=64),
                                                            AX.X, ALU.add))
                        for b in SLABS.get(s, []):
                            if b == 0:
                                dve.wait_ge(d_qb, done(r.n1.at(0)))
                            dve.wait_ge(d_kld[b % 2], (r.n4.at(b // 2) * PAGES) * 16 + 16 * PAGES)
                            ch.link(nc.vector.tensor_tensor(
                                prod[:, 0:PG].rearrange("p (g d) -> p g d", g=PAGES),
                                kring[:, b % 2, :].rearrange("p (g d) -> p g d", g=PAGES),
                                QB[:, b * P:(b + 1) * P].rearrange("p (a d) -> p a d", a=1)
                                .to_broadcast([P, PAGES, P]), ALU.mult))
                            nc.vector.tensor_reduce(stok[:, :, :, b].rearrange("p m g -> p g m"),
                                                    prod[:, 0:PG].rearrange("p (g m d) -> p g m d", g=PAGES, m=2),
                                                    AX.X, ALU.add).then_inc(d_ku, 1)
                            dve.wait_ge(d_ku, r.n8.at(b) + 3)
                        if s in NORM_AT:
                            norm(r, NORM_AT.index(s))
                        if s == 9:
                            for m in range(2):
                                last = nc.vector.tensor_tensor(stok[:, m, :, :], stok[:, m, :, :],
                                                               sbt.rearrange("p (g a) -> p g a", a=1)
                                                               .to_broadcast([P, PAGES, NS]), ALU.add)
                            last.then_inc(d_sb, 1)
                    if r.proj and s == 10:
                        dve.wait_ge(d_st, done(r.n1.at(0)))
                        nc.vector.tensor_reduce(smx[0:NS, 0:1], SSC[0][0:NS, :], AX.X, ALU.max)
                        ch.link(nc.vector.tensor_reduce(smx[0:NS, 1:2], SSC[1][0:NS, :], AX.X, ALU.max))
                        ch.link(nc.vector.tensor_tensor(smx[0:NS, :], smx[0:NS, :], sself[0:NS, :], ALU.max))
                        nc.vector.tensor_scalar(snm[0:NS, :], smx[0:NS, :], -1.0, None, ALU.mult).then_inc(d_snm, 1)
                        dve.wait_ge(d_sex, done(r.n1.at(0)))
                        ch.link(nc.vector.tensor_tensor(sl[0:NS, :], sl[0:NS, :], sef[0:NS, :], ALU.add))
                        ch.link(nc.vector.reciprocal(sl[0:NS, :], sl[0:NS, :]))
                        ch.link(nc.vector.tensor_tensor(sl[0:NS, 1:2], sl[0:NS, 1:2], negl[0:NS, :], ALU.mult))
                        nc.vector.tensor_scalar(es[0:NS, 1, :], es[0:NS, 1, :], sl[0:NS, 1:2], None, ALU.mult)
                        ch.link(nc.vector.tensor_scalar(wself[0:NS, :], sef[0:NS, 1:2], sl[0:NS, 1:2], None, ALU.mult))
                        ch.link(nc.vector.scalar_tensor_tensor(wself[0:NS, :], sef[0:NS, 0:1], sl[0:NS, 0:1],
                                                               wself[0:NS, :], ALU.mult, ALU.add))
                        nc.vector.tensor_scalar(diagw[0:NS, :], ident[0:NS, 0:NS], wself[0:NS, :], None, ALU.mult)
                        nc.vector.scalar_tensor_tensor(es[0:NS, 0, :], es[0:NS, 0, :], sl[0:NS, 0:1], es[0:NS, 1, :],
                                                       ALU.mult, ALU.add).then_inc(d_spc, 1)
                    if r.attn and s == 9:
                        dve.wait_ge(d_tr, done(r.tr("F")))
                        nc.vector.tensor_copy(fsum, DTR[:, 0:NS]).then_inc(d_te, 1)
                        dve.wait_ge(d_te, done(r.tr("F")))
                        rsqrt(dve, ch, fsum, 1.0 / DV, ors, ont)
                        nc.vector.scalar_tensor_tensor(osm, osm, sgf, ors, ALU.mult, ALU.mult).then_inc(d_sfo, 1)
                if r.proj:
                    dve.wait_ge(d_tr, done(r.tr("P")))
                    nc.vector.tensor_copy(pTs, DTR[:, 0:72]).then_inc(d_te, 1)
                    dve.wait_ge(d_te, done(r.tr("P")))

            diff_rounds(dve, body, ch)
            out_dve(dve, ch, 1, UNIT_AT[1] + 32, [(4, 0)], LAST == 1, 0.5)

        def diff_pool(pool):
            with pool.Fori(0, DH) as h:
                unit, n2, n4 = Pos(UNIT_AT[1], h, 4), Pos(0, h, 2), Pos(0, h, 4)
                for j in range(4):
                    split_lo(pool, unit, j + 1)
                    if j in (0, 1):
                        v, gain = ((qtk, gqb), (ktk, gkb))[j]
                        g3 = v.rearrange("p (g d) -> p g d", d=64)
                        pool.wait_ge(d_t3, done(n2.at(j)))
                        pool.wait_ge(d_nr, prior(n2.at(j)))
                        pool.tensor_tensor(nsq[1], v[:, SEQ:TX], v[:, SEQ:TX], ALU.mult)
                        pool.tensor_tensor(nsq[0], v[:, 0:SEQ], v[:, 0:SEQ], ALU.mult).then_inc(d_ns, 1)
                        pool.wait_ge(d_nn, done(n2.at(j)))
                        for x, (ga_, ge) in enumerate(((16, 18), (0, 16))):
                            part = g3[:, ga_:ge, :]
                            pool.tensor_tensor(part, part, rsn[:, ga_:ge].rearrange("p (g a) -> p g a", a=1)
                                               .to_broadcast([P, ge - ga_, 64]), ALU.mult).then_inc(d_ng, 1)
                            pool.wait_ge(d_ng, done(n4.at(2 * j + x)))
                            pool.tensor_tensor(part, part, gain.rearrange("p (a d) -> p a d", a=1)
                                               .to_broadcast([P, ge - ga_, 64]), ALU.mult).then_inc((d_qs, d_kn)[x], 1)
            out_pool(pool, 1, UNIT_AT[1] + 32, [(4, 0)], LAST == 1)

        LC0, LH0, LW, LB, LBA, LBX, LY, LNY = 0, 24, 32, 36, 37, 38, 39, 40
        NPAR, NOUT = 40, 36
        OH, OC, OHS, OCS = 0, 1, 4, 12
        al = arena()
        xpad = al.take(3 + SEQ)
        xcv, gtr, gti, ga, gm, hb, lg, pb = (al.take(T) for _ in range(8))
        al.at = LRU_STAGE + 2 * KT * WMAX
        lrow = al.take(LRU_W)
        lpar = al.take(LRU_B, NPAR + 1)
        lout = al.take(LRU_B, NOUT)
        lp, lo = al.take(NPAR + 1), al.take(NOUT)
        xs8 = al.take(NS)
        wax = al.take(2, 2, P)
        sp_ = [al.take(LRU_B) for _ in range(6)]
        tmp_s = al.take(NS)
        LTR = bank[2]
        l_ld, l_set, l_ptr, l_z = sem("l_ld"), sem("l_set"), sem("l_ptr"), sem("l_z")
        l_xc = sem("l_xc")
        l_gt, l_tg = sem("l_gt"), sem("l_tg")
        l_at, l_m, l_sq, l_h = sem("l_at"), sem("l_m"), sem("l_sq"), sem("l_h")
        l_th = sem("l_th")
        l_wl = sems("l_wl", 2)
        l_pr, l_hst, l_ost = sem("l_pr"), sem("l_hst"), sem("l_ost")
        l_otr, l_oev = sem("l_otr"), sem("l_oev")
        CREDITS += [(x, 1) for x in (l_xc, l_tg, l_at, l_m, l_sq, l_h, l_th, l_pr)] + [(l_gt, 12)]
        CREDITS += [(x, 16) for x in (l_hst,)]
        LU, LF = UNIT_AT[2], FILL_AT[2]

        def lru_at(n):
            return (Pos(LU, n, 2), Pos(0, n, 1), Pos(0, n, 2), Pos(0, n, 3), Pos(0, n, 6))

        def store_states(sp, n):
            sp.wait_ge(l_pr, n + 2)
            sp.dma_start(on_d[bass.ds(n, 1), :, :].rearrange("a p t -> (a p) t"), pb).then_inc(l_hst, 16)

        def gates(sp, n, slot):
            for x, name in enumerate(("lru_wa", "lru_wx")):
                sp.dma_start(wax[:, slot, x, :], A[name][0, bass.ds(n, 1), :, :].rearrange("a c d -> (a c) d"))\
                  .then_inc(l_wl[slot], 16)

        def lru_setup_sp(sp):
            rows = 0
            for name in ("state_lru_conv", "state_lru_h", "lru_conv_w", "lru_conv_b", "lru_ba", "lru_bx", "lru_lambda"):
                src = {"state_lru_conv": lambda a: a[0].rearrange("b r w -> (b r) w"),
                       "state_lru_h": lambda a: a[0], "lru_conv_w": lambda a: a[0]}.get(name, lambda a: a)(A[name])
                sp.dma_start(lrow[rows:rows + src.shape[0], :], src).then_inc(l_ld, 16)
                rows += src.shape[0]
            gates(sp, 0, 0)
            gates(sp, 1, 1)

        def lru_sp(sp):
            win, wout = A["lru_w_in"][0], A["lru_w_out"][0]

            def weights(n):
                for j in range(2):
                    load_w(sp, Pos(LU, n, 2), j, w_block(win, 0, KT, n * P + j * LRU_W))

            weights(0)

            def block_pair(n, more):
                for x in range(2):
                    if more or x == 0:
                        weights(n + (x + 1))
                        store_states(sp, n + x)
                    if more:
                        gates(sp, n + (x + 2), x)

            with sp.Fori(0, LRU_B // 2 - 1) as i:
                block_pair(i * 2, True)
            block_pair(LRU_B - 2, False)
            sp.wait_ge(l_hst, 16 * (LRU_B - 2) + 16)
            for c in range(2):
                stage_load(sp, stage_of(2), 6, 0, c)
            out_sp(sp, 2, wout, LU + LRU_IN, LU + LRU_IN, [(6, 0), (7, KT)], lru_stage_wait)

        def lru_stage_wait(sp, lay):
            store_states(sp, LRU_B - 1)
            sp.wait_ge(l_hst, 16 * LRU_B + 16)
            sp.wait_ge(l_ost, 16 * 4)

        def lru_pe(pe):
            pe.wait_ge(l_ld, 16 * 7)
            for n in range(LRU_B):
                last = nc.tensor.transpose(LTR[:, n * NPAR:(n + 1) * NPAR], lrow[0:NPAR, n * P:(n + 1) * P],
                                           ident[0:NPAR, 0:NPAR])
            last.then_inc(l_ptr, 1)

            def block(n, slot, pair):
                unit, n1, n2, n3, n6 = lru_at(n)
                for s in range(6):
                    unit_chunk(pe, unit, s // NC_, s % NC_, LF)
                    if s == 4:
                        pe.wait_ge(l_set, 1)
                        pe.wait_ge(l_xc, done(n1.at(0)))
                        pe.wait_ge(l_wl[slot], pair * 32 + 32)
                        pe.wait_ge(l_tg, prior(n6.at(0)))
                        for c in range(NC_):
                            c0, w = CHUNKS[c]
                            for x in range(2):
                                nc.tensor.matmul(bank[2 + 3 * x + c][:, 0:w], wax[:, slot, x, :], xcv[:, c0:c0 + w],
                                                 start=True, stop=True).then_inc(l_gt, 1)

            with pe.Fori(0, LRU_B // 2) as i:
                block(i * 2, 0, i)
                block(i * 2 + 1, 1, i)
            pe.wait_ge(l_h, done(LRU_B - 1))
            pe.wait_ge(l_tg, done(6 * LRU_B - 1))
            pe.wait_ge(l_oev, 1)
            for n in range(LRU_B):
                last = nc.tensor.transpose(bank[2 + n // 4][0:NOUT, (n % 4) * P:(n % 4 + 1) * P], lout[:, n, :], ident[:, :])
            last.then_inc(l_otr, 1)
            out_pe(pe, 2, LU + LRU_IN, [(6, 0), (7, KT)], LAST == 2)

        def lru_act(act):
            act.wait_ge(l_z, 1)
            act.activation(sp_[1], sp_[1], ACT.Exp).then_inc(l_z, 1)

            def block(n):
                unit, n1, n2, n3, n6 = lru_at(n)

                def g_tanh(c):
                    c0, w = CHUNKS[c]
                    act.wait_ge(unit_ps, ps_val(unit.at(1), c))
                    act.wait_ge(l_pr, prior(n1.at(0)))
                    act.activation(lg[:, c0:c0 + w], unit_bank(1, c)[:, 0:w], ACT.Tanh, scale=0.5).then_inc(l_th, 1)

                split_hi(act, unit, unit, 1)
                act.wait_ge(l_xc, prior(n1.at(0)))
                for c in range(NC_):
                    c0, w = CHUNKS[c]
                    act.wait_ge(unit_ps, ps_val(unit.at(0), c))
                    wp = min(w, SEQ - c0)
                    if wp < w:
                        act.activation(xs8, unit_bank(0, c)[:, wp:w], ACT.Copy)
                    act.activation(xpad[:, 3 + c0:3 + c0 + wp], unit_bank(0, c)[:, 0:wp], ACT.Copy).then_inc(unit_ev, 1)
                split_hi(act, unit, unit, 2)
                g_tanh(0)
                g_tanh(1)
                for c in range(NC_):
                    c0, w = CHUNKS[c]
                    for x in range(2):
                        act.wait_ge(l_gt, n6.at(2 * c + x) + 13)
                        act.activation((gtr, gti)[x][:, c0:c0 + w], bank[2 + 3 * x + c][:, 0:w], ACT.Tanh, scale=0.5,
                                       bias=lp[:, LBA + x:LBA + x + 1]).then_inc(l_tg, 1)
                act.wait_ge(l_tg, done(n6.at(5)))
                act.wait_ge(l_h, prior(n1.at(0)))
                act.activation(ga, gtr, ACT.Exp, scale=lp[:, LNY:LNY + 1], bias=lp[:, LNY:LNY + 1])
                act.activation(gtr, gtr, ACT.Tanh, scale=lp[:, LY:LY + 1], bias=lp[:, LY:LY + 1]).then_inc(l_at, 1)
                g_tanh(2)
                act.wait_ge(l_m, done(n1.at(0)))
                act.activation(gm, gm, ACT.Sqrt, scale=0.25).then_inc(l_sq, 1)
                act.wait_ge(unit_ev, ev_val(unit.at(1), 2))

            with act.Fori(0, LRU_B) as n:
                block(n)
            act.wait_ge(l_otr, 1)
            for x in range(3):
                last = act.activation(lrow[0:NOUT, x * 512:(x + 1) * 512], bank[2 + x][0:NOUT, :], ACT.Copy)
            last.then_inc(l_otr, 1)
            act.wait_ge(l_otr, 2)
            for name, at, n in (("lru_h_prompt", OH, 1), ("lru_conv_prompt", OC, 3), ("lru_h_sample", OHS, NS),
                                ("lru_conv_sample", OCS, 3 * NS)):
                dst = A[name][0] if len(A[name].shape) == 3 else A[name] if n == 1 else A[name][0]
                if name == "lru_conv_prompt":
                    dst = A[name][0, 0]
                if name == "lru_conv_sample":
                    dst = A[name][0].rearrange("b r w -> (b r) w")
                act.dma_start(dst, lrow[at:at + n, :]).then_inc(l_ost, 16)
            out_act(act, 2, LU + LRU_IN, LU + LRU_IN, [(6, 0), (7, KT)], LAST == 2)

        LCH_PER = 9

        def lru_dve(dve, ch):
            dve.wait_ge(l_ptr, 1)
            nc.vector.memset(xpad[:, 0:3], 0.0)
            ch.link(nc.vector.tensor_copy(lpar[:, :, 0:NPAR], LTR[:, 0:LRU_B * NPAR].rearrange("p (n c) -> p n c", n=LRU_B)))
            lam, z, s, q, p, neg = sp_
            ch.link(nc.vector.tensor_copy(lam, lpar[:, :, LY]))
            ch.link(nc.vector.tensor_scalar(neg, lam, -1.0, None, ALU.mult))
            nc.vector.tensor_tensor(z, lam, neg, ALU.min).then_inc(l_z, 1)
            dve.wait_ge(l_z, 2)
            ch.link(nc.vector.tensor_scalar(s, z, 2.0, None, ALU.add))
            ch.link(nc.vector.reciprocal(s, s))
            ch.link(nc.vector.tensor_tensor(s, s, z, ALU.mult))
            ch.link(nc.vector.tensor_tensor(q, s, s, ALU.mult))
            ch.link(nc.vector.tensor_scalar(p, q, 1.0 / 19, None, ALU.mult))
            for k in range(17, 2, -2):
                ch.link(nc.vector.scalar_tensor_tensor(p, p, 1.0 / k, q, ALU.add, ALU.mult))
            ch.link(nc.vector.scalar_tensor_tensor(p, p, 1.0, s, ALU.add, ALU.mult))
            ch.link(nc.vector.tensor_scalar(neg, neg, 0.0, 0.5, ALU.max, ALU.mult))
            ch.link(nc.vector.tensor_tensor(p, p, neg, ALU.add))
            nc.vector.tensor_scalar(lpar[:, :, LY], p, 8.0, None, ALU.mult)
            nc.vector.tensor_scalar(lpar[:, :, LNY], p, -8.0, None, ALU.mult)
            ch.link(nc.vector.tensor_scalar(lpar[:, :, LBA:LBX + 1], lpar[:, :, LBA:LBX + 1], 0.5, None, ALU.mult))
            dve.sem_inc(l_set, 1)

            def block(n):
                unit, n1, n2, n3, n6 = lru_at(n)
                ch.link(nc.vector.tensor_copy(lp, lpar[:, bass.ds(n, 1), :].rearrange("p a c -> p (a c)")))
                dve.wait_ge(unit_ev, ev_val(unit.at(0), 2))
                dve.wait_ge(l_gt, n6.at(0) + 12)
                cs = lp[:, LC0:LC0 + 24].rearrange("p (b r) -> p b r", r=3)
                oc = lo[:, OCS:OCS + 24].rearrange("p (b r) -> p b r", r=3)
                nc.vector.tensor_copy(lo[:, OC:OC + 3], xpad[:, SEQ:SEQ + 3])
                nc.vector.tensor_copy(oc[:, :, 0:2], cs[:, :, 1:3])
                nc.vector.tensor_copy(oc[:, :, 2], xs8)
                for k in range(4):
                    tap = lp[:, LW + k:LW + k + 1]
                    src_s = cs[:, :, k] if k < 3 else xs8
                    if k == 0:
                        nc.vector.tensor_scalar(xcv[:, SEQ:T], src_s, tap, lp[:, LB:LB + 1], ALU.mult, ALU.add)
                        ins = nc.vector.tensor_scalar(xcv[:, 0:SEQ], xpad[:, 0:SEQ], tap, lp[:, LB:LB + 1], ALU.mult,
                                                      ALU.add)
                    else:
                        nc.vector.scalar_tensor_tensor(xcv[:, SEQ:T], src_s, tap, xcv[:, SEQ:T], ALU.mult, ALU.add)
                        ins = nc.vector.scalar_tensor_tensor(xcv[:, 0:SEQ], xpad[:, k:k + SEQ], tap, xcv[:, 0:SEQ],
                                                             ALU.mult, ALU.add)
                    if k < 3:
                        ch.link(ins)
                ins.then_inc(l_xc, 1)

                def g_mul(c):
                    c0, w = CHUNKS[c]
                    dve.wait_ge(l_th, done(n3.at(c)))
                    dve.wait_ge(unit_ev, ev_val(unit.at(1), c) - 1)
                    nc.vector.scalar_tensor_tensor(lg[:, c0:c0 + w], lg[:, c0:c0 + w], 1.0,
                                                   unit_bank(1, c)[:, 0:w], ALU.add, ALU.mult).then_inc(unit_ev, 1)

                g_mul(0)
                g_mul(1)
                dve.wait_ge(l_at, done(n1.at(0)))
                ch.link(nc.vector.tensor_tensor(gm, ga, ga, ALU.mult))
                nc.vector.scalar_tensor_tensor(gm, gm, 1.0, gtr, ALU.add, ALU.mult).then_inc(l_m, 1)
                ch.link(nc.vector.scalar_tensor_tensor(gti, gti, 1.0, xcv, ALU.add, ALU.mult))
                g_mul(2)
                dve.wait_ge(l_sq, done(n1.at(0)))
                dve.wait_ge(l_pr, prior(n1.at(0)))
                nc.vector.tensor_tensor(tmp_s, ga[:, SEQ:T], lp[:, LH0:LH0 + NS], ALU.mult)
                ch.link(nc.vector.tensor_tensor(gti, gti, gm, ALU.mult))
                nc.vector.tensor_tensor(hb[:, SEQ:T], tmp_s, gti[:, SEQ:T], ALU.add)
                nc.vector.tensor_tensor_scan(hb[:, 0:SEQ], ga[:, 0:SEQ], gti[:, 0:SEQ], 0.0, ALU.mult, ALU.add)\
                  .then_inc(l_h, 1)
                dve.wait_ge(l_h, done(n1.at(0)))
                nc.vector.tensor_copy(lo[:, OHS:OHS + NS], hb[:, SEQ:T])
                ch.link(nc.vector.tensor_copy(lo[:, OH:OH + 1], hb[:, SEQ - 1:SEQ]))
                ch.link(nc.vector.tensor_copy(lout[:, bass.ds(n, 1), :].rearrange("p a c -> p (a c)"), lo))

            with dve.Fori(0, LRU_B) as n:
                ch.loop(n, 0, LCH_PER)
                block(n)
            ch.done(LRU_B)
            dve.sem_inc(l_oev, 1)
            out_dve(dve, ch, 2, LU + LRU_IN, [(6, 0), (7, KT)], LAST == 2, 0.5)

        def lru_pool(pool):
            with pool.Fori(0, LRU_B) as n:
                unit = Pos(LU, n, 2)
                for j in range(2):
                    split_lo(pool, unit, j + 1)
                pool.wait_ge(l_h, done(n))
                pool.wait_ge(l_hst, n * 16 + 16)
                pool.tensor_tensor(pb, hb, lg, ALU.mult).then_inc(l_pr, 1)
            out_pool(pool, 2, LU + LRU_IN, [(6, 0), (7, KT)], LAST == 2)

        block = ctx.enter_context(nc.Block())
        LAST = LAYERS - 1
        outp = output_parts(LAYERS)
        ret_fills = {lay: [(FILL_AT[lay] + 1, 0), (FILL_AT[lay] + 2, KT)] for lay in (0, 3)}

        @block.sync
        def _(sp):
            for x, n in CREDITS:
                sp.sem_inc(x, n)
            sp.sem_inc(unit_ps, CR_PS)
            sp.sem_inc(unit_ev, CR)
            input_sp(sp)
            ret_sp(sp, 0)
            if LAYERS > 1:
                diff_sp(sp)
            if LAYERS > 2:
                lru_sp(sp)
            if LAYERS > 3:
                ret_sp(sp, 3)
            outp[3](sp)

        @block.tensor
        def _(pe):
            pe.wait_ge(const_ms, 2)
            input_pe(pe)
            for lay in range(LAYERS):
                if lay in (0, 3):
                    ret_pe(pe, lay)
                    out_pe(pe, lay, UNIT_AT[lay] + 48, ret_fills[lay], LAST == lay)
                else:
                    (diff_pe, lru_pe)[lay - 1](pe)
            outp[0](pe)

        @block.scalar
        def _(act):
            act.wait_ge(const_ms, 2)
            input_act(act)
            for lay in range(LAYERS):
                if lay in (0, 3):
                    ret_act(act, lay)
                    out_act(act, lay, UNIT_AT[lay] + 48, RAW_AT[lay] + 48, ret_fills[lay], LAST == lay)
                else:
                    (diff_act, lru_act)[lay - 1](act)
            outp[1](act)

        @block.vector
        def _(dve):
            ch = Chain(dve, dve_own)
            input_dve(dve, ch)
            for lay in range(LAYERS):
                if lay in (0, 3):
                    ret_dve(dve, ch, lay)
                    out_dve(dve, ch, lay, UNIT_AT[lay] + 48, ret_fills[lay], LAST == lay, 1.0)
                else:
                    (diff_dve, lru_dve)[lay - 1](dve, ch)
            outp[2](dve)

        @block.gpsimd
        def _(pool):
            for c in range(NC_):
                fill_parts(None, None, pool, 0, c)
                if c == 0:
                    split_lo(pool, Pos(0), 0)
            for lay in range(LAYERS):
                if lay in (0, 3):
                    ret_pool(pool, lay)
                    out_pool(pool, lay, UNIT_AT[lay] + 48, ret_fills[lay], LAST == lay)
                else:
                    (diff_pool, lru_pool)[lay - 1](pool)


_OUTS = (("y_prompt", (1, SEQ, D_MODEL)), ("y_sample", (NS, 1, D_MODEL)),
         ("ret_state_prompt", (2, 1, RH, RDK, RDV)), ("ret_state_sample", (2, NS, RH, RDK, RDV)),
         ("k_rows_prompt", (1, 1, SEQ, DH, DV)), ("v_rows_prompt", (1, 1, SEQ, DH, DV)),
         ("k_rows_sample", (1, NS, 1, DH, DV)), ("v_rows_sample", (1, NS, 1, DH, DV)),
         ("lru_h_prompt", (1, 1, LRU_W)), ("lru_conv_prompt", (1, 1, 3, LRU_W)),
         ("lru_h_sample", (1, NS, LRU_W)), ("lru_conv_sample", (1, NS, 3, LRU_W)))


def kernel(**inputs):
    import numpy as _np
    import concourse.bacc as _bacc
    from concourse import mybir as _mybir
    from concourse.bass_utils import run_bass_kernel_spmd as _run

    nc = _bacc.Bacc("TRN2", target_bir_lowering=False, num_devices=1)
    arrays, A = {}, {}
    for name, value in {**inputs, **constants()}.items():
        a = _np.ascontiguousarray(value)
        arrays[f"in_{name}"] = a
        A[name] = nc.dram_tensor(f"in_{name}", a.shape, _mybir.dt.from_np(a.dtype), kind="ExternalInput").ap()
    for name, shape in _OUTS:
        A[name] = nc.dram_tensor(f"out_{name}", shape, _mybir.dt.float32, kind="ExternalOutput").ap()
    trunk(nc, A)
    r = _run(nc, [arrays], core_ids=[0])
    return tuple(r.results[0][f"out_{name}"] for name, _ in _OUTS)
```
